# Optimizing a Trainium2 kernel written in Bass

```python
import jax, jax.numpy as jnp
from jax import lax
import numpy as np
import math

D_MODEL = 1024
BATCH = 1
SEQ = 256
DEPTH = 1

D_MIX = D_MODEL
D_CONV = D_MIX // 2
CONV_GROUPS = 8
CONV_GROUP_DIM = D_CONV // CONV_GROUPS
CONV_WIDTH = 3
GDN_HEADS = 4
GDN_HEAD_DIM = (D_MIX - D_CONV) // GDN_HEADS
GDN_WIDTH = GDN_HEADS * GDN_HEAD_DIM
GDN_CONV_WIDTH = 4
GDN_CHUNK = 64
D_FF = 2816
NORM_EPS = 1e-6
D_IN_PROJ = 3 * D_CONV + 4 * GDN_WIDTH + 2 * GDN_HEADS


def rmsnorm(x, w, eps=NORM_EPS):
    xf = x.astype(jnp.float32)
    y = xf * lax.rsqrt(jnp.mean(xf * xf, axis=-1, keepdims=True) + eps)
    return (y * w.astype(jnp.float32)).astype(x.dtype)

def l2norm(x, eps=NORM_EPS):
    return x * lax.rsqrt(jnp.sum(x * x, axis=-1, keepdims=True) + eps)

def swiglu_ffn(x, w_in, w_out):
    gate, up = jnp.split(x @ w_in, 2, axis=-1)
    return (jax.nn.silu(gate) * up) @ w_out

def causal_depthwise_conv(x, w):
    K, C = w.shape
    return lax.conv_general_dilated(
        x, w[:, None, :].astype(x.dtype), window_strides=(1,), padding=[(K - 1, 0)],
        dimension_numbers=('NWC', 'WIO', 'NWC'), feature_group_count=C)

def short_conv_mixer(b_gate, c_gate, h, conv_w, out_gain):
    y = b_gate * causal_depthwise_conv(c_gate * h, conv_w)
    bsz, t, _ = y.shape
    y = rmsnorm(y.reshape(bsz, t, CONV_GROUPS, CONV_GROUP_DIM),
                out_gain.reshape(CONV_GROUPS, CONV_GROUP_DIM))
    return y.reshape(bsz, t, D_CONV)

def gated_delta_rule_chunked(q, k, v, g, beta):
    bsz, t, nh, dk = q.shape
    dv = v.shape[-1]
    c = GDN_CHUNK
    n = t // c
    q = q * (dk ** -0.5)
    to_chunks = lambda a: a.reshape(bsz, n, c, nh, a.shape[-1]).transpose(0, 3, 1, 2, 4)
    q, k, v = to_chunks(q), to_chunks(k), to_chunks(v)
    beta = beta.reshape(bsz, n, c, nh).transpose(0, 3, 1, 2)
    g = jnp.cumsum(g.reshape(bsz, n, c, nh).transpose(0, 3, 1, 2), axis=-1)
    k_beta = k * beta[..., None]
    v_beta = v * beta[..., None]
    causal = jnp.tril(jnp.ones((c, c), dtype=bool))
    strict = jnp.tril(jnp.ones((c, c), dtype=bool), -1)
    gdiff = g[..., :, None] - g[..., None, :]
    decay = jnp.exp(jnp.where(causal, gdiff, -jnp.inf))
    lower = jnp.where(strict, jnp.einsum('bhncd,bhnsd->bhncs', k_beta, k) * decay, 0.0)
    rhs = jnp.concatenate([v_beta, k_beta * jnp.exp(g)[..., None]], axis=-1)
    sol = lax.linalg.triangular_solve(lower, rhs, left_side=True, lower=True, unit_diagonal=True)
    u, w = sol[..., :dv], sol[..., dv:]
    attn_intra = jnp.where(causal, jnp.einsum('bhncd,bhnsd->bhncs', q, k) * decay, 0.0)
    q_dec = q * jnp.exp(g)[..., None]
    k_dec = k * jnp.exp(g[..., -1:] - g)[..., None]
    g_last = jnp.exp(g[..., -1])
    xs = tuple(jnp.moveaxis(a, 2, 0) for a in (q_dec, k_dec, u, w, attn_intra, g_last))

    def step(state, inp):
        q_c, k_c, u_c, w_c, a_c, gl = inp
        v_new = u_c - jnp.einsum('bhck,bhkv->bhcv', w_c, state)
        o_c = jnp.einsum('bhck,bhkv->bhcv', q_c, state) + jnp.einsum('bhcs,bhsv->bhcv', a_c, v_new)
        state = state * gl[..., None, None] + jnp.einsum('bhck,bhcv->bhkv', k_c, v_new)
        return state, o_c

    s0 = jnp.zeros((bsz, nh, dk, dv), jnp.float32)
    _, o = lax.scan(step, s0, xs)
    return o.transpose(1, 0, 3, 2, 4).reshape(bsz, t, nh, dv)

def gated_deltanet_mixer(q, k, v, z, b, a, conv_w, A_log, dt_bias, norm_w):
    bsz, t, _ = q.shape
    qkv = jax.nn.silu(causal_depthwise_conv(jnp.concatenate([q, k, v], axis=-1), conv_w))
    q, k, v = jnp.split(qkv.astype(jnp.float32), 3, axis=-1)
    heads = lambda a_: a_.reshape(bsz, t, GDN_HEADS, GDN_HEAD_DIM)
    q, k, v = l2norm(heads(q)), l2norm(heads(k)), heads(v)
    beta = jax.nn.sigmoid(b.astype(jnp.float32))
    g = -jnp.exp(A_log.astype(jnp.float32)) * jax.nn.softplus(a.astype(jnp.float32) + dt_bias.astype(jnp.float32))
    o = gated_delta_rule_chunked(q, k, v, g, beta)
    o = rmsnorm(o, norm_w) * jax.nn.silu(heads(z).astype(jnp.float32))
    return o.reshape(bsz, t, GDN_WIDTH).astype(z.dtype)

def first_inputs(seed: int = 0) -> dict:
    key = jax.random.key(seed)
    ks = jax.random.split(key, 20)
    nrm = lambda k_, shape, fan_in: jax.random.normal(k_, shape, jnp.float32) * (fan_in ** -0.5)
    gain = lambda k_, shape: 1.0 + 0.05 * jax.random.normal(k_, shape, jnp.float32)
    L = DEPTH
    return {
        'x': jax.random.normal(ks[0], (BATCH, SEQ, D_MODEL), jnp.float32),
        'ffn1_norm': gain(ks[1], (L, D_MODEL)),
        'ffn1_w_in': nrm(ks[2], (L, D_MODEL, 2 * D_FF), D_MODEL),
        'ffn1_w_out': nrm(ks[3], (L, D_FF, D_MODEL), D_FF),
        'mix_norm': gain(ks[4], (L, D_MODEL)),
        'w_mix_in': nrm(ks[5], (L, D_MODEL, D_IN_PROJ), D_MODEL),
        'conv_short_w': nrm(ks[6], (L, CONV_WIDTH, D_CONV), CONV_WIDTH),
        'conv_out_norm': gain(ks[7], (L, D_CONV)),
        'gdn_conv_w': nrm(ks[8], (L, GDN_CONV_WIDTH, 3 * GDN_WIDTH), GDN_CONV_WIDTH),
        'gdn_A_log': jnp.log(jax.random.uniform(ks[9], (L, GDN_HEADS), jnp.float32, 1.0, 16.0)),
        'gdn_dt_bias': 1.0 + 0.1 * jax.random.normal(ks[10], (L, GDN_HEADS), jnp.float32),
        'gdn_out_norm': gain(ks[11], (L, GDN_HEAD_DIM)),
        'w_mix_out': nrm(ks[12], (L, D_MIX, D_MODEL), D_MIX),
        'ffn2_norm': gain(ks[13], (L, D_MODEL)),
        'ffn2_w_in': nrm(ks[14], (L, D_MODEL, 2 * D_FF), D_MODEL),
        'ffn2_w_out': nrm(ks[15], (L, D_FF, D_MODEL), D_FF),
        'final_norm': gain(ks[16], (D_MODEL,)),
    }

def first_block(x, ffn1_norm, ffn1_w_in, ffn1_w_out, mix_norm, w_mix_in, conv_short_w, conv_out_norm,
              gdn_conv_w, gdn_A_log, gdn_dt_bias, gdn_out_norm, w_mix_out, ffn2_norm, ffn2_w_in,
              ffn2_w_out, final_norm):
    sizes = [D_CONV, D_CONV, D_CONV, GDN_WIDTH, GDN_WIDTH, GDN_WIDTH, GDN_WIDTH, GDN_HEADS, GDN_HEADS]
    splits = np.cumsum(sizes)[:-1].tolist()
    h = x
    for layer in range(DEPTH):
        h = h + 0.5 * swiglu_ffn(rmsnorm(h, ffn1_norm[layer]), ffn1_w_in[layer], ffn1_w_out[layer])
        u = rmsnorm(h, mix_norm[layer]) @ w_mix_in[layer]
        cb, cc, ch, gq, gk, gv, gz, gb, ga = jnp.split(u, splits, axis=-1)
        y_conv = short_conv_mixer(cb, cc, ch, conv_short_w[layer], conv_out_norm[layer])
        y_gdn = gated_deltanet_mixer(gq, gk, gv, gz, gb, ga, gdn_conv_w[layer], gdn_A_log[layer],
                                     gdn_dt_bias[layer], gdn_out_norm[layer])
        h = h + jnp.concatenate([y_conv, y_gdn], axis=-1) @ w_mix_out[layer]
        h = h + 0.5 * swiglu_ffn(rmsnorm(h, ffn2_norm[layer]), ffn2_w_in[layer], ffn2_w_out[layer])
    return rmsnorm(h, final_norm)


CONV_DIM = 1024
CONV_KERNEL = 31
N_HEADS = 8
QK_NOPE_DIM = 128
QK_ROPE_DIM = 64
V_HEAD_DIM = 128
Q_LORA_RANK = 384
KV_LORA_RANK = 256
ROPE_THETA = 10000.0
Q_BLOCK = 128
D_FF_2 = 4 * D_MODEL
N_BRANCHES = 2
EPS = 1e-6

IN_WIDTHS = (2 * CONV_DIM, Q_LORA_RANK, KV_LORA_RANK, QK_ROPE_DIM, N_BRANCHES * D_MODEL)
IN_DIM = sum(IN_WIDTHS)
IN_SPLIT = tuple(int(v) for v in np.cumsum(IN_WIDTHS)[:-1])


def rms_norm(x, g):
    xf = x.astype(jnp.float32)
    y = xf * lax.rsqrt(jnp.mean(xf * xf, axis=-1, keepdims=True) + EPS)
    return (y * g.astype(jnp.float32)).astype(x.dtype)

def layer_norm(x, g, b):
    xf = x.astype(jnp.float32)
    mu = jnp.mean(xf, axis=-1, keepdims=True)
    var = jnp.mean(jnp.square(xf - mu), axis=-1, keepdims=True)
    y = (xf - mu) * lax.rsqrt(var + EPS)
    return (y * g.astype(jnp.float32) + b.astype(jnp.float32)).astype(x.dtype)

def rope_tables(positions):
    inv_freq = 1.0 / (ROPE_THETA ** (jnp.arange(0, QK_ROPE_DIM, 2, dtype=jnp.float32) / QK_ROPE_DIM))
    ang = positions.astype(jnp.float32)[..., None] * inv_freq
    return jnp.cos(ang), jnp.sin(ang)

def apply_rope(t, cos, sin):
    t1, t2 = jnp.split(t, 2, axis=-1)
    cos = cos.astype(t.dtype)
    sin = sin.astype(t.dtype)
    return jnp.concatenate([t1 * cos - t2 * sin, t2 * cos + t1 * sin], axis=-1)

def causal_depthwise_conv_2(u, w, b):
    return lax.conv_general_dilated(
        u, w[:, None, :].astype(u.dtype), window_strides=(1,),
        padding=[(CONV_KERNEL - 1, 0)],
        dimension_numbers=("NWC", "WIO", "NWC"),
        feature_group_count=CONV_DIM) + b

def mla_attention(q_nope, q_rope, k_nope, k_rope, v):
    b, s, h, _ = q_nope.shape
    nb = s // Q_BLOCK
    scale = 1.0 / math.sqrt(QK_NOPE_DIM + QK_ROPE_DIM)
    qn = jnp.moveaxis(q_nope.reshape(b, nb, Q_BLOCK, h, QK_NOPE_DIM), 1, 0)
    qr = jnp.moveaxis(q_rope.reshape(b, nb, Q_BLOCK, h, QK_ROPE_DIM), 1, 0)
    k_idx = jnp.arange(s)

    def one_block(args):
        qn_b, qr_b, blk = args
        sc = (jnp.einsum("bqhd,bkhd->bhqk", qn_b, k_nope)
              + jnp.einsum("bqhr,bkr->bhqk", qr_b, k_rope)).astype(jnp.float32) * scale
        q_idx = blk * Q_BLOCK + jnp.arange(Q_BLOCK)
        causal = q_idx[:, None] >= k_idx[None, :]
        sc = jnp.where(causal[None, None], sc, -1e30)
        p = jax.nn.softmax(sc, axis=-1).astype(v.dtype)
        return jnp.einsum("bhqk,bkhd->bqhd", p, v)

    out = lax.map(one_block, (qn, qr, jnp.arange(nb)))
    return jnp.moveaxis(out, 0, 1).reshape(b, s, h * V_HEAD_DIM)

def token_mixer(h, cos, sin, w_in, conv_w, conv_b, conv_norm_g, conv_norm_b, w_conv_out,
                q_norm_g, w_uq, kv_norm_g, w_ukv, w_attn_out, w_out):
    b, s, _ = h.shape
    z = h @ w_in
    u_glu, q_lat, kv_lat, k_r, gate_logits = jnp.split(z, IN_SPLIT, axis=-1)

    ua, ub = jnp.split(u_glu, 2, axis=-1)
    u = ua * jax.nn.sigmoid(ub)
    u = causal_depthwise_conv_2(u, conv_w, conv_b)
    u = jax.nn.silu(layer_norm(u, conv_norm_g, conv_norm_b))
    y_a = u @ w_conv_out

    q = (rms_norm(q_lat, q_norm_g) @ w_uq).reshape(b, s, N_HEADS, QK_NOPE_DIM + QK_ROPE_DIM)
    q_nope, q_rope = jnp.split(q, [QK_NOPE_DIM], axis=-1)
    q_rope = apply_rope(q_rope, cos[:, :, None, :], sin[:, :, None, :])
    kv = (rms_norm(kv_lat, kv_norm_g) @ w_ukv).reshape(b, s, N_HEADS, QK_NOPE_DIM + V_HEAD_DIM)
    k_nope, v = jnp.split(kv, [QK_NOPE_DIM], axis=-1)
    k_rope = apply_rope(k_r, cos, sin)
    o = mla_attention(q_nope, q_rope, k_nope, k_rope, v)
    y_b = o @ w_attn_out

    g_a, g_b = jnp.split(jax.nn.sigmoid(gate_logits), N_BRANCHES, axis=-1)
    return (g_a * y_a + g_b * y_b) @ w_out

def second_inputs(seed: int = 0) -> dict:
    key = jax.random.key(seed)
    ks = jax.random.split(key, 32)
    L = DEPTH

    def nrm(k, shape, fan_in, mult=1.0):
        return jax.random.normal(k, shape, jnp.float32) * (mult * fan_in ** -0.5)

    def gain(k, shape):
        return 1.0 + 0.05 * jax.random.normal(k, shape, jnp.float32)

    offsets = jax.random.randint(ks[2], (BATCH, 1), 0, 1024, dtype=jnp.int32)
    positions = offsets + jnp.arange(SEQ, dtype=jnp.int32)[None, :]
    return {
        "x": jax.random.normal(ks[0], (BATCH, SEQ, D_MODEL), jnp.float32),
        "c": jax.random.normal(ks[1], (BATCH, D_MODEL), jnp.float32),
        "positions": positions,
        "w_ada": nrm(ks[3], (L, D_MODEL, 6 * D_MODEL), D_MODEL, 0.2),
        "b_ada": 0.01 * jax.random.normal(ks[4], (L, 6 * D_MODEL), jnp.float32),
        "g_pre_mix": gain(ks[5], (L, D_MODEL)),
        "g_post_mix": gain(ks[6], (L, D_MODEL)),
        "g_pre_mlp": gain(ks[7], (L, D_MODEL)),
        "g_post_mlp": gain(ks[8], (L, D_MODEL)),
        "w_in": nrm(ks[9], (L, D_MODEL, IN_DIM), D_MODEL),
        "conv_w": nrm(ks[10], (L, CONV_KERNEL, CONV_DIM), CONV_KERNEL),
        "conv_b": 0.01 * jax.random.normal(ks[11], (L, CONV_DIM), jnp.float32),
        "conv_norm_g": gain(ks[12], (L, CONV_DIM)),
        "conv_norm_b": 0.01 * jax.random.normal(ks[13], (L, CONV_DIM), jnp.float32),
        "w_conv_out": nrm(ks[14], (L, CONV_DIM, D_MODEL), CONV_DIM),
        "q_norm_g": gain(ks[15], (L, Q_LORA_RANK)),
        "w_uq": nrm(ks[16], (L, Q_LORA_RANK, N_HEADS * (QK_NOPE_DIM + QK_ROPE_DIM)), Q_LORA_RANK),
        "kv_norm_g": gain(ks[17], (L, KV_LORA_RANK)),
        "w_ukv": nrm(ks[18], (L, KV_LORA_RANK, N_HEADS * (QK_NOPE_DIM + V_HEAD_DIM)), KV_LORA_RANK),
        "w_attn_out": nrm(ks[19], (L, N_HEADS * V_HEAD_DIM, D_MODEL), N_HEADS * V_HEAD_DIM),
        "w_out": nrm(ks[20], (L, D_MODEL, D_MODEL), D_MODEL),
        "w_mlp_in": nrm(ks[21], (L, D_MODEL, D_FF_2), D_MODEL),
        "w_mlp_out": nrm(ks[22], (L, D_FF_2, D_MODEL), D_FF_2),
    }

def second_block(x, c, positions, w_ada, b_ada, g_pre_mix, g_post_mix, g_pre_mlp, g_post_mlp,
              w_in, conv_w, conv_b, conv_norm_g, conv_norm_b, w_conv_out,
              q_norm_g, w_uq, kv_norm_g, w_ukv, w_attn_out, w_out, w_mlp_in, w_mlp_out):
    cos, sin = rope_tables(positions)
    c_act = jax.nn.silu(c)
    for l in range(DEPTH):
        mod = c_act @ w_ada[l] + b_ada[l]
        shift1, scale1, gate1, shift2, scale2, gate2 = [m[:, None, :] for m in jnp.split(mod, 6, axis=-1)]

        h = rms_norm(x, g_pre_mix[l]) * (1.0 + scale1) + shift1
        y = token_mixer(h, cos, sin, w_in[l], conv_w[l], conv_b[l], conv_norm_g[l], conv_norm_b[l],
                        w_conv_out[l], q_norm_g[l], w_uq[l], kv_norm_g[l], w_ukv[l],
                        w_attn_out[l], w_out[l])
        x = x + gate1 * rms_norm(y, g_post_mix[l])

        h = rms_norm(x, g_pre_mlp[l]) * (1.0 + scale2) + shift2
        y = jnp.square(jax.nn.relu(h @ w_mlp_in[l])) @ w_mlp_out[l]
        x = x + gate2 * rms_norm(y, g_post_mlp[l])
    return x


def setup_inputs(seed=0):
    out = dict(first_inputs(seed))
    for name, value in second_inputs(seed + 1).items():
        if name != "x":
            out[name + "_2"] = value
    return out


def reference(
    x, ffn1_norm, ffn1_w_in, ffn1_w_out, mix_norm, w_mix_in, conv_short_w, conv_out_norm,
    gdn_conv_w, gdn_A_log, gdn_dt_bias, gdn_out_norm, w_mix_out, ffn2_norm, ffn2_w_in,
    ffn2_w_out, final_norm, c_2, positions_2, w_ada_2, b_ada_2, g_pre_mix_2, g_post_mix_2,
    g_pre_mlp_2, g_post_mlp_2, w_in_2, conv_w_2, conv_b_2, conv_norm_g_2, conv_norm_b_2,
    w_conv_out_2, q_norm_g_2, w_uq_2, kv_norm_g_2, w_ukv_2, w_attn_out_2, w_out_2, w_mlp_in_2,
    w_mlp_out_2,
):
    x = first_block(
        x, ffn1_norm, ffn1_w_in, ffn1_w_out, mix_norm, w_mix_in, conv_short_w, conv_out_norm,
        gdn_conv_w, gdn_A_log, gdn_dt_bias, gdn_out_norm, w_mix_out, ffn2_norm, ffn2_w_in,
        ffn2_w_out, final_norm,
    )
    return second_block(
        x, c_2, positions_2, w_ada_2, b_ada_2, g_pre_mix_2, g_post_mix_2, g_pre_mlp_2,
        g_post_mlp_2, w_in_2, conv_w_2, conv_b_2, conv_norm_g_2, conv_norm_b_2, w_conv_out_2,
        q_norm_g_2, w_uq_2, kv_norm_g_2, w_ukv_2, w_attn_out_2, w_out_2, w_mlp_in_2,
        w_mlp_out_2,
    )


_drawn_inputs = setup_inputs


def setup_inputs(seed=0):
    import zlib

    import numpy as np

    out = dict(_drawn_inputs(seed))
    spreads = {}
    factors = {'gdn_A_log': 3.783,
     'gdn_dt_bias': 8.0,
     'gdn_out_norm': 3.848,
     'ffn2_norm': 3.378,
     'b_ada_2': 3.886,
     'g_pre_mix_2': 7.503,
     'g_post_mix_2': 8.0,
     'g_pre_mlp_2': 8.0,
     'g_post_mlp_2': 8.0,
     'conv_b_2': 52.902,
     'conv_norm_g_2': 7.974,
     'conv_norm_b_2': 64.0,
     'q_norm_g_2': 8.0,
     'kv_norm_g_2': 8.0}
    for name, (base, spread) in spreads.items():
        noise = np.random.default_rng([zlib.crc32(name.encode()), seed]).standard_normal(out[name].shape)
        drawn = base * np.exp(spread * noise) if base else spread * noise
        out[name] = __import__('jax').numpy.asarray(drawn.astype(out[name].dtype))
    for name, factor in factors.items():
        out[name] = (out[name] * factor).astype(out[name].dtype)
    return out
```

```python
from contextlib import ExitStack

import numpy as np

import concourse.bass as bass
from concourse import mybir

F32 = mybir.dt.float32
F32R = mybir.dt.float32r
BF16 = mybir.dt.bfloat16
I32 = mybir.dt.int32
ACT = mybir.ActivationFunctionType
ALU = mybir.AluOpType
AX_X = mybir.AxisListType.X

P = 128
T = 256
D = 1024
KT = D // P
EPS = 1e-6

D_FF = 2816
FF_STEPS = D_FF // 256
D_CONV = 512
HEADS = 4
DH = 128
CH = 128
UNITS = HEADS * (T // CH)
LEVELS = 7
MIX_COLS = 3592

TAPS = 31
PAD = TAPS - 1
NH = 8
NOPE = 128
ROPE = 64
Q_LAT = 384
KV_LAT = 256
D_MLP = 4096
MLP_STEPS = D_MLP // 256
POOL_TILES = 3
DVE_TILES = KT - POOL_TILES

N_VEC = 21
ATT_SCALE = float((NOPE + ROPE) ** -0.5)
SLOTS = 3
SLAB = 2048
ADA_SLAB = 1024
ADA_TILES = 6 * KT

_at = 0
C = {}
for _name, _width in (("ident", P), ("ones", P), ("swap", P), ("upper", P), ("levels", LEVELS * P),
                      ("causal", 3 * P), ("row_of", 64), ("grp_row_of", 32), ("row_sel", 8 * P),
                      ("grp_sel", 4 * P), ("restart", T), ("inv_freq", 1), ("eps", 1), ("qk_scale", 1),
                      ("half_pi", 1)):
    C[_name] = _at
    _at += _width
N_CONST = _at

VECS = {}
_rows = [0, 0, 0, 0]
for _g, _name, _n in ((0, "ffn1_norm", 8), (0, "mix_norm", 8), (0, "conv_out_norm", 4), (0, "gdn_out_norm", 1),
                      (0, "ffn2_norm", 8), (0, "final_norm", 8), (0, "conv_short_w", 12), (0, "gdn_conv_w", 48),
                      (1, "g_pre_mix_2", 8), (1, "g_post_mix_2", 8), (1, "g_pre_mlp_2", 8), (1, "g_post_mlp_2", 8),
                      (1, "conv_b_2", 8), (1, "conv_norm_g_2", 8), (1, "conv_norm_b_2", 8), (1, "q_norm_g_2", 3),
                      (1, "kv_norm_g_2", 2), (1, "c_2", 8), (1, "b_ada_2", 48)):
    VECS[_name] = (_g, _rows[_g])
    _rows[_g] += _n
_rows[2] = _rows[3] = 124
STAGE_ROWS = tuple(_rows)


def constants():
    t = np.zeros((P, N_CONST), np.float32)
    p = np.arange(P)

    def put(name, a):
        t[:a.shape[0], C[name]:C[name] + a.shape[1]] = a

    put("ident", np.eye(P))
    put("ones", np.ones((P, P)))
    swap = np.zeros((P, P))
    for m in range(P):
        if m % ROPE < ROPE // 2:
            swap[m + ROPE // 2, m] = -1
        else:
            swap[m - ROPE // 2, m] = 1
    put("swap", swap)
    j, i = p[:, None], p[None, :]
    put("upper", (i >= j) * 1.0)
    for lev in range(LEVELS):
        s = 1 << lev
        m = (i // (2 * s) == j // (2 * s)) & ((i // s) % 2 == 1) & ((j // s) % 2 == 0)
        t[:, C["levels"] + lev * P:C["levels"] + (lev + 1) * P] = m
    diag = np.where(p[:, None] >= p[None, :], 0.0, -1e30)
    put("causal", np.concatenate([diag, np.zeros((P, P)), diag], 1))
    row_of = np.zeros((P, 8, 8))
    for r in range(8):
        row_of[:, r, r] = 1
    put("row_of", row_of.reshape(P, 64))
    grp = np.zeros((P, 4, 8))
    sel = np.zeros((8, 4, P))
    for r in range(4):
        grp[:64, r, 2 * r] = 1
        grp[64:, r, 2 * r + 1] = 1
        sel[2 * r, r, :64] = 1
        sel[2 * r + 1, r, 64:] = 1
    put("grp_row_of", grp.reshape(P, 32))
    put("grp_sel", sel.reshape(8, 512))
    rs = np.zeros((8, 8, P))
    for r in range(8):
        rs[r, r, :] = 1
    put("row_sel", rs.reshape(8, 1024))
    restart = np.ones((8, T))
    restart[:, ::CH] = 0
    put("restart", restart)
    freq = 1.0 / np.power(np.float32(10000.0), np.arange(0, ROPE, 2, dtype=np.float32) / np.float32(ROPE)).astype(np.float32)
    put("inv_freq", freq.astype(np.float32)[p % (ROPE // 2)][:, None])
    put("eps", np.full((P, 1), EPS))
    qk = np.ones((8, 1))
    qk[:HEADS] = DH ** -0.5
    put("qk_scale", qk)
    put("half_pi", np.full((P, 1), np.pi / 2))
    return t


def slab_plan():
    plan = []

    def ffn(name):
        plan.extend([(name + "_gate", 0), (name + "_up", 0)])
        for k in range(1, FF_STEPS):
            plan.extend([(name + "_gate", k), (name + "_up", k), (name + "_down", k - 1)])
        plan.append((name + "_down", FF_STEPS - 1))

    ffn("ffn1")
    plan.extend([("mix", n) for n in range(15)])
    plan.extend([("mix_out", n) for n in range(4)])
    ffn("ffn2")
    for phase, n in (("glu", 8), ("lat", 3), ("uq", 3), ("ukv", 2), ("gate_b", 4), ("attn_out", 4), ("gate_a", 4),
                     ("conv_out", 4), ("w_out", 4)):
        plan.extend([(phase, k) for k in range(n)])
    plan.append(("mlp_in", 0))
    for k in range(1, MLP_STEPS):
        plan.extend([("mlp_in", k), ("mlp_out", k - 1)])
    plan.append(("mlp_out", MLP_STEPS - 1))
    return plan


SEQUENCES = {
    "x_high": (("n1_xh", 8), ("n2_xh", 8), ("mo_xh", 4), ("n3_xh", 8), ("h_xh", 8), ("w_xh", 8), ("h2_xh", 8)),
    "x_low": (("n1_xl", 8), ("n2_xl", 8), ("mo_xl", 4), ("n3_xl", 8), ("h_xl", 8), ("w_xl", 8), ("h2_xl", 8)),
    "y_high": (("lat_yh", 5), ("o_yh", 8), ("c_yh", 8)),
    "y_low": (("lat_yl", 5), ("o_yl", 8), ("c_yl", 8)),
    "squares": (("n1_sq", 1), ("n2_sq", 1), ("n3_sq", 1), ("f_sq", 2)),
    "sums": (("n1_stat", 1), ("n2_stat", 1), ("qk_stat", 1), ("short_stat", 1), ("o_stat", 1), ("n3_stat", 1),
             ("f_stat", 2), ("lat_stat", 1), ("ln_stat", 1), ("y_stat", 1), ("x3_stat", 1), ("z_stat", 1)),
    "roots": (("n1_std", 1), ("n2_std", 1), ("qk_std", 1), ("short_std", 1), ("o_std", 1), ("n3_std", 1), ("f_std", 1),
              ("g_std", 1), ("lat_std", 2), ("ln_std", 1), ("y_std", 1), ("x3_std", 1), ("z_std", 1)),
    "inverses": (("n1_rstd", 1), ("n2_rstd", 1), ("qk_rstd", 1), ("short_rstd", 1), ("o_rstd", 1), ("n3_rstd", 1),
                 ("f_rstd", 1), ("g_rstd", 1), ("ln_rstd", 1), ("y_rstd", 1), ("x3_rstd", 1), ("z_rstd", 1)),
    "resid_ready": (("x_in", 4), ("ffn1_resid", 4), ("mix_resid", 4), ("ffn2_resid", 4), ("x3", 4), ("x4", 4)),
    "hidden_gate": (("ffn1_gate", FF_STEPS), ("ffn2_gate", FF_STEPS), ("mlp_relu", MLP_STEPS)),
    "hidden_up": (("ffn1_up", FF_STEPS), ("ffn2_up", FF_STEPS)),
    "hidden_silu": (("ffn1_silu", FF_STEPS), ("ffn2_silu", FF_STEPS)),
    "hidden": (("ffn1_h", FF_STEPS), ("ffn2_h", FF_STEPS), ("mlp_sq", MLP_STEPS)),
    "hidden_high": (("ffn1_fh", FF_STEPS), ("ffn2_fh", FF_STEPS), ("mlp_fh", MLP_STEPS)),
    "hidden_low": (("ffn1_fl", FF_STEPS), ("ffn2_fl", FF_STEPS), ("mlp_fl", MLP_STEPS)),
}
SHARED = {}
for _sem, _stages in SEQUENCES.items():
    _n = 0
    for _stage, _count in _stages:
        SHARED[_stage] = (_sem, _n)
        _n += _count

PLAN = slab_plan()
FIRST = {}
for _s, (_phase, _step) in enumerate(PLAN):
    FIRST.setdefault(_phase, _s)
N_SLABS = len(PLAN)
MIX_COL = [1536, 1792, 2048, 2304, 2560, 2816, -1, 512, 768, 1024, 1280, 0, 256, 3072, 3328]
MIX_AB = 6


def slab_dmas(s):
    phase, step = PLAN[s]
    if phase == "mix" and step == MIX_AB:
        return 2
    if phase == "lat" and step == 2:
        return 3
    return {"uq": 3, "ukv": 2}.get(phase, 1)


def landed(s):
    return 16 * sum(slab_dmas(n) for n in range(s % SLOTS, s + 1, SLOTS))


def two_pi():
    c1 = 6.28125
    c2 = float((np.float32(2 * np.pi - c1).view(np.uint32) & np.uint32(0xFFFFF000)).view(np.float32))
    return c1, c2, float(np.float32(2 * np.pi - c1 - c2))


class Steps:

    def __init__(self, engine, semaphore):
        self.engine, self.semaphore, self.n = engine, semaphore, 0

    def __call__(self, instruction):
        instruction.then_inc(self.semaphore, 1)
        self.n += 1

    def sync(self):
        self.engine.wait_ge(self.semaphore, self.n)


def slab_floats(s):
    phase, step = PLAN[s]
    if phase == "mix" and step == MIX_AB:
        return KT * P
    if phase == "uq":
        return 3 * 512
    return SLAB


def two_blocks(nc, a):
    with ExitStack() as ctx:
        def sem(name):
            return ctx.enter_context(nc.semaphore(name))

        def sb(name, shape, dt=F32, where=ctx):
            return where.enter_context(nc.sbuf_tensor(name, shape, dt))

        con = sb("con", [P, N_CONST])
        raw = sb("raw", [P, SLOTS, SLAB])
        wh = sb("wh", [P, SLOTS, SLAB], F32R)
        wl = sb("wl", [P, SLOTS, SLAB], F32R)
        resid = sb("resid", [P, KT, T])
        xh = sb("xh", [P, KT, T], F32R)
        xl = sb("xl", [P, KT, T], F32R)
        vec = sb("vec", [P, 4, P])
        ada_raw = sb("ada_raw", [P, 2, ADA_SLAB])
        ada = sb("ada", [P, ADA_TILES])
        mods = sb("mods", [P, 4, KT])
        c_act = sb("c_act", [P, KT])
        rstd = sb("rstd", [P, T])
        std = sb("std", [P, T])
        zero = sb("zero", [1, 512], BF16)
        fh = sb("fh", [P, 2, T], F32R)
        fl = sb("fl", [P, 2, T], F32R)
        hid = sb("hid", [P, 4, 2 * T])
        a_log = sb("a_log", [4, 2])
        ipos = sb("ipos", [P, T], I32)
        g_cum = sb("g_cum", [4, T])
        beta_row = sb("beta_row", [4, T])
        att_col = sb("att_col", [P, 16])

        with ExitStack() as first:
            work1 = sb("work1", [P, 17600], where=first)
        yh = sb("yh", [P, KT, T], F32R)
        yl = sb("yl", [P, KT, T], F32R)
        work2 = sb("work2", [P, 13560])
        pt_mem = ada_raw[:, :, :].rearrange("p a b -> p (a b)")
        pool_mem = pt_mem[:, 6 * P:6 * P + POOL_TILES * T]
        ps = [ctx.enter_context(nc.psum_tensor(f"ps{i}", [P, 512], F32)) for i in range(8)]

        def const(name, width, rows=P):
            return con[0:rows, C[name]:C[name] + width]

        ident, ones = const("ident", P), const("ones", P)
        eps = const("eps", 1)

        def col(name, t, rows=P):
            g, r = VECS[name]
            return vec[0:rows, g, r + t:r + t + 1]

        def tap(k, t):
            r = k * KT + t
            return vec[:, 2 + r // 124, r % 124:r % 124 + 1]

        def pair(ap):
            return ap.rearrange("p (m t) -> p m t", m=2)

        def spread(ap, n):
            return ap.unsqueeze(1).to_broadcast([ap.shape[0], n, ap.shape[1]])

        used = {"w1": 0, "w2": 0}

        def w1(n):
            used["w1"] += n
            return work1[:, used["w1"] - n:used["w1"]]

        def w2(n):
            used["w2"] += n
            return work2[:, used["w2"] - n:used["w2"]]

        def tiles(ap, n):
            return ap.rearrange("p (n t) -> p n t", n=n)

        QW = T + 3
        w_qkvp = w1(12 * QW)
        qkvp = tiles(w_qkvp, 12)
        t_mat, tt_mat, x_mat = (w_qkvp[:, n * 1024:(n + 1) * 1024] for n in range(3))
        qkv = tiles(w1(12 * T), 12)
        w_sq = w1(2048)
        sq = tiles(w_sq, KT)
        gz = tiles(w1(1024), 4)
        w_cb = w1(1024)
        cb = tiles(w_cb, 4)
        w_cc = w1(1024)
        cc = tiles(w_cc, 4)
        mpad = tiles(w1(4 * (T + 2)), 4)
        g_row = tiles(w1(1024), 4)
        w_kb = w1(1024)
        kb = tiles(w_kb, 4)
        dt_mat = w1(1024)
        lt_mat = w1(1024)
        at_mat = w1(1024)
        q_n, k_n = qkv[:, 0:4, :], qkv[:, 4:8, :]
        v_beta = qkv[:, 8:12, :].rearrange("p n t -> p (n t)")
        k_be = qkv[:, 4:6, :].rearrange("p n t -> p (n t)")
        k_dec = qkv[:, 6:8, :].rearrange("p n t -> p (n t)")
        state = dt_mat[:, 0:512]
        o_t = tiles(w_cc, 4)
        v_new = w_kb
        cols = w1(48)
        small = tiles(hid[0:8, :, :].rearrange("p n t -> p (n t)"), 8)
        b_mat = w_sq[:, 0:1024]

        UW = T + PAD
        upad = tiles(w2(KT * UW), KT)
        conv = tiles(w2(2048), KT)
        w_qn = w2(2048)
        qn = tiles(w_qn, KT)
        w_kn = w2(2048)
        kn = tiles(w_kn, KT)
        w_qr = w2(2048)
        qr_raw = tiles(w_qr[:, 0:1024], 4)
        qr = tiles(w_qr[:, 1024:2048], 4)
        w_v = w2(2048)
        v = tiles(w_v, 2)
        kr_raw = w2(T)
        kr = w2(T)
        cosines = w2(T)
        sines = w2(T)

        stage = tiles(lt_mat[:, 0:512], 4)
        lat = tiles(w_v[:, 0:5 * T], 5)
        lat_sq = tiles(w_qr[:, 0:5 * T], 5)
        v_sq = tiles(w_v, KT)
        upad_out = w_qr.rearrange("p (a n) -> p a n", a=2)
        score = [hid[:, n, 0:3 * P] for n in range(2)]
        prob = [hid[:, 2 + n, 0:3 * P] for n in range(2)]

        prob_t = [pt_mem[:, n * 3 * P:(n + 1) * 3 * P] for n in range(2)]
        work_pool = pool_mem
        assert used["w1"] <= 17600 and used["w2"] <= 13560, used

        named = {}

        def S(name):
            name = SHARED.get(name, (name, 0))[0]
            if name not in named:
                named[name] = sem("s_" + name)
            return named[name]

        def at(name, count):
            return S(name), count + SHARED.get(name, (name, 0))[1]

        slot_loaded = [sem(f"slot{i}_loaded") for i in range(SLOTS)]
        high_done = sem("high_done")
        low_done = sem("low_done")
        taken = sem("taken")
        s_vstep, s_astep, s_pstep = sem("vector_step"), sem("scalar_step"), sem("pool_step")

        dram = {n: a[n][0] for n in ("ffn1_w_in", "ffn1_w_out", "ffn2_w_in", "ffn2_w_out", "w_mix_in", "w_mix_out",
                                     "w_ada_2", "w_in_2", "w_conv_out_2", "w_uq_2", "w_ukv_2", "w_attn_out_2",
                                     "w_out_2", "w_mlp_in_2", "w_mlp_out_2")}
        rows = {n: w.rearrange("(k p) n -> p k n", p=P) for n, w in dram.items()}
        x_rows = a["x"][0].rearrange("(k p) n -> p k n", p=P)
        out_rows = a["out"][0].rearrange("(k p) n -> p k n", p=P)
        gu, gq = 0, 2048

        block = ctx.enter_context(nc.Block())

        @block.sync
        def _(sp):
            def slot(s, k):
                n = SLAB if k != 3 else 1536
                return raw[:, s % SLOTS, 0:n].rearrange("p (k m) -> p k m", k=k)

            def free(s):
                if not isinstance(s, int) or s >= SLOTS:
                    sp.wait_ge(low_done, s - SLOTS + 1)

            def wide(s, slot_of, w, c0):
                free(s)
                sp.dma_start(slot(slot_of, KT), rows[w][:, :, bass.ds(c0, 256)]).then_inc(slot_loaded[slot_of % SLOTS], 16)

            def deep(s, slot_of, w, step):
                free(s)
                sp.dma_start(slot(slot_of, 2), rows[w][:, bass.ds(step * 2, 2), :]).then_inc(slot_loaded[slot_of % SLOTS], 16)

            def ffn(name, w_in, w_out, start):
                s0 = FIRST[name + "_gate"]
                wide(s0, s0, w_in, 0)
                wide(s0 + 1, s0 + 1, w_in, D_FF)
                for k in range(1, start):
                    s = s0 + 3 * k - 1
                    wide(s, s, w_in, 256 * k)
                    wide(s + 1, s + 1, w_in, D_FF + 256 * k)
                    deep(s + 2, s + 2, w_out, k - 1)
                with sp.Fori(0, FF_STEPS - start) as i:
                    s = s0 + 3 * start - 1
                    wide(s + i * 3, s, w_in, i * 256 + 256 * start)
                    wide(s + 1 + i * 3, s + 1, w_in, i * 256 + (D_FF + 256 * start))
                    deep(s + 2 + i * 3, s + 2, w_out, i + (start - 1))
                s = s0 + 3 * FF_STEPS - 1
                deep(s, s, w_out, FF_STEPS - 1)

            sp.dma_start(sq.rearrange("p (a b) t -> p a (b t)", a=2), x_rows).then_inc(S("x_loaded"), 16)
            ffn("ffn1", "ffn1_w_in", "ffn1_w_out", 2)
            for n, c0 in enumerate(MIX_COL):
                s = FIRST["mix"] + n
                if n == MIX_AB:
                    free(s)
                    dst = raw[:, s % SLOTS, 0:KT * P].rearrange("p (k m) -> p k m", k=KT)
                    for m, c in ((0, 3584), (32, 3588)):
                        sp.dma_start(dst[:, :, m:m + HEADS], rows["w_mix_in"][:, :, c:c + HEADS])\
                            .then_inc(slot_loaded[s % SLOTS], 16)
                else:
                    wide(s, s, "w_mix_in", c0)
            for n in range(4):
                wide(FIRST["mix_out"] + n, FIRST["mix_out"] + n, "w_mix_out", 256 * n)
            ffn("ffn2", "ffn2_w_in", "ffn2_w_out", 1)
            for n in range(4):
                s = FIRST["glu"] + 2 * n
                wide(s, s, "w_in_2", 256 * n)
                wide(s + 1, s + 1, "w_in_2", 1024 + 256 * n)
            s = FIRST["lat"]
            wide(s, s, "w_in_2", gq)
            wide(s + 1, s + 1, "w_in_2", gq + 256)
            free(s + 2)
            for m, c, n in ((0, gq + 512, 128), (128, gq + 640, ROPE), (192, gq + 640, ROPE)):
                sp.dma_start(slot(s + 2, KT)[:, :, m:m + n], rows["w_in_2"][:, :, c:c + n])\
                    .then_inc(slot_loaded[(s + 2) % SLOTS], 16)
            uq = rows["w_uq_2"].rearrange("p k (h c) -> p k h c", c=NOPE + ROPE)
            for n in range(3):
                s = FIRST["uq"] + n
                free(s)
                for k in range(3):
                    dst = slot(s, 3)[:, k, :]
                    if n < 2:
                        dst, src = dst.rearrange("p (h c) -> p h c", h=4), uq[:, k, 4 * n:4 * n + 4, 0:NOPE]
                    else:
                        dst, src = dst.rearrange("p (h c) -> p h c", h=NH), uq[:, k, :, NOPE:NOPE + ROPE]
                    sp.dma_start(dst, src).then_inc(slot_loaded[s % SLOTS], 16)
            ukv = rows["w_ukv_2"].rearrange("p k (h c) -> p k h c", c=2 * P)
            for n in range(2):
                s = FIRST["ukv"] + n
                free(s)
                for k in range(2):
                    dst = slot(s, 2)[:, k, :].rearrange("p (h c) -> p h c", h=NH)
                    sp.dma_start(dst, ukv[:, k, :, n * P:(n + 1) * P]).then_inc(slot_loaded[s % SLOTS], 16)
            for phase, w, c0 in (("gate_b", "w_in_2", 3776), ("attn_out", "w_attn_out_2", 0), ("gate_a", "w_in_2", 2752),
                                 ("conv_out", "w_conv_out_2", 0), ("w_out", "w_out_2", 0)):
                for n in range(4):
                    wide(FIRST[phase] + n, FIRST[phase] + n, w, c0 + 256 * n)
            s0 = FIRST["mlp_in"]
            wide(s0, s0, "w_mlp_in_2", 0)
            with sp.Fori(0, (MLP_STEPS - 1) // SLOTS) as i:
                for r in range(SLOTS):
                    s = s0 + 1 + 2 * r
                    wide(s + i * 6, s, "w_mlp_in_2", i * 768 + 256 * (r + 1))
                    deep(s + 1 + i * 6, s + 1, "w_mlp_out_2", i * 3 + r)
            deep(N_SLABS - 1, N_SLABS - 1, "w_mlp_out_2", MLP_STEPS - 1)
            for tk in range(2):
                sp.wait_ge(*at("out_ready", 4 * (tk + 1)))
                sp.dma_start(out_rows[:, tk, :], upad_out[:, tk, :]).then_inc(S("stored"), 16)
            sp.wait_ge(*at("stored", 32))

        @block.gpsimd
        def _(pool):
            ps_ = Steps(pool, s_pstep)
            pool.memset(zero[:, :], 0.0).then_inc(S("zero"), 1)
            pool.memset(qkvp[:, :, 0:3], 0.0).then_inc(S("pads"), 1)
            pool.memset(mpad[:, :, 0:2], 0.0).then_inc(S("pads"), 1)
            for n in range(2):
                pool.dma_start(ada_raw[:, n, :].rearrange("p (k m) -> p k m", k=KT),
                               rows["w_ada_2"][:, :, n * P:(n + 1) * P]).then_inc(S(f"ada{n}_loaded"), 16)
            pool.wait_ge(*at("conv4_done", 12))
            for m in (t_mat, tt_mat):
                pool.tensor_copy(tiles(m, UNITS), spread(ident, UNITS)).then_inc(S("inv_start"), 1)
            with pool.Fori(0, ADA_TILES // 2 - 1) as i:
                for n in range(2):
                    pool.wait_ge(*at("ada_taken", i * 2 + (n + 1)))
                    pool.dma_start(ada_raw[:, n, :].rearrange("p (k m) -> p k m", k=KT),
                                   rows["w_ada_2"][:, :, bass.ds(i * 256 + (2 + n) * P, P)])\
                        .then_inc(S(f"ada{n}_loaded"), 16)
            pool.wait_ge(*at("ffn2_resid", 4))
            pool.memset(upad[:, :, 0:PAD], 0.0).then_inc(S("upads"), 1)
            tmp = tiles(work_pool[:, :], POOL_TILES)
            pool.wait_ge(*at("glu", 4))
            for k in range(TAPS):
                for t in range(DVE_TILES, KT):
                    dst = conv[:, t, :] if k == 0 else tmp[:, t - DVE_TILES, :]
                    if k == 0:
                        ins = pool.tensor_scalar(dst, upad[:, t, k:k + T], tap(k, t), col("conv_b_2", t), ALU.mult, ALU.add)
                    else:
                        ins = pool.tensor_scalar(dst, upad[:, t, k:k + T], tap(k, t), 0.0, ALU.mult, ALU.add)
                ps_(ins)
                ps_.sync()
                if k:
                    ins = pool.tensor_tensor(conv[:, DVE_TILES:KT, :], conv[:, DVE_TILES:KT, :], tmp, ALU.add)
                    if k == TAPS - 1:
                        ins.then_inc(S("long_conv"), 1)
                    else:
                        ps_(ins)
                        ps_.sync()

        @block.scalar
        def _(act):
            st = Steps(act, s_astep)

            def cast(s):
                act.wait_ge(slot_loaded[s % SLOTS], landed(s))
                if s >= SLOTS:
                    act.wait_ge(taken, s - SLOTS + 1)
                n = slab_floats(s)
                act.activation(wh[:, s % SLOTS, 0:n], raw[:, s % SLOTS, 0:n], ACT.Copy).then_inc(high_done, 1)

            def cast_in_loop(s, i, per, count):
                act.wait_ge(slot_loaded[s % SLOTS], i * (16 * count) + landed(s))
                act.wait_ge(taken, i * per + (s - SLOTS + 1))
                act.activation(wh[:, s % SLOTS, :], raw[:, s % SLOTS, :], ACT.Copy).then_inc(high_done, 1)

            def norm_in(n, ready, gain):
                for t in range(KT):
                    if t % 2 == 0:
                        act.wait_ge(*at(ready, t // 2 + 1))
                    act.activation(xh[:, t, :], resid[:, t, :], ACT.Copy, scale=col(gain, t)).then_inc(S(n + "_xh"), 1)
                act.activation(sq[:, :, :], resid[:, :, :], ACT.Square).then_inc(S(n + "_sq"), 1)

            def root(n, src, dst, width):
                act.wait_ge(*at(n + "_stat", 1))
                act.activation(dst, src, ACT.Sqrt, scale=1.0 / width, bias=eps[0:dst.shape[0], :]).then_inc(S(n + "_std"), 1)

            def ffn(name):
                s0 = FIRST[name + "_gate"]

                def silu(count):
                    act.wait_ge(*at(name + "_gate", count))
                    act.activation(hid[:, 1, :], hid[:, 0, :], ACT.Silu).then_inc(S(name + "_silu"), 1)

                def round_hidden(count):
                    act.wait_ge(*at(name + "_h", count))
                    act.activation(fh[:, :, :], pair(hid[:, 3, :]), ACT.Copy).then_inc(S(name + "_fh"), 1)

                cast(s0 + 3)
                silu(1)
                cast(s0 + 4)
                round_hidden(1)
                with act.Fori(0, FF_STEPS - 1) as i:
                    s = s0 + 2
                    cast_in_loop(s + 3, i, 3, 1)
                    silu(i + 2)
                    cast_in_loop(s + 4, i, 3, 1)
                    act.wait_ge(taken, i * 3 + (s + 3))
                    round_hidden(i + 2)
                    cast_in_loop(s + 5, i, 3, 1)
                cast(s0 + 3 * FF_STEPS + 2)

            act.dma_start(con[:, :], a["table"]).then_inc(S("con"), 16)
            n_vec = 0
            for name, (g, r) in VECS.items():
                src = a[name]
                if name == "conv_short_w" or name == "gdn_conv_w":
                    src = src[0].rearrange("k (t p) -> (k t) p", p=P)
                elif name == "final_norm":
                    src = src.rearrange("(t p) -> t p", p=P)
                elif name == "gdn_out_norm":
                    src = src
                else:
                    src = src.rearrange("a (t p) -> (a t) p", p=P)
                act.dma_start(stage[r:r + src.shape[0], g, :], src).then_inc(S("vec_loaded"), 16)
                n_vec += 1
            taps = a["conv_w_2"][0].rearrange("k (t p) -> (k t) p", p=P)
            for g in range(2):
                act.dma_start(stage[0:124, 2 + g, :], taps[g * 124:(g + 1) * 124, :]).then_inc(S("vec_loaded"), 16)
                n_vec += 1
            assert n_vec == N_VEC
            act.dma_start(a_log[:, 0:1], a["gdn_A_log"].rearrange("a h -> h a")).then_inc(S("small_loaded"), 16)
            act.dma_start(a_log[:, 1:2], a["gdn_dt_bias"].rearrange("a h -> h a")).then_inc(S("small_loaded"), 16)
            act.dma_start(ipos[:, :], a["positions_2"].to_broadcast([P, T])).then_inc(S("small_loaded"), 16)
            for s in range(SLOTS):
                cast(s)
            act.wait_ge(*at("con", 16))
            act.wait_ge(*at("vec", 1))
            norm_in("n1", "x_in", "ffn1_norm")
            root("n1", ps[6][:, 0:T], std[:, :], D)
            ffn("ffn1")
            g, r = VECS["c_2"]
            act.activation(c_act[:, :], vec[:, g, r:r + KT], ACT.Silu).then_inc(S("c_act"), 1)

            norm_in("n2", "ffn1_resid", "mix_norm")
            root("n2", ps[6][:, 0:T], std[:, :], D)
            s0 = FIRST["mix"]
            for n in range(6):
                cast(s0 + n + 3)
                act.wait_ge(*at("conv4_done", 2 * (n + 1)))
                act.activation(qkv[:, 2 * n:2 * n + 2, :], qkv[:, 2 * n:2 * n + 2, :], ACT.Silu).then_inc(S("qkv_silu"), 1)
                if n < 4:
                    act.wait_ge(*at("qkv_silu", n + 1))
                    if n == 0:
                        act.wait_ge(*at("n2_stat", 1))
                    act.activation(sq[:, 2 * n:2 * n + 2, :], qkv[:, 2 * n:2 * n + 2, :], ACT.Square).then_inc(S("qk_sq"), 1)
            cast(s0 + 6 + 3)
            act.wait_ge(*at("small_loaded", 48))
            act.wait_ge(*at("ab_abs", 1))
            st(act.activation(a_log[:, 0:1], a_log[:, 0:1], ACT.Exp))
            act.activation(small[0:4, 2, :], small[0:4, 1, :], ACT.Exp).then_inc(S("ab_exp"), 1)
            act.wait_ge(*at("ab_one", 1))
            act.activation(small[0:4, 4, :], small[0:4, 3, :], ACT.Ln).then_inc(S("ab_ln"), 1)
            act.activation(beta_row[0:4, :], small[0:4, 5, :], ACT.Sigmoid).then_inc(S("beta"), 1)
            cast(s0 + 7 + 3)
            cast(s0 + 8 + 3)
            root("qk", ps[0][0:8, 0:T], small[0:8, 6, :], 1)
            for n in range(9, 12):
                cast(s0 + n + 3)
            for n in range(2):
                act.wait_ge(*at("g_spread", n + 1))
                act.activation(g_row[:, 2 * n:2 * n + 2, :], pair(ps[n][:, :]), ACT.Copy).then_inc(S("g_row"), 1)
            cast(s0 + 12 + 3)
            act.wait_ge(*at("short_y", 1))
            act.wait_ge(*at("qk_stat", 1))
            act.activation(sq[:, 0:4, :], cc[:, :, :], ACT.Square).then_inc(S("short_sq"), 1)
            root("short", ps[0][0:8, 0:T], small[0:8, 6, :], 64)
            act.wait_ge(*at("dt_diff", 1))
            act.activation(dt_mat, dt_mat, ACT.Exp).then_inc(S("dt_exp"), 1)
            act.activation(cols[:, 16:20], cols[:, 4:8], ACT.Exp).then_inc(S("g_exp"), 1)
            act.activation(cols[:, 20:24], cols[:, 24:28], ACT.Exp).then_inc(S("g_exp"), 1)
            act.activation(tiles(b_mat, 4)[:, :, 0:CH], g_row[:, :, CH:2 * CH], ACT.Exp).then_inc(S("g_exp"), 1)
            for n in range(13, 15):
                cast(s0 + n + 3)
                act.wait_ge(*at("mix_evac", n + 1))
                act.activation(gz[:, 2 * (n - 13):2 * (n - 13) + 2, :], gz[:, 2 * (n - 13):2 * (n - 13) + 2, :], ACT.Silu)\
                    .then_inc(S("gz_silu"), 1)
            for n in range(2):
                act.wait_ge(*at("short_out", n + 1))
                act.wait_ge(taken, FIRST["mix_out"])
                act.activation(xh[:, 2 * n:2 * n + 2, :], cb[:, 2 * n:2 * n + 2, :], ACT.Copy).then_inc(S("mo_xh"), 1)
            act.wait_ge(*at("cols_ready", 1))
            act.wait_ge(*at("k_turned", 2))
            act.wait_ge(*at("at_done", 1))
            for u in range(UNITS):
                dst = k_dec[:, u * P:(u + 1) * P] if u < 4 else k_be[:, (u - 4) * P:(u - 3) * P]
                scale = cols[:, 20 + u:21 + u] if u < 4 else cols[:, 28 + u - 4:29 + u - 4]
                act.activation(dst, ps[4 + u // 4][:, (u % 4) * P:(u % 4 + 1) * P], ACT.Copy, scale=scale)\
                    .then_inc(S("k_nat"), 1)
            act.wait_ge(*at("v_turned", 2))
            for u in range(UNITS):
                act.activation(v_beta[:, u * P:(u + 1) * P], ps[2 + u // 4][:, (u % 4) * P:(u % 4 + 1) * P], ACT.Copy,
                               scale=cols[:, 8 + u:9 + u]).then_inc(S("v_nat"), 1)
            with act.Fori(0, LEVELS) as i:
                act.wait_ge(*at("inv_x", i * 2 + 2))
                act.activation(x_mat[:, 512:1024], ps[1][:, :], ACT.Copy).then_inc(S("inv_xa"), 1)
            act.wait_ge(*at("w_mm", 1))
            act.activation(x_mat[:, 0:512], ps[1][:, :], ACT.Copy).then_inc(S("w_t"), 1)
            act.wait_ge(*at("s_mm", 1))
            act.activation(state, ps[2][:, :], ACT.Copy).then_inc(S("state"), 1)
            for c in range(2):
                act.wait_ge(*at("o_mm", c + 1))
                act.activation(o_t[:, :, c * CH:(c + 1) * CH], tiles(ps[3 + 2 * c][:, :], 4), ACT.Copy).then_inc(S("o_t"), 1)
            act.wait_ge(*at("o_t", 2))
            act.activation(sq[:, 0:4, :], o_t[:, :, :], ACT.Square).then_inc(S("o_sq"), 1)
            root("o", ps[0][0:8, 0:T], small[0:8, 6, :], DH)
            for n in range(2):
                act.wait_ge(*at("gdn_out", n + 1))
                act.activation(xh[:, 4 + 2 * n:6 + 2 * n, :], o_t[:, 2 * n:2 * n + 2, :], ACT.Copy).then_inc(S("mo_xh"), 1)
            for n in range(4):
                cast(FIRST["mix_out"] + n + 3)

            norm_in("n3", "mix_resid", "ffn2_norm")
            root("n3", ps[6][:, 0:T], std[:, :], D)
            ffn("ffn2")

            act.wait_ge(*at("ffn2_resid", 4))
            act.activation(kn[:, :, :], resid[:, :, :], ACT.Square).then_inc(S("f_sq"), 1)
            act.wait_ge(*at("x2_scaled", KT))
            act.activation(qn[:, :, :], resid[:, :, :], ACT.Square).then_inc(S("f_sq"), 1)
            root("f", ps[6][:, 0:T], std[:, :], D)
            act.wait_ge(*at("m2", 1))
            act.activation(kr, kr_raw, ACT.Sqrt, scale=1.0 / D, bias=eps).then_inc(S("g_std"), 1)
            for t in range(KT):
                act.wait_ge(*at("h_f", t + 1))
                act.activation(xh[:, t, :], kn[:, t, :], ACT.Copy).then_inc(S("h_xh"), 1)
            for n in range(4):
                s = FIRST["glu"] + 2 * n
                cast(s + 3)
                act.wait_ge(taken, s + 2)
                if n:
                    act.wait_ge(*at("glu", n))
                act.activation(hid[:, 0, :], ps[5][:, :], ACT.Sigmoid).then_inc(S("glu_sig"), 1)
                cast(s + 4)
            act.wait_ge(*at("angles", 1))
            act.activation(sines, sines, ACT.Sin).then_inc(S("rope_tables"), 1)
            act.activation(cosines, cosines, ACT.Sin).then_inc(S("rope_tables"), 1)
            s = FIRST["lat"]
            for n in range(3):
                cast(s + n + 3)
                act.wait_ge(taken, s + n + 1)
                bank = ps[4 + n % 2]
                if n < 2:
                    act.activation(lat[:, 2 * n:2 * n + 2, :], pair(bank[:, :]), ACT.Copy).then_inc(S("lat"), 1)
                else:
                    act.activation(lat[:, 4, :], bank[:, 0:T], ACT.Copy).then_inc(S("lat"), 1)
                    act.activation(kr_raw, bank[:, T:2 * T], ACT.Copy).then_inc(S("lat"), 1)
            act.wait_ge(*at("lat", 4))
            act.activation(lat_sq, lat[:, :, :], ACT.Square).then_inc(S("lat_sq"), 1)
            act.wait_ge(*at("lat_stat", 1))
            act.activation(hid[:, 0, 0:T], ps[6][:, 0:T], ACT.Sqrt, scale=1.0 / Q_LAT, bias=eps).then_inc(S("lat_std"), 1)
            act.activation(hid[:, 0, T:2 * T], ps[6][:, T:2 * T], ACT.Sqrt, scale=1.0 / KV_LAT, bias=eps).then_inc(S("lat_std"), 1)
            for t in range(5):
                act.wait_ge(*at("lat_n", 1))
                gain = col("q_norm_g_2", t) if t < 3 else col("kv_norm_g_2", t - 3)
                act.activation(yh[:, t, :], lat[:, t, :], ACT.Copy, scale=gain).then_inc(S("lat_yh"), 1)
            for n in range(3):
                s = FIRST["uq"] + n
                cast(s + 3)
                act.wait_ge(taken, s + 1)
                dst = qn[:, 4 * n:4 * n + 4, :] if n < 2 else qr_raw[:, :, :]
                for b in range(2):
                    act.activation(dst[:, 2 * b:2 * b + 2, :], pair(ps[4 + b][:, :]), ACT.Copy).then_inc(S("q"), 1)
            s = FIRST["ukv"]
            cast(s + 3)
            act.wait_ge(taken, s + 1)
            for b in range(4):
                act.activation(kn[:, 2 * b:2 * b + 2, :], pair(ps[b][:, :]), ACT.Copy).then_inc(S("k"), 1)
            cast(s + 4)
            act.wait_ge(taken, s + 2)
            act.wait_ge(*at("lat_yl", 5))
            for b in range(4):
                act.activation(v[:, b // 2, (b % 2) * 512:(b % 2 + 1) * 512], ps[b][:, :], ACT.Copy).then_inc(S("v"), 1)

            def attn_exp(h):
                act.wait_ge(*at("att_max", h + 1))
                if h >= 2:
                    act.wait_ge(*at("att_norm", h - 1))
                for qt in range(2):
                    w = (qt + 1) * P
                    o = qt * P
                    act.activation(prob[h % 2][:, o:o + w], score[h % 2][:, o:o + w], ACT.Exp,
                                   scale=ATT_SCALE, bias=att_col[:, 8 * (h % 2) + 2 + qt:8 * (h % 2) + 3 + qt],
                                   accum_out=att_col[:, 8 * (h % 2) + 4 + qt:8 * (h % 2) + 5 + qt]).then_inc(S("att_exp"), 1)

            def attn_out(h):
                act.wait_ge(*at("att_turned", h + 1))
                act.activation(prob_t[h % 2], ps[2 + h % 2][:, 0:3 * P], ACT.Copy).then_inc(S("att_pt"), 1)
                act.wait_ge(*at("att_o", h + 1))
                if h == 0:
                    act.wait_ge(taken, FIRST["ukv"] + 2)
                act.activation(yh[:, h, :], ps[4 + h % 2][:, 0:T], ACT.Copy).then_inc(S("o_yh"), 1)

            for h in range(NH + 1):
                if h < NH:
                    attn_exp(h)
                if h >= 1:
                    attn_out(h - 1)

            def gate(phase, n):
                s = FIRST[phase] + n
                cast(s + 3)
                act.wait_ge(taken, s + 1)
                if phase == "gate_a":
                    act.wait_ge(*at("mixed_b", n + 1))
                act.activation(qn[:, 2 * n:2 * n + 2, :], pair(ps[4 + n % 2][:, :]), ACT.Sigmoid).then_inc(S(phase), 1)

            for n in range(4):
                gate("gate_b", n)
            for n in range(4):
                cast(FIRST["attn_out"] + n + 3)
            for n in range(4):
                gate("gate_a", n)
            act.wait_ge(*at("ln_cen", 1))
            act.activation(v_sq, conv[:, :, :], ACT.Square).then_inc(S("ln_sq"), 1)
            root("ln", ps[6][:, 0:T], std[:, :], D)
            act.wait_ge(*at("ln_n", 1))
            for t in range(KT):
                act.activation(conv[:, t, :], conv[:, t, :], ACT.Silu, scale=col("conv_norm_g_2", t),
                               bias=col("conv_norm_b_2", t)).then_inc(S("ln_silu"), 1)
                act.wait_ge(*at("ln_silu", t + 1))
                act.activation(yh[:, t, :], conv[:, t, :], ACT.Copy).then_inc(S("c_yh"), 1)
            for n in range(4):
                cast(FIRST["conv_out"] + n + 3)
            for t in range(KT):
                act.wait_ge(*at("mixed", t // 2 + 1))
                act.activation(xh[:, t, :], kn[:, t, :], ACT.Copy).then_inc(S("w_xh"), 1)
            for n in range(4):
                s = FIRST["w_out"] + n
                cast(s + 3)
                act.wait_ge(taken, s + 1)
                act.activation(conv[:, 2 * n:2 * n + 2, :], pair(ps[4 + n % 2][:, :]), ACT.Copy).then_inc(S("y"), 1)
                act.wait_ge(*at("y", n + 1))
                act.activation(v_sq[:, 2 * n:2 * n + 2, :], conv[:, 2 * n:2 * n + 2, :], ACT.Square).then_inc(S("y_sq"), 1)
            root("y", ps[6][:, 0:T], std[:, :], D)
            act.wait_ge(*at("x3", 4))
            act.activation(v_sq, resid[:, :, :], ACT.Square).then_inc(S("x3_sq"), 1)
            root("x3", ps[6][:, T:2 * T], std[:, :], D)
            for t in range(KT):
                act.wait_ge(*at("h2_f", t + 1))
                act.activation(xh[:, t, :], qn[:, t, :], ACT.Copy).then_inc(S("h2_xh"), 1)

            s0 = FIRST["mlp_in"]

            def square(count):
                act.wait_ge(*at("mlp_relu", count))
                act.activation(fh[:, :, :], pair(hid[:, 0, :]), ACT.Square).then_inc(S("mlp_fh"), 1)

            cast(s0 + 3)
            square(1)
            with act.Fori(0, (MLP_STEPS - 1) // SLOTS - 1) as i:
                for r in range(SLOTS):
                    s = s0 + 1 + 2 * r
                    cast_in_loop(s + 3, i, 6, 2)
                    act.wait_ge(taken, i * 6 + (s + 2))
                    square(i * 3 + (r + 2))
                    cast_in_loop(s + 4, i, 6, 2)
            for k in range(MLP_STEPS - SLOTS, MLP_STEPS):
                s = s0 + 2 * k - 1
                if s + 3 < N_SLABS:
                    cast(s + 3)
                act.wait_ge(taken, s + 2)
                square(k + 1)
                if s + 4 < N_SLABS:
                    cast(s + 4)
            act.wait_ge(taken, N_SLABS)
            for n in range(4):
                act.activation(v_sq[:, 2 * n:2 * n + 2, :], pair(ps[n][:, :]), ACT.Square).then_inc(S("z_sq"), 1)
            root("z", ps[6][:, 0:T], std[:, :], D)
            for tk in range(2):
                for n in range(0, 2):
                    act.wait_ge(*at("turned", 2 * tk + n + 1))
                    act.activation(upad_out[:, tk, n * 512:(n + 1) * 512], ps[4 + 2 * tk + n][:, :], ACT.Copy)\
                        .then_inc(S("out_ready"), 2)

        @block.vector
        def _(dve):
            st = Steps(dve, s_vstep)

            def sub(s):
                n = slab_floats(s)
                dve.wait_ge(high_done, s + 1)
                dve.tensor_tensor(wl[:, s % SLOTS, 0:n], raw[:, s % SLOTS, 0:n], wh[:, s % SLOTS, 0:n].bitcast(F32),
                                  ALU.subtract).then_inc(low_done, 1)

            def sub_in_loop(s, i, per):
                dve.wait_ge(high_done, i * per + (s + 1))
                dve.tensor_tensor(wl[:, s % SLOTS, :], raw[:, s % SLOTS, :], wh[:, s % SLOTS, :].bitcast(F32),
                                  ALU.subtract).then_inc(low_done, 1)

            def norm_in(n, gain):
                for t in range(KT):
                    dve.wait_ge(*at(n + "_xh", t + 1))
                    dve.scalar_tensor_tensor(xl[:, t, :], resid[:, t, :], col(gain, t), xh[:, t, :].bitcast(F32),
                                             ALU.mult, ALU.subtract).then_inc(S(n + "_xl"), 1)

            def inverse(n, dst, src):
                dve.wait_ge(*at(n + "_std", 1))
                dve.reciprocal(dst, src).then_inc(S(n + "_rstd"), 1)
                dve.wait_ge(*at(n + "_rstd", 1))

            def scaled(dst, bank, r=rstd):
                return dve.tensor_tensor(dst, pair(bank[:, :]), spread(r[:, :], 2), ALU.mult)

            def ffn(name, n):
                s0 = FIRST[name + "_gate"]

                def gate(s, count):
                    dve.wait_ge(taken, s + 1)
                    scaled(pair(hid[:, 0, :]), ps[4]).then_inc(S(name + "_gate"), 1)

                def up(s, count):
                    dve.wait_ge(taken, s + 1)
                    scaled(pair(hid[:, 2, :]), ps[5]).then_inc(S(name + "_up"), 1)

                def hidden(count):
                    dve.wait_ge(*at(name + "_silu", count))
                    dve.wait_ge(*at(name + "_up", count))
                    dve.tensor_tensor(hid[:, 3, :], hid[:, 1, :], hid[:, 2, :], ALU.mult).then_inc(S(name + "_h"), 1)

                def rest(count):
                    dve.wait_ge(*at(name + "_fh", count))
                    dve.tensor_tensor(fl[:, :, :], pair(hid[:, 3, :]), fh[:, :, :].bitcast(F32), ALU.subtract)\
                        .then_inc(S(name + "_fl"), 1)

                inverse(n, rstd[:, :], std[:, :])
                gate(s0, 1)
                sub(s0 + 3)
                up(s0 + 1, 1)
                sub(s0 + 4)
                hidden(1)
                rest(1)
                with dve.Fori(0, FF_STEPS - 1) as i:
                    s = s0 + 2
                    gate(i * 3 + s, i + 2)
                    sub_in_loop(s + 3, i, 3)
                    up(i * 3 + (s + 1), i + 2)
                    sub_in_loop(s + 4, i, 3)
                    hidden(i + 2)
                    rest(i + 2)
                    sub_in_loop(s + 5, i, 3)
                s = s0 + 3 * FF_STEPS - 1
                dve.wait_ge(taken, s + 1)
                for b in range(4):
                    dve.scalar_tensor_tensor(resid[:, 2 * b:2 * b + 2, :], pair(ps[b][:, :]), 0.5,
                                             resid[:, 2 * b:2 * b + 2, :], ALU.mult, ALU.add).then_inc(S(name + "_resid"), 1)
                sub(s + 3)

            dve.wait_ge(*at("x_turned", 4))
            for b in range(4):
                dve.tensor_copy(resid[:, 2 * b:2 * b + 2, :], pair(ps[4 + b][:, :])).then_inc(S("x_in"), 1)
            dve.wait_ge(*at("vec_turned", 1))
            for g in range(4):
                ins = dve.tensor_copy(vec[:, g, 0:STAGE_ROWS[g]], ps[0][:, g * P:g * P + STAGE_ROWS[g]])
            ins.then_inc(S("vec"), 1)
            dve.wait_ge(*at("vec", 1))
            for s in range(SLOTS):
                sub(s)
            dve.wait_ge(*at("x_in", 4))
            norm_in("n1", "ffn1_norm")
            ffn("ffn1", "n1")

            dve.wait_ge(*at("ffn1_resid", 4))
            norm_in("n2", "mix_norm")
            inverse("n2", rstd[:, :], std[:, :])
            s0 = FIRST["mix"]
            dve.wait_ge(*at("pads", 2))

            def evac(n, dst):
                dve.wait_ge(taken, s0 + n + 1)
                scaled(dst, ps[4 + n % 2]).then_inc(S("mix_evac"), 1)
                dve.wait_ge(*at("mix_evac", n + 1))

            for n in range(6):
                evac(n, qkvp[:, 2 * n:2 * n + 2, 3:3 + T])
                sub(s0 + n + 3)
                for k in range(4):
                    for t in (2 * n, 2 * n + 1):
                        if k == 0:
                            ins = dve.tensor_scalar(qkv[:, t, :], qkvp[:, t, 0:T], col("gdn_conv_w", t), None, ALU.mult)
                        else:
                            ins = dve.scalar_tensor_tensor(qkv[:, t, :], qkvp[:, t, k:k + T], col("gdn_conv_w", 12 * k + t),
                                                           qkv[:, t, :], ALU.mult, ALU.add)
                        if k == 3:
                            ins.then_inc(S("conv4_done"), 1)
                    if k < 3:
                        st(ins)
                        st.sync()
            dve.wait_ge(taken, s0 + MIX_AB + 1)
            dve.tensor_tensor(small[0:4, 5, :], ps[4][0:4, 0:T], rstd[0:4, :], ALU.mult)
            st(dve.tensor_tensor(small[0:4, 0, :], ps[4][32:36, 0:T], rstd[32:36, :], ALU.mult))
            st.sync()
            dve.wait_ge(*at("small_loaded", 48))
            dve.tensor_scalar(small[0:4, 0, :], small[0:4, 0, :], a_log[:, 1:2], None, ALU.add).then_inc(S("mix_evac"), 1)
            dve.wait_ge(*at("mix_evac", MIX_AB + 1))
            dve.scalar_tensor_tensor(small[0:4, 1, :], small[0:4, 0, :], -1.0, small[0:4, 0, :], ALU.mult, ALU.min).then_inc(S("ab_abs"), 1)
            sub(s0 + MIX_AB + 3)
            dve.wait_ge(*at("ab_exp", 1))
            dve.tensor_scalar(small[0:4, 3, :], small[0:4, 2, :], 1.0, None, ALU.add).then_inc(S("ab_one"), 1)
            dve.wait_ge(*at("ab_one", 1))
            dve.wait_ge(*at("ab_ln", 1))
            st(dve.tensor_scalar(small[0:4, 3, :], small[0:4, 3, :], 1.0, None, ALU.subtract))
            st.sync()
            st(dve.tensor_scalar(small[0:4, 1, :], small[0:4, 3, :], 0.0, None, ALU.is_equal))
            st.sync()
            dve.tensor_tensor(small[0:4, 4, :], small[0:4, 4, :], small[0:4, 1, :], ALU.add)
            st(dve.tensor_tensor(small[0:4, 3, :], small[0:4, 3, :], small[0:4, 1, :], ALU.add))
            st.sync()
            st(dve.reciprocal(small[0:4, 1, :], small[0:4, 3, :]))
            st.sync()
            st(dve.tensor_tensor(small[0:4, 4, :], small[0:4, 4, :], small[0:4, 1, :], ALU.mult))
            st.sync()
            st(dve.tensor_tensor(small[0:4, 4, :], small[0:4, 4, :], small[0:4, 2, :], ALU.mult))
            st.sync()
            st(dve.scalar_tensor_tensor(small[0:4, 4, :], small[0:4, 0, :], 0.0, small[0:4, 4, :], ALU.max, ALU.add))
            st.sync()
            st(dve.tensor_scalar(small[0:4, 4, :], small[0:4, 4, :], a_log[:, 0:1], -1.0, ALU.mult, ALU.mult))
            st.sync()
            dve.tensor_tensor_scan(g_cum[0:4, :], const("restart", T, 4), small[0:4, 4, :], 0.0, ALU.mult, ALU.add)\
                .then_inc(S("g_cum"), 1)

            def pairs(n, dst):
                evac(n, dst)
                sub(s0 + n + 3)

            pairs(7, cc[:, 0:2, :])
            pairs(8, cc[:, 2:4, :])
            inverse("qk", small[0:8, 7, :], small[0:8, 6, :])
            dve.tensor_scalar(small[0:8, 7, :], small[0:8, 7, :], const("qk_scale", 1, 8), None, ALU.mult).then_inc(S("qk_row"), 1)
            for n in (9, 10):
                b = n - 9
                evac(n, mpad[:, 2 * b:2 * b + 2, 2:2 + T])
                st(dve.tensor_tensor(mpad[:, 2 * b:2 * b + 2, 2:2 + T], mpad[:, 2 * b:2 * b + 2, 2:2 + T],
                                     cc[:, 2 * b:2 * b + 2, :], ALU.mult))
                sub(s0 + n + 3)
            dve.wait_ge(*at("qk_spread", 4))
            for b in range(4):
                dve.tensor_tensor(qkv[:, 2 * b:2 * b + 2, :], qkv[:, 2 * b:2 * b + 2, :], pair(ps[b][:, :]), ALU.mult)\
                    .then_inc(S("qk_n"), 1)
            pairs(11, cb[:, 0:2, :])
            pairs(12, cb[:, 2:4, :])
            for b in range(2):
                dve.wait_ge(*at("b_spread", b + 1))
                dve.tensor_tensor(kb[:, 2 * b:2 * b + 2, :], k_n[:, 2 * b:2 * b + 2, :], pair(ps[2 + b][:, :]), ALU.mult)\
                    .then_inc(S("kb"), 1)
            st.sync()
            for k in range(3):
                for t in range(4):
                    if k == 0:
                        ins = dve.tensor_scalar(cc[:, t, :], mpad[:, t, 0:T], col("conv_short_w", t), None, ALU.mult)
                    else:
                        ins = dve.scalar_tensor_tensor(cc[:, t, :], mpad[:, t, k:k + T], col("conv_short_w", 4 * k + t),
                                                       cc[:, t, :], ALU.mult, ALU.add)
                st(ins)
                st.sync()
            dve.tensor_tensor(cc[:, :, :], cc[:, :, :], cb[:, :, :], ALU.mult).then_inc(S("short_y"), 1)
            dve.wait_ge(*at("col_turned", 4))
            dve.wait_ge(*at("g_row", 2))
            st(dve.tensor_copy(cols[:, 0:16], ps[6][:, 0:16]))
            st.sync()
            for u in range(UNITS):
                c, h = u // HEADS, u % HEADS
                ins = dve.tensor_scalar(dt_mat[:, u * P:(u + 1) * P], g_row[:, h, c * CH:(c + 1) * CH], cols[:, u:u + 1], 0.0,
                                        ALU.subtract, ALU.min)
            st(ins)
            dve.tensor_tensor(cols[:, 24:28], g_row[:, :, CH - 1], cols[:, 0:4], ALU.subtract).then_inc(S("dt_diff"), 1)
            inverse("short", small[0:8, 7, :], small[0:8, 6, :])
            dve.wait_ge(*at("short_spread", 2))
            for b in range(2):
                for t in (2 * b, 2 * b + 1):
                    ins = dve.scalar_tensor_tensor(cb[:, t, :], cc[:, t, :], col("conv_out_norm", t),
                                                   ps[b][:, (t % 2) * T:(t % 2 + 1) * T], ALU.mult, ALU.mult)
                ins.then_inc(S("short_out"), 1)
            pairs(13, gz[:, 0:2, :])
            dve.wait_ge(*at("mix_evac", 14))
            dve.wait_ge(*at("g_exp", 3))
            dve.wait_ge(*at("dt_exp", 1))
            st(dve.scalar_tensor_tensor(cols[:, 28:32], cols[:, 12:16], -1.0, cols[:, 16:20], ALU.mult, ALU.mult))
            st.sync()
            for b in range(2):
                dve.wait_ge(*at("lt_mm", b + 1))
                dve.tensor_tensor(lt_mat[:, b * 512:(b + 1) * 512], ps[b][:, :], dt_mat[:, b * 512:(b + 1) * 512], ALU.mult)\
                    .then_inc(S("lt"), 1)
            dve.wait_ge(*at("lt", 2))
            st(dve.tensor_tensor(tiles(dt_mat, UNITS), tiles(dt_mat, UNITS), spread(const("upper", P), UNITS), ALU.mult))
            st.sync()
            for b in range(2):
                dve.wait_ge(*at("at_mm", b + 1))
                ins = dve.tensor_tensor(at_mat[:, b * 512:(b + 1) * 512], ps[b][:, :], dt_mat[:, b * 512:(b + 1) * 512], ALU.mult)
            ins.then_inc(S("at_done"), 1)
            dve.wait_ge(*at("at_done", 1))
            st(dve.tensor_tensor(q_n[:, :, CH:2 * CH], q_n[:, :, CH:2 * CH], tiles(b_mat, 4)[:, :, 0:CH], ALU.mult))
            st.sync()
            dve.tensor_copy(cols[:, 32:36], cols[:, 28:32]).then_inc(S("cols_ready"), 1)
            pairs(14, gz[:, 2:4, :])
            for b in range(2):
                dve.wait_ge(*at("mo_xh", b + 1))
                dve.tensor_tensor(xl[:, 2 * b:2 * b + 2, :], cb[:, 2 * b:2 * b + 2, :], xh[:, 2 * b:2 * b + 2, :].bitcast(F32),
                                  ALU.subtract).then_inc(S("mo_xl"), 1)
            dve.wait_ge(*at("inv_start", 2))
            with dve.Fori(0, LEVELS) as i:
                dve.tensor_tensor(tiles(b_mat, UNITS), tiles(lt_mat, UNITS),
                                  con[:, bass.ds(i * P + C["levels"], P)].unsqueeze(1).to_broadcast([P, UNITS, P]), ALU.mult)\
                    .then_inc(S("inv_b"), 1)
                dve.wait_ge(*at("inv_x", i * 2 + 1))
                dve.tensor_copy(x_mat[:, 0:512], ps[0][:, :]).then_inc(S("inv_xv"), 1)
                for b in range(2):
                    dve.wait_ge(*at("inv_y", i * 4 + (b + 1)))
                    dve.tensor_tensor(t_mat[:, b * 512:(b + 1) * 512], t_mat[:, b * 512:(b + 1) * 512], ps[2 + b][:, :],
                                      ALU.subtract).then_inc(S("inv_t"), 1)
                for b in range(2):
                    dve.wait_ge(*at("inv_y", i * 4 + (b + 3)))
                    dve.tensor_tensor(tt_mat[:, b * 512:(b + 1) * 512], tt_mat[:, b * 512:(b + 1) * 512], ps[4 + b][:, :],
                                      ALU.subtract).then_inc(S("inv_t"), 1)
                dve.wait_ge(*at("inv_t", i * 4 + 4))
            dve.wait_ge(*at("v_mm", 1))
            dve.tensor_copy(v_new[:, 0:512], ps[0][:, :]).then_inc(S("v_new"), 1)
            dve.wait_ge(*at("v_mm", 2))
            dve.tensor_copy(v_new[:, 512:1024], ps[4][:, :]).then_inc(S("v_new"), 1)
            dve.wait_ge(*at("ada_taken", ADA_TILES))
            g, r = VECS["b_ada_2"]
            st(dve.tensor_tensor(ada[:, :], ps[7][:, 0:ADA_TILES], vec[:, g, r:r + ADA_TILES], ALU.add))
            st.sync()

            def vecs(name):
                g, r = VECS[name]
                return vec[:, g, r:r + KT]

            dve.scalar_tensor_tensor(mods[:, 0, :], ada[:, 8:16], 1.0, vecs("g_pre_mix_2"), ALU.add, ALU.mult)
            dve.tensor_tensor(mods[:, 1, :], ada[:, 16:24], vecs("g_post_mix_2"), ALU.mult)
            dve.scalar_tensor_tensor(mods[:, 2, :], ada[:, 32:40], 1.0, vecs("g_pre_mlp_2"), ALU.add, ALU.mult)
            st(dve.tensor_tensor(mods[:, 3, :], ada[:, 40:48], vecs("g_post_mlp_2"), ALU.mult))
            st.sync()
            inverse("o", small[0:8, 7, :], small[0:8, 6, :])
            dve.wait_ge(*at("gz_silu", 2))
            for b in range(2):
                dve.wait_ge(*at("o_spread", b + 1))
                st(dve.scalar_tensor_tensor(o_t[:, 2 * b:2 * b + 2, :], o_t[:, 2 * b:2 * b + 2, :], col("gdn_out_norm", 0),
                                            pair(ps[b][:, :]), ALU.mult, ALU.mult))
                st.sync()
                dve.tensor_tensor(o_t[:, 2 * b:2 * b + 2, :], o_t[:, 2 * b:2 * b + 2, :], gz[:, 2 * b:2 * b + 2, :], ALU.mult)\
                    .then_inc(S("gdn_out"), 1)
            for b in range(2):
                dve.wait_ge(*at("mo_xh", b + 3))
                dve.tensor_tensor(xl[:, 4 + 2 * b:6 + 2 * b, :], o_t[:, 2 * b:2 * b + 2, :],
                                  xh[:, 4 + 2 * b:6 + 2 * b, :].bitcast(F32), ALU.subtract).then_inc(S("mo_xl"), 1)
            for n in range(4):
                s = FIRST["mix_out"] + n
                dve.wait_ge(taken, s + 1)
                dve.tensor_tensor(resid[:, 2 * n:2 * n + 2, :], pair(ps[4 + n % 2][:, :]), resid[:, 2 * n:2 * n + 2, :],
                                  ALU.add).then_inc(S("mix_resid"), 1)
                sub(s + 3)
            dve.wait_ge(*at("mix_resid", 4))
            norm_in("n3", "ffn2_norm")
            ffn("ffn2", "n3")

            dve.wait_ge(*at("ffn2_resid", 4))
            dve.wait_ge(*at("f_sq", 1))
            for t in range(KT):
                dve.tensor_scalar(resid[:, t, :], resid[:, t, :], col("final_norm", t), None, ALU.mult).then_inc(S("x2_scaled"), 1)
            inverse("f", rstd[:, :], std[:, :])
            dve.wait_ge(*at("f_stat", 2))
            st(dve.tensor_tensor(kr_raw, ps[7][:, 0:T], rstd[:, :], ALU.mult))
            st.sync()
            dve.tensor_tensor(kr_raw, kr_raw, rstd[:, :], ALU.mult).then_inc(S("m2"), 1)
            dve.wait_ge(*at("x2_scaled", KT))
            st(dve.tensor_tensor(resid[:, :, :], resid[:, :, :], spread(rstd[:, :], KT), ALU.mult))
            st.sync()
            inverse("g", rstd[:, :], kr)
            for t in range(KT):
                st(dve.scalar_tensor_tensor(kn[:, t, :], resid[:, t, :], mods[:, 0, t:t + 1], rstd[:, :], ALU.mult, ALU.mult))
                st.sync()
                dve.tensor_scalar(kn[:, t, :], kn[:, t, :], ada[:, t:t + 1], None, ALU.add).then_inc(S("h_f"), 1)
                dve.wait_ge(*at("h_xh", t + 1))
                dve.tensor_tensor(xl[:, t, :], kn[:, t, :], xh[:, t, :].bitcast(F32), ALU.subtract).then_inc(S("h_xl"), 1)
            dve.wait_ge(*at("upads", 1))
            for n in range(4):
                s = FIRST["glu"] + 2 * n
                sub(s + 3)
                dve.wait_ge(*at("glu_sig", n + 1))
                dve.tensor_tensor(upad[:, 2 * n:2 * n + 2, PAD:PAD + T], pair(ps[4][:, :]), pair(hid[:, 0, :]), ALU.mult)\
                    .then_inc(S("glu"), 1)
                sub(s + 4)
            dve.wait_ge(*at("glu", 4))
            dve.wait_ge(*at("small_loaded", 48))
            c1, c2, c3 = two_pi()
            magic = 12582912.0
            lim = 3.1415925
            ang, turns = hid[:, 1, 0:T], hid[:, 1, T:2 * T]
            st(dve.tensor_copy(ang, ipos[:, :]))
            st.sync()
            st(dve.tensor_scalar(ang, ang, const("inv_freq", 1), None, ALU.mult))
            st.sync()
            for dst, quarter, shift in ((sines, 0.0, 0.0), (cosines, 0.25, float(np.float32(np.pi / 2)))):
                st(dve.tensor_scalar(turns, ang, float(np.float32(1 / (2 * np.pi))), quarter, ALU.mult, ALU.add))
                st.sync()
                st(dve.tensor_scalar(turns, turns, magic, None, ALU.add))
                st.sync()
                st(dve.tensor_scalar(turns, turns, magic, None, ALU.subtract))
                st.sync()
                src = ang
                for c in (c1, c2, c3):
                    st(dve.scalar_tensor_tensor(dst, turns, -c, src, ALU.mult, ALU.add))
                    st.sync()
                    src = dst
                st(dve.tensor_scalar(dst, dst, shift, lim, ALU.add, ALU.min))
                st.sync()
                ins = dve.tensor_scalar(dst, dst, -lim, None, ALU.max)
                if quarter:
                    ins.then_inc(S("angles"), 1)
                else:
                    st(ins)

            taps_left = list(range(TAPS))

            def convolve(n):
                for _ in range(n):
                    if not taps_left:
                        return
                    k = taps_left.pop(0)
                    for t in range(DVE_TILES):
                        if k == 0:
                            ins = dve.tensor_scalar(conv[:, t, :], upad[:, t, 0:T], tap(0, t), col("conv_b_2", t),
                                                    ALU.mult, ALU.add)
                        else:
                            ins = dve.scalar_tensor_tensor(conv[:, t, :], upad[:, t, k:k + T], tap(k, t), conv[:, t, :],
                                                           ALU.mult, ALU.add)
                    st(ins)
                    st.sync()

            for n in range(3):
                sub(FIRST["lat"] + n + 3)
                convolve(1)
            dve.wait_ge(*at("lat_std", 2))
            st(dve.reciprocal(hid[:, 1, :], hid[:, 0, :]))
            st.sync()
            st(dve.tensor_tensor(lat[:, 0:3, :], lat[:, 0:3, :], spread(hid[:, 1, 0:T], 3), ALU.mult))
            dve.tensor_tensor(lat[:, 3:5, :], lat[:, 3:5, :], spread(hid[:, 1, T:2 * T], 2), ALU.mult).then_inc(S("lat_n"), 1)
            dve.wait_ge(*at("lat_n", 1))
            for t in range(5):
                gain = col("q_norm_g_2", t) if t < 3 else col("kv_norm_g_2", t - 3)
                dve.wait_ge(*at("lat_yh", t + 1))
                dve.scalar_tensor_tensor(yl[:, t, :], lat[:, t, :], gain, yh[:, t, :].bitcast(F32), ALU.mult, ALU.subtract)\
                    .then_inc(S("lat_yl"), 1)
            dve.wait_ge(*at("rope_tables", 2))
            dve.wait_ge(*at("kr_swap", 1))
            dve.wait_ge(*at("lat", 4))
            st(dve.tensor_tensor(kr, kr_raw, cosines, ALU.mult))
            st(dve.tensor_tensor(hid[:, 2, 0:T], ps[7][:, 0:T], sines, ALU.mult))
            st.sync()
            dve.tensor_tensor(kr, kr, hid[:, 2, 0:T], ALU.add).then_inc(S("kr"), 1)
            for n in range(3):
                sub(FIRST["uq"] + n + 3)
                convolve(1)
            dve.wait_ge(*at("q", 6))
            st(dve.tensor_tensor(qr[:, :, :], qr_raw[:, :, :], spread(cosines, 4), ALU.mult))
            for b in range(2):
                dve.wait_ge(*at("q_swap", b + 1))
                st(dve.tensor_tensor(pair(hid[:, 2 + b, :]), pair(ps[6 + b][:, :]), spread(sines, 2), ALU.mult))
            st.sync()
            dve.tensor_tensor(qr[:, :, :], qr[:, :, :], tiles(hid[:, 2:4, :].rearrange("p a t -> p (a t)"), 4), ALU.add)\
                .then_inc(S("qr"), 1)
            sub(FIRST["ukv"] + 3)
            sub(FIRST["ukv"] + 4)

            def attn_max(h):
                c = 8 * (h % 2)
                dve.wait_ge(*at("att_s", h + 1))
                st(dve.tensor_tensor(score[h % 2], ps[h % 2][:, 0:3 * P], const("causal", 3 * P), ALU.add))
                st.sync()
                dve.tensor_reduce(att_col[:, c:c + 1], score[h % 2][:, 0:P], AX_X, ALU.max)
                st(dve.tensor_reduce(att_col[:, c + 1:c + 2], score[h % 2][:, P:3 * P], AX_X, ALU.max))
                st.sync()
                dve.tensor_scalar(att_col[:, c + 2:c + 4], att_col[:, c:c + 2], -ATT_SCALE, None, ALU.mult)\
                    .then_inc(S("att_max"), 1)

            def attn_norm(h):
                c = 8 * (h % 2)
                dve.wait_ge(*at("att_exp", 2 * (h + 1)))
                st(dve.reciprocal(att_col[:, c + 6:c + 8], att_col[:, c + 4:c + 6]))
                st.sync()
                st(dve.tensor_scalar(prob[h % 2][:, 0:P], prob[h % 2][:, 0:P], att_col[:, c + 6:c + 7], None, ALU.mult))
                dve.tensor_scalar(prob[h % 2][:, P:3 * P], prob[h % 2][:, P:3 * P], att_col[:, c + 7:c + 8], None, ALU.mult)\
                    .then_inc(S("att_norm"), 1)

            def attn_rest(h):
                dve.wait_ge(*at("o_yh", h + 1))
                dve.tensor_tensor(yl[:, h, :], ps[4 + h % 2][:, 0:T], yh[:, h, :].bitcast(F32), ALU.subtract)\
                    .then_inc(S("o_yl"), 1)

            for h in range(NH + 2):
                if h < NH:
                    attn_max(h)
                convolve(1)
                if 1 <= h <= NH:
                    attn_norm(h - 1)
                if h >= 2:
                    attn_rest(h - 2)
            for n in range(4):
                sub(FIRST["gate_b"] + n + 3)
                convolve(2)
            for n in range(4):
                s = FIRST["attn_out"] + n
                dve.wait_ge(taken, s + 1)
                dve.wait_ge(*at("gate_b", n + 1))
                dve.tensor_tensor(kn[:, 2 * n:2 * n + 2, :], pair(ps[4 + n % 2][:, :]), qn[:, 2 * n:2 * n + 2, :], ALU.mult)\
                    .then_inc(S("mixed_b"), 1)
                sub(s + 3)
                convolve(1)
            for n in range(4):
                sub(FIRST["gate_a"] + n + 3)
                if n == 0:
                    convolve(TAPS)
                    dve.wait_ge(*at("long_conv", 1))
                    dve.tensor_copy(att_col[:, 0:1], att_col[:, 0:1]).then_inc(S("conv_done"), 1)
                if n == 2:
                    dve.wait_ge(*at("ln_mean", 1))
                    st(dve.tensor_scalar(hid[:, 0, 0:T], ps[7][:, 0:T], 1.0 / D, None, ALU.mult))
                    st.sync()
                    dve.tensor_tensor(conv[:, :, :], conv[:, :, :], spread(hid[:, 0, 0:T], KT), ALU.subtract)\
                        .then_inc(S("ln_cen"), 1)
            inverse("ln", rstd[:, :], std[:, :])
            dve.wait_ge(*at("ln_cen", 1))
            dve.tensor_tensor(conv[:, :, :], conv[:, :, :], spread(rstd[:, :], KT), ALU.mult).then_inc(S("ln_n"), 1)
            for t in range(KT):
                dve.wait_ge(*at("c_yh", t + 1))
                dve.tensor_tensor(yl[:, t, :], conv[:, t, :], yh[:, t, :].bitcast(F32), ALU.subtract).then_inc(S("c_yl"), 1)
            for n in range(4):
                s = FIRST["conv_out"] + n
                dve.wait_ge(taken, s + 1)
                dve.wait_ge(*at("gate_a", n + 1))
                st(dve.tensor_tensor(pair(hid[:, n, :]), pair(ps[4 + n % 2][:, :]), qn[:, 2 * n:2 * n + 2, :], ALU.mult))
                st.sync()
                dve.wait_ge(*at("mixed_b", 4))
                dve.tensor_tensor(kn[:, 2 * n:2 * n + 2, :], kn[:, 2 * n:2 * n + 2, :], pair(hid[:, n, :]), ALU.add)\
                    .then_inc(S("mixed"), 1)
                sub(s + 3)
            dve.wait_ge(*at("mixed", 4))
            for t in range(KT):
                dve.wait_ge(*at("w_xh", t + 1))
                dve.tensor_tensor(xl[:, t, :], kn[:, t, :], xh[:, t, :].bitcast(F32), ALU.subtract).then_inc(S("w_xl"), 1)
            for n in range(4):
                sub(FIRST["w_out"] + n + 3)

            def add_normed(tag, src, gain):
                for b in range(4):
                    for t in (2 * b, 2 * b + 1):
                        ins = dve.scalar_tensor_tensor(qn[:, t, :], src(t), mods[:, gain, t:t + 1], rstd[:, :], ALU.mult, ALU.mult)
                    st(ins)
                    st.sync()
                    dve.tensor_tensor(resid[:, 2 * b:2 * b + 2, :], resid[:, 2 * b:2 * b + 2, :], qn[:, 2 * b:2 * b + 2, :],
                                      ALU.add).then_inc(S(tag), 1)

            inverse("y", rstd[:, :], std[:, :])
            add_normed("x3", lambda t: conv[:, t, :], 1)
            inverse("x3", rstd[:, :], std[:, :])
            dve.wait_ge(*at("x3", 4))
            for t in range(KT):
                st(dve.scalar_tensor_tensor(qn[:, t, :], resid[:, t, :], mods[:, 2, t:t + 1], rstd[:, :], ALU.mult, ALU.mult))
                st.sync()
                dve.tensor_scalar(qn[:, t, :], qn[:, t, :], ada[:, 24 + t:25 + t], None, ALU.add).then_inc(S("h2_f"), 1)
                dve.wait_ge(*at("h2_xh", t + 1))
                dve.tensor_tensor(xl[:, t, :], qn[:, t, :], xh[:, t, :].bitcast(F32), ALU.subtract).then_inc(S("h2_xl"), 1)

            s0 = FIRST["mlp_in"]

            def relu(s):
                dve.wait_ge(taken, s + 1)
                dve.tensor_scalar(hid[:, 0, :], ps[4][:, :], 0.0, None, ALU.max).then_inc(S("mlp_relu"), 1)

            def rest(count):
                dve.wait_ge(*at("mlp_relu", count))
                dve.tensor_tensor(hid[:, 1, :], hid[:, 0, :], hid[:, 0, :], ALU.mult).then_inc(S("mlp_sq"), 1)
                dve.wait_ge(*at("mlp_sq", count))
                dve.wait_ge(*at("mlp_fh", count))
                dve.tensor_tensor(fl[:, :, :], pair(hid[:, 1, :]), fh[:, :, :].bitcast(F32), ALU.subtract)\
                    .then_inc(S("mlp_fl"), 1)

            relu(s0)
            sub(s0 + 3)
            rest(1)
            with dve.Fori(0, (MLP_STEPS - 1) // SLOTS - 1) as i:
                for r in range(SLOTS):
                    s = s0 + 1 + 2 * r
                    relu(i * 6 + s)
                    sub_in_loop(s + 3, i, 6)
                    rest(i * 3 + (r + 2))
                    sub_in_loop(s + 4, i, 6)
            for k in range(MLP_STEPS - SLOTS, MLP_STEPS):
                s = s0 + 2 * k - 1
                relu(s)
                if s + 3 < N_SLABS:
                    sub(s + 3)
                rest(k + 1)
                if s + 4 < N_SLABS:
                    sub(s + 4)
            inverse("z", rstd[:, :], std[:, :])
            add_normed("x4", lambda t: ps[t // 2][:, (t % 2) * T:(t % 2 + 1) * T], 3)

        @block.tensor
        def _(pe):
            def wide(s, bank, x, y, tile_ready=None, tile_base=0, slab=None, m_tiles=2):
                slab = s if slab is None else slab
                pe.wait_ge(low_done, s + 1)
                n = KT * P * m_tiles
                h, l = (w[:, slab % SLOTS, 0:n].rearrange("p (k m) -> p k m", k=KT) for w in (wh, wl))
                for m in range(m_tiles):
                    for k in range(KT):
                        if tile_ready is not None and m == 0:
                            pe.wait_ge(*at(tile_ready, tile_base(k)))
                        for j, (w, r) in enumerate(((h, x), (h, y), (l, x))):
                            mm = pe.matmul(bank[:, m * T:(m + 1) * T], w[:, k, m * P:(m + 1) * P], r[:, k, :],
                                           start=(m == 0 and k == 0 and j == 0), stop=(k == KT - 1 and j == 2),
                                           skip_group_check=True)
                mm.then_inc(taken, 1)

            def deep(s, slab=None):
                slab = s if slab is None else slab
                pe.wait_ge(low_done, s + 1)
                h, l = (w[:, slab % SLOTS, :].rearrange("p (k m) -> p k m", k=2) for w in (wh, wl))
                for k in range(2):
                    for m in range(KT):
                        for w, r in ((h, fh), (h, fl), (l, fh)):
                            mm = pe.matmul(ps[m // 2][:, (m % 2) * T:(m % 2 + 1) * T], w[:, k, m * P:(m + 1) * P], r[:, k, :],
                                           start=False, stop=False, skip_group_check=True)
                mm.then_inc(taken, 1)

            def clear_sums():
                for b in range(4):
                    pe.matmul(ps[b][:, :], zero[0:1, 0:P], zero[0:1, :], start=True, stop=True, skip_group_check=True)

            def column_sums(n, src, k_tiles, out, ready, signal=True):
                pe.wait_ge(*at(*ready))
                for k in range(k_tiles):
                    mm = pe.matmul(out, ones, src(k), start=(k == 0), stop=(k == k_tiles - 1), skip_group_check=True)
                if signal:
                    mm.then_inc(S(n + "_stat"), 1)

            def one(k):
                return k + 1

            def ffn(name, n, prev_free):
                s0 = FIRST[name + "_gate"]
                wide(s0, ps[4], xh, xl, n + "_xl", one)
                column_sums(n, lambda k: sq[:, k, :], KT, ps[6][:, 0:T], (n + "_sq", 1))
                if prev_free:
                    pe.wait_ge(*at(*prev_free))
                wide(s0 + 1, ps[5], xh, xl)
                clear_sums()
                with pe.Fori(0, FF_STEPS - 1) as i:
                    s = s0 + 2
                    pe.wait_ge(*at(name + "_gate", i + 1))
                    wide(i * 3 + s, ps[4], xh, xl, slab=s)
                    pe.wait_ge(*at(name + "_up", i + 1))
                    wide(i * 3 + (s + 1), ps[5], xh, xl, slab=s + 1)
                    pe.wait_ge(*at(name + "_fl", i + 1))
                    deep(i * 3 + (s + 2), slab=s + 2)
                pe.wait_ge(*at(name + "_fl", FF_STEPS))
                deep(s0 + 3 * FF_STEPS - 1)

            pe.wait_ge(*at("con", 16))
            pe.wait_ge(*at("zero", 1))
            pe.wait_ge(*at("vec_loaded", 16 * N_VEC))
            for g in range(4):
                n = STAGE_ROWS[g]
                mm = pe.transpose(ps[0][:, g * P:g * P + n], stage[0:n, g, :], ident[0:n, 0:n])
            mm.then_inc(S("vec_turned"), 1)
            pe.wait_ge(*at("x_loaded", 16))
            xin = sq.rearrange("p (a b) t -> p a (b t)", a=2)
            for b in range(4):
                for t in (2 * b, 2 * b + 1):
                    for tk in range(2):
                        mm = pe.transpose(ps[4 + b][:, (t % 2) * T + tk * P:(t % 2) * T + (tk + 1) * P],
                                          xin[:, tk, t * P:(t + 1) * P], ident)
                mm.then_inc(S("x_turned"), 1)
            pe.wait_ge(*at("x_in", 4))
            pe.wait_ge(*at("vec", 1))
            ffn("ffn1", "n1", None)

            s0 = FIRST["mix"]

            def mix(n, **kw):
                if n >= 2:
                    pe.wait_ge(*at("mix_evac", n - 1))
                wide(s0 + n, ps[4 + n % 2], xh, xl, m_tiles=1 if n == MIX_AB else 2, **kw)

            mix(0, tile_ready="n2_xl", tile_base=one)
            column_sums("n2", lambda k: sq[:, k, :], KT, ps[6][:, 0:T], ("n2_sq", 1))
            for n in range(1, 9):
                mix(n)

            def row_sums(n, name, count, ready):
                pe.wait_ge(*at(*ready))
                sel = const(name, 8 * count).rearrange("p (t r) -> p t r", r=8)
                for t in range(count):
                    mm = pe.matmul(ps[0][0:8, 0:T], sel[:, t, :], sq[:, t, :], start=(t == 0), stop=(t == count - 1),
                                   skip_group_check=True)
                mm.then_inc(S(n + "_stat"), 1)

            def spread_rows(n, name, src, count, k_rows, banks=0):
                sel = const(name, P * count, k_rows).rearrange("p (t m) -> p t m", m=P)
                for t in range(count):
                    mm = pe.matmul(ps[banks + t // 2][:, (t % 2) * T:(t % 2 + 1) * T], sel[:, t, :], src,
                                   start=(t % 2 == 0), stop=True, skip_group_check=True)
                    if t % 2:
                        mm.then_inc(S(n), 1)

            pe.wait_ge(*at("ffn1_resid", 4))
            row_sums("qk", "row_of", 8, ("qk_sq", 4))
            mix(9)
            pe.wait_ge(*at("qk_row", 1))
            spread_rows("qk_spread", "row_sel", small[0:8, 7, :], 8, 8)
            mix(10)
            mix(11)
            pe.wait_ge(*at("g_cum", 1))
            pe.wait_ge(*at("qk_n", 4))
            pe.wait_ge(*at("beta", 1))
            spread_rows("g_spread", "row_sel", g_cum[0:4, :], 4, 4)
            spread_rows("b_spread", "row_sel", beta_row[0:4, :], 4, 4, banks=2)
            for q, src in enumerate((g_cum, beta_row)):
                for c in range(2):
                    pe.transpose(ps[6][:, 8 * q + 4 * c:8 * q + 4 * c + 4], src[0:4, c * CH:(c + 1) * CH], ident[0:4, 0:4])\
                        .then_inc(S("col_turned"), 1)
            mix(12)
            pe.wait_ge(*at("g_row", 2))
            row_sums("short", "grp_row_of", 4, ("short_sq", 1))
            mix(13)
            pe.wait_ge(*at("short_rstd", 1))
            pe.wait_ge(*at("kb", 2))
            spread_rows("short_spread", "grp_sel", small[0:8, 7, :], 4, 8)
            mix(14)

            def unit(m, u):
                return m[:, u * P:(u + 1) * P]

            def chan(m, u):
                c, h = u // HEADS, u % HEADS
                return m[:, h, c * CH:(c + 1) * CH]

            def per_unit(bank, name, lhs, rhs, second=None):
                for u in range(UNITS):
                    mm = pe.matmul(ps[bank + u // 4][:, (u % 4) * P:(u % 4 + 1) * P], lhs(u), rhs(u), start=(u % 4 == 0),
                                   stop=True, skip_group_check=True)
                    if u % 4 == 3:
                        mm.then_inc(S(name), 1)

            pe.wait_ge(*at("short_out", 2))
            per_unit(0, "lt_mm", lambda u: chan(k_n, u), lambda u: chan(kb, u))
            pe.wait_ge(*at("mix_evac", 14))
            for u in range(UNITS):
                mm = pe.transpose(unit(ps[2 + u // 4], u % 4), chan(qkv[:, 8:12, :], u), ident)
                if u % 4 == 3:
                    mm.then_inc(S("v_turned"), 1)
            pe.wait_ge(*at("lt", 2))
            per_unit(0, "at_mm", lambda u: chan(k_n, u), lambda u: chan(q_n, u))
            pe.wait_ge(*at("mix_evac", 15))
            for u in range(UNITS):
                mm = pe.transpose(unit(ps[4 + u // 4], u % 4), chan(k_n, u), ident)
                if u % 4 == 3:
                    mm.then_inc(S("k_turned"), 1)

            def modulate(tile, n):
                pe.wait_ge(*at(f"ada{n}_loaded", 8 * (tile - n) + 16))
                w = ada_raw[:, n, :].rearrange("p (k m) -> p k m", k=KT)
                for k in range(KT):
                    mm = pe.matmul(ps[7][:, bass.ds(tile, 1)], w[:, k, :], c_act[:, k:k + 1], start=(k == 0),
                                   stop=(k == KT - 1), skip_group_check=True)
                mm.then_inc(S("ada_taken"), 1)

            pe.wait_ge(*at("c_act", 1))
            for t in range(6):
                modulate(t, t % 2)
            pe.wait_ge(*at("at_done", 1))
            pe.wait_ge(*at("k_nat", 8))
            pe.wait_ge(*at("v_nat", 8))
            pe.wait_ge(*at("inv_start", 2))
            with pe.Fori(0, LEVELS) as i:
                pe.wait_ge(*at("inv_b", i + 1))
                per_unit(0, "inv_x", lambda u: unit(b_mat, u), lambda u: unit(t_mat, u))
                for n in range(3):
                    modulate(i * 6 + (6 + n), n % 2)
                pe.wait_ge(*at("inv_xv", i + 1))
                pe.wait_ge(*at("inv_xa", i + 1))
                per_unit(2, "inv_y", lambda u: unit(tt_mat, u), lambda u: unit(x_mat, u))
                per_unit(4, "inv_y", lambda u: unit(x_mat, u), lambda u: unit(tt_mat, u))
                for n in range(3, 6):
                    modulate(i * 6 + (6 + n), n % 2)
            pe.wait_ge(*at("inv_t", 4 * LEVELS))
            for h in range(HEADS):
                mm = pe.matmul(unit(ps[0], h), unit(tt_mat, h), unit(v_beta, h), start=(h == 0), stop=True, skip_group_check=True)
            mm.then_inc(S("v_mm"), 1)
            for h in range(HEADS):
                mm = pe.matmul(unit(ps[1], h), unit(k_be, h), unit(tt_mat, HEADS + h), start=(h == 0), stop=True,
                               skip_group_check=True)
            mm.then_inc(S("w_mm"), 1)
            pe.wait_ge(*at("v_new", 1))
            for h in range(HEADS):
                mm = pe.matmul(unit(ps[2], h), unit(k_dec, h), unit(v_new, h), start=(h == 0), stop=True, skip_group_check=True)
            mm.then_inc(S("s_mm"), 1)
            for h in range(HEADS):
                mm = pe.matmul(unit(ps[3], h), unit(v_new, h), unit(at_mat, h), start=(h == 0), stop=True, skip_group_check=True)
            mm.then_inc(S("o_mm"), 1)
            pe.wait_ge(*at("w_t", 1))
            pe.wait_ge(*at("state", 1))
            for h in range(HEADS):
                pe.matmul(unit(ps[4], h), unit(tt_mat, HEADS + h), unit(v_beta, HEADS + h), start=(h == 0), stop=False,
                          skip_group_check=True)
                mm = pe.matmul(unit(ps[4], h), unit(x_mat, h), unit(state, h), start=False, stop=True, skip_group_check=True)
            mm.then_inc(S("v_mm"), 1)
            pe.wait_ge(*at("v_new", 2))
            for h in range(HEADS):
                pe.matmul(unit(ps[5], h), unit(state, h), q_n[:, h, CH:2 * CH], start=(h == 0), stop=False, skip_group_check=True)
                mm = pe.matmul(unit(ps[5], h), unit(v_new, HEADS + h), unit(at_mat, HEADS + h), start=False, stop=True,
                               skip_group_check=True)
            mm.then_inc(S("o_mm"), 1)
            row_sums("o", "row_of", 4, ("o_sq", 1))
            pe.wait_ge(*at("o_rstd", 1))
            spread_rows("o_spread", "row_sel", small[0:8, 7, :], 4, 8)
            pe.wait_ge(*at("o_t", 2))
            for n in range(4):
                if n >= 2:
                    pe.wait_ge(*at("mix_resid", n - 1))
                wide(FIRST["mix_out"] + n, ps[4 + n % 2], xh, xl, "mo_xl" if n == 0 else None, lambda k: k // 2 + 1)
            pe.wait_ge(*at("mix_resid", 3))
            ffn("ffn2", "n3", ("mix_resid", 4))

            column_sums("f", lambda k: kn[:, k, :], KT, ps[6][:, 0:T], ("f_sq", 1))
            column_sums("f", lambda k: qn[:, k, :], KT, ps[7][:, 0:T], ("f_sq", 2))
            for n in range(4):
                s = FIRST["glu"] + 2 * n
                if n:
                    pe.wait_ge(*at("glu", n))
                wide(s, ps[4], xh, xl, "h_xl" if n == 0 else None, one)
                wide(s + 1, ps[5], xh, xl)
            s = FIRST["lat"]
            pe.wait_ge(*at("glu", 4))
            for n in range(3):
                if n == 2:
                    pe.wait_ge(*at("lat", 1))
                wide(s + n, ps[4 + n % 2], xh, xl)
            pe.wait_ge(*at("m2", 1))
            pe.wait_ge(*at("lat_sq", 1))
            for k in range(3):
                pe.matmul(ps[6][:, 0:T], ones, lat_sq[:, k, :], start=(k == 0), stop=(k == 2), skip_group_check=True)
            for k in range(2):
                mm = pe.matmul(ps[6][:, T:2 * T], ones, lat_sq[:, 3 + k, :], start=(k == 0), stop=(k == 1), skip_group_check=True)
            mm.then_inc(S("lat_stat"), 1)
            pe.wait_ge(*at("lat", 4))
            swap = const("swap", P)
            pe.matmul(ps[7][:, 0:T], swap, kr_raw, start=True, stop=True).then_inc(S("kr_swap"), 1)
            for n in range(3):
                s = FIRST["uq"] + n
                pe.wait_ge(low_done, s + 1)
                if n:
                    pe.wait_ge(*at("q", 2 * n))
                h, l = (w[:, s % SLOTS, 0:1536].rearrange("p (k m) -> p k m", k=3) for w in (wh, wl))
                for m in range(4):
                    for k in range(3):
                        if n == 0 and m == 0:
                            pe.wait_ge(*at("lat_yl", k + 1))
                        for j, (w, r) in enumerate(((h, yh), (h, yl), (l, yh))):
                            mm = pe.matmul(ps[4 + m // 2][:, (m % 2) * T:(m % 2 + 1) * T], w[:, k, m * P:(m + 1) * P], r[:, k, :],
                                           start=(m % 2 == 0 and k == 0 and j == 0), stop=(k == 2 and j == 2),
                                           skip_group_check=True)
                mm.then_inc(taken, 1)
            s = FIRST["ukv"]
            pe.wait_ge(low_done, s + 1)
            pe.wait_ge(*at("lat_yl", 5))
            h, l = (w[:, s % SLOTS, :].rearrange("p (k m) -> p k m", k=2) for w in (wh, wl))
            for m in range(NH):
                for k in range(2):
                    for j, (w, r) in enumerate(((h, yh), (h, yl), (l, yh))):
                        mm = pe.matmul(ps[m // 2][:, (m % 2) * T:(m % 2 + 1) * T], w[:, k, m * P:(m + 1) * P], r[:, 3 + k, :],
                                       start=(m % 2 == 0 and k == 0 and j == 0), stop=(k == 1 and j == 2), skip_group_check=True)
            mm.then_inc(taken, 1)
            pe.wait_ge(*at("q", 6))
            pe.wait_ge(*at("kr", 1))
            for b in range(2):
                pe.matmul(pair(ps[6 + b][:, :]), swap, qr_raw[:, 2 * b:2 * b + 2, :], start=True, stop=True).then_inc(S("q_swap"), 1)
            pe.wait_ge(low_done, s + 2)
            pe.wait_ge(*at("k", 4))
            h, l = (w[:, (s + 1) % SLOTS, :].rearrange("p (k m) -> p k m", k=2) for w in (wh, wl))
            for tk in range(2):
                for half in range(2):
                    for k in range(2):
                        for j, (w, r) in enumerate(((h, yh), (h, yl), (l, yh))):
                            mm = pe.matmul(ps[2 * tk + half][:, :], r[:, 3 + k, tk * P:(tk + 1) * P],
                                           w[:, k, half * 512:(half + 1) * 512], start=(k == 0 and j == 0),
                                           stop=(k == 1 and j == 2), skip_group_check=True)
            mm.then_inc(taken, 1)

            def scores(h):
                if h >= 2:
                    pe.wait_ge(*at("att_max", h - 1))
                bank, off = ps[h % 2], ROPE * (h % 2)
                for qt in range(2):
                    out = bank[:, qt * P:qt * P + (qt + 1) * P]
                    n = (qt + 1) * P
                    pe.matmul(out, qn[:, h, qt * P:(qt + 1) * P], kn[:, h, 0:n], start=(qt == 0), stop=False, skip_group_check=True)
                    mm = pe.matmul(out, qr[off:off + ROPE, h // 2, qt * P:(qt + 1) * P], kr[off:off + ROPE, 0:n], start=False,
                                   stop=True, skip_group_check=True)
                mm.then_inc(S("att_s"), 1)

            def turn(h):
                pe.wait_ge(*at("att_norm", h + 1))
                if h >= 2:
                    pe.wait_ge(*at("att_pt", h - 1))
                for j in range(3):
                    mm = pe.transpose(ps[2 + h % 2][:, j * P:(j + 1) * P], prob[h % 2][:, j * P:(j + 1) * P], ident)
                mm.then_inc(S("att_turned"), 1)

            def weigh(h):
                pe.wait_ge(*at("att_pt", h + 1))
                if h >= 2:
                    pe.wait_ge(*at("o_yl", h - 1))
                bank = ps[4 + h % 2]
                pe.matmul(bank[:, 0:T], v[:, 0, h * P:(h + 1) * P], prob_t[h % 2][:, 0:T], start=True, stop=False,
                          skip_group_check=True)
                pe.matmul(bank[:, P:T], v[:, 1, h * P:(h + 1) * P], prob_t[h % 2][:, T:T + P], start=False, stop=True,
                          skip_group_check=True).then_inc(S("att_o"), 1)

            pe.wait_ge(*at("v", 4))
            pe.wait_ge(*at("qr", 1))
            for h in range(NH + 2):
                if h < NH:
                    scores(h)
                if 1 <= h <= NH:
                    turn(h - 1)
                if h >= 2:
                    weigh(h - 2)

            def four(phase, x, y, freed, first=None, base=one, start_free=None):
                for n in range(4):
                    if n < 2 and start_free:
                        pe.wait_ge(*at(*start_free[n]))
                    if n >= 2:
                        pe.wait_ge(*at(freed, n - 1))
                    wide(FIRST[phase] + n, ps[4 + n % 2], x, y, first if n == 0 else None, base)

            four("gate_b", xh, xl, "gate_b", start_free=(("o_yl", 7), ("o_yl", 8)))
            four("attn_out", yh, yl, "mixed_b", start_free=(("gate_b", 3), ("gate_b", 4)))
            four("gate_a", xh, xl, "gate_a", start_free=(("mixed_b", 3), ("mixed_b", 4)))
            pe.wait_ge(*at("conv_done", 1))
            for k in range(KT):
                mm = pe.matmul(ps[7][:, 0:T], ones, conv[:, k, :], start=(k == 0), stop=(k == KT - 1), skip_group_check=True)
            mm.then_inc(S("ln_mean"), 1)
            column_sums("ln", lambda k: v_sq[:, k, :], KT, ps[6][:, 0:T], ("ln_sq", 1))
            four("conv_out", yh, yl, "mixed", "c_yl", one, start_free=(("gate_a", 3), ("gate_a", 4)))
            four("w_out", xh, xl, "y", "w_xl", one, start_free=(("mixed", 3), ("mixed", 4)))
            column_sums("y", lambda k: v_sq[:, k, :], KT, ps[6][:, 0:T], ("y_sq", 4))
            column_sums("x3", lambda k: v_sq[:, k, :], KT, ps[6][:, T:2 * T], ("x3_sq", 1))

            s0 = FIRST["mlp_in"]
            pe.wait_ge(*at("y", 4))
            clear_sums()
            wide(s0, ps[4], xh, xl, "h2_xl", one)
            with pe.Fori(0, (MLP_STEPS - 1) // SLOTS) as i:
                for r in range(SLOTS):
                    s = s0 + 1 + 2 * r
                    pe.wait_ge(*at("mlp_relu", i * 3 + (r + 1)))
                    wide(i * 6 + s, ps[4], xh, xl, slab=s)
                    pe.wait_ge(*at("mlp_fl", i * 3 + (r + 1)))
                    deep(i * 6 + (s + 1), slab=s + 1)
            pe.wait_ge(*at("mlp_fl", MLP_STEPS))
            deep(N_SLABS - 1)
            column_sums("z", lambda k: v_sq[:, k, :], KT, ps[6][:, 0:T], ("z_sq", 4))
            for tk in range(2):
                for half in range(2):
                    for t in range(4 * half, 4 * half + 4):
                        pe.wait_ge(*at("x4", t // 2 + 1))
                        if tk == 1:
                            pe.wait_ge(*at("z_std", 1))
                        mm = pe.transpose(ps[4 + 2 * tk + half][:, (t % 4) * P:(t % 4 + 1) * P],
                                          resid[:, t, tk * P:(tk + 1) * P], ident)
                    mm.then_inc(S("turned"), 1)


_INS = ["x", "ffn1_norm", "ffn1_w_in", "ffn1_w_out", "mix_norm", "w_mix_in", "conv_short_w", "conv_out_norm",
        "gdn_conv_w", "gdn_A_log", "gdn_dt_bias", "gdn_out_norm", "w_mix_out", "ffn2_norm", "ffn2_w_in", "ffn2_w_out",
        "final_norm", "c_2", "positions_2", "w_ada_2", "b_ada_2", "g_pre_mix_2", "g_post_mix_2", "g_pre_mlp_2",
        "g_post_mlp_2", "w_in_2", "conv_w_2", "conv_b_2", "conv_norm_g_2", "conv_norm_b_2", "w_conv_out_2",
        "q_norm_g_2", "w_uq_2", "kv_norm_g_2", "w_ukv_2", "w_attn_out_2", "w_out_2", "w_mlp_in_2", "w_mlp_out_2"]


def kernel(**inputs):
    import concourse.bacc as bacc
    from concourse.bass_utils import run_bass_kernel_spmd

    nc = bacc.Bacc("TRN2", target_bir_lowering=False, num_devices=1)
    arrays = {f"in_{n}": np.ascontiguousarray(inputs[n]) for n in _INS}
    arrays["in_table"] = constants()
    aps = {n[3:]: nc.dram_tensor(n, v.shape, mybir.dt.from_np(v.dtype), kind="ExternalInput").ap()
           for n, v in arrays.items()}
    aps["out"] = nc.dram_tensor("out", (1, T, D), F32, kind="ExternalOutput").ap()
    two_blocks(nc, aps)
    return run_bass_kernel_spmd(nc, [arrays], core_ids=[0]).results[0]["out"]
```

```python
from contextlib import ExitStack

import numpy as np

import concourse.bass as bass
from concourse import mybir

F32 = mybir.dt.float32
F32R = mybir.dt.float32r
BF16 = mybir.dt.bfloat16
I32 = mybir.dt.int32
ACT = mybir.ActivationFunctionType
ALU = mybir.AluOpType
AX_X = mybir.AxisListType.X

P = 128
T = 256
D = 1024
KT = D // P
EPS = 1e-6

D_FF = 2816
FF_STEPS = D_FF // 256
D_CONV = 512
HEADS = 4
DH = 128
CH = 128
UNITS = HEADS * (T // CH)
LEVELS = 7
MIX_COLS = 3592

TAPS = 31
PAD = TAPS - 1
NH = 8
NOPE = 128
ROPE = 64
Q_LAT = 384
KV_LAT = 256
D_MLP = 4096
MLP_STEPS = D_MLP // 256
POOL_TILES = 3
DVE_TILES = KT - POOL_TILES

N_VEC_0 = 8
N_VEC = 21
ATT_SCALE = float((NOPE + ROPE) ** -0.5)
SLOTS = 3
SLAB = 2048
ADA_TILES = 6 * KT
ADA_STEPS = ADA_TILES // 2
ADA_MIX = 4

_at = 0
C = {}
for _name, _width in (("ident", P), ("ones", P), ("eps", 1), ("inv_freq", 1), ("qk_scale", 1), ("half_pi", 1), ("swap", P), ("upper", P), ("levels", LEVELS * P),
                      ("causal", 3 * P), ("row_of", 64), ("grp_row_of", 32), ("row_sel", 8 * P),
                      ("grp_sel", 4 * P), ("restart", T)):
    C[_name] = _at
    _at += _width
N_CONST = _at
N_CONST_FIRST = C["swap"]

VECS = {}
_rows = [0, 0, 0, 0]
for _g, _name, _n in ((0, "ffn1_norm", 8), (0, "mix_norm", 8), (0, "conv_out_norm", 4), (0, "gdn_out_norm", 1),
                      (0, "ffn2_norm", 8), (0, "final_norm", 8), (0, "conv_short_w", 12), (0, "gdn_conv_w", 48),
                      (1, "g_pre_mix_2", 8), (1, "g_post_mix_2", 8), (1, "g_pre_mlp_2", 8), (1, "g_post_mlp_2", 8),
                      (1, "conv_b_2", 8), (1, "conv_norm_g_2", 8), (1, "conv_norm_b_2", 8), (1, "q_norm_g_2", 3),
                      (1, "kv_norm_g_2", 2), (1, "c_2", 8), (1, "b_ada_2", 48)):
    VECS[_name] = (_g, _rows[_g])
    _rows[_g] += _n
_rows[2] = _rows[3] = 124
STAGE_ROWS = tuple(_rows)


def constants():
    t = np.zeros((P, N_CONST), np.float32)
    p = np.arange(P)

    def put(name, a):
        t[:a.shape[0], C[name]:C[name] + a.shape[1]] = a

    put("ident", np.eye(P))
    put("ones", np.ones((P, P)))
    swap = np.zeros((P, P))
    for m in range(P):
        if m % ROPE < ROPE // 2:
            swap[m + ROPE // 2, m] = -1
        else:
            swap[m - ROPE // 2, m] = 1
    put("swap", swap)
    j, i = p[:, None], p[None, :]
    put("upper", (i >= j) * 1.0)
    for lev in range(LEVELS):
        s = 1 << lev
        m = (i // (2 * s) == j // (2 * s)) & ((i // s) % 2 == 1) & ((j // s) % 2 == 0)
        t[:, C["levels"] + lev * P:C["levels"] + (lev + 1) * P] = m
    diag = np.where(p[:, None] >= p[None, :], 0.0, -1e30)
    put("causal", np.concatenate([diag, np.zeros((P, P)), diag], 1))
    row_of = np.zeros((P, 8, 8))
    for r in range(8):
        row_of[:, r, r] = 1
    put("row_of", row_of.reshape(P, 64))
    grp = np.zeros((P, 4, 8))
    sel = np.zeros((8, 4, P))
    for r in range(4):
        grp[:64, r, 2 * r] = 1
        grp[64:, r, 2 * r + 1] = 1
        sel[2 * r, r, :64] = 1
        sel[2 * r + 1, r, 64:] = 1
    put("grp_row_of", grp.reshape(P, 32))
    put("grp_sel", sel.reshape(8, 512))
    rs = np.zeros((8, 8, P))
    for r in range(8):
        rs[r, r, :] = 1
    put("row_sel", rs.reshape(8, 1024))
    restart = np.ones((8, T))
    restart[:, ::CH] = 0
    put("restart", restart)
    freq = 1.0 / np.power(np.float32(10000.0), np.arange(0, ROPE, 2, dtype=np.float32) / np.float32(ROPE)).astype(np.float32)
    put("inv_freq", freq.astype(np.float32)[p % (ROPE // 2)][:, None])
    put("eps", np.full((P, 1), EPS))
    qk = np.ones((8, 1))
    qk[:HEADS] = DH ** -0.5
    put("qk_scale", qk)
    put("half_pi", np.full((P, 1), np.pi / 2))
    return t


def slab_plan():
    plan = []

    def ffn(name):
        plan.extend([(name + "_gate", 0), (name + "_up", 0)])
        for k in range(1, FF_STEPS):
            plan.extend([(name + "_gate", k), (name + "_up", k), (name + "_down", k - 1)])
        plan.append((name + "_down", FF_STEPS - 1))

    ffn("ffn1")
    plan.extend([("mix", n) for n in range(15)])
    plan.extend([("mix_out", n) for n in range(4)])
    ffn("ffn2")
    for phase, n in (("glu", 8), ("lat", 3), ("uq", 3), ("ukv", 2), ("gate_b", 4), ("attn_out", 4), ("gate_a", 4),
                     ("conv_out", 4), ("w_out", 4)):
        plan.extend([(phase, k) for k in range(n)])
    plan.append(("mlp_in", 0))
    for k in range(1, MLP_STEPS):
        plan.extend([("mlp_in", k), ("mlp_out", k - 1)])
    plan.append(("mlp_out", MLP_STEPS - 1))
    return plan


SEQUENCES = {
    "x_high": (("n1_xh", 8), ("n2_xh", 8), ("mo_xh", 4), ("n3_xh", 8), ("h_xh", 8), ("w_xh", 8), ("h2_xh", 8)),
    "x_low": (("n1_xl", 8), ("n2_xl", 8), ("mo_xl", 4), ("n3_xl", 8), ("h_xl", 8), ("w_xl", 8), ("h2_xl", 8)),
    "y_high": (("lat_yh", 5), ("o_yh", 8), ("c_yh", 8)),
    "y_low": (("lat_yl", 5), ("o_yl", 8), ("c_yl", 8)),
    "squares": (("n1_sq", 4), ("n2_sq", 4), ("n3_sq", 4), ("f_sq", 4)),
    "sums": (("n1_stat", 1), ("n2_stat", 1), ("qk_stat", 1), ("short_stat", 1), ("o_stat", 1), ("n3_stat", 1),
             ("f_stat", 2), ("lat_stat", 1), ("ln_stat", 1), ("y_stat", 1), ("x3_stat", 1), ("z_stat", 1)),
    "roots": (("n1_std", 1), ("n2_std", 1), ("qk_std", 1), ("short_std", 1), ("o_std", 1), ("n3_std", 1), ("f_std", 1),
              ("g_std", 1), ("lat_std", 2), ("ln_std", 1), ("y_std", 1), ("x3_std", 1), ("z_std", 1)),
    "inverses": (("n1_rstd", 1), ("n2_rstd", 1), ("qk_rstd", 1), ("short_rstd", 1), ("o_rstd", 1), ("n3_rstd", 1),
                 ("f_rstd", 1), ("g_rstd", 1), ("ln_rstd", 1), ("y_rstd", 1), ("x3_rstd", 1), ("z_rstd", 1)),
    "resid_ready": (("x_in", 4), ("ffn1_resid", 4), ("mix_resid", 4), ("ffn2_resid", 4), ("x3", 4), ("x4", 4)),
    "hidden_gate": (("ffn1_gate", FF_STEPS), ("ffn2_gate", FF_STEPS), ("mlp_relu", MLP_STEPS)),
    "hidden_up": (("ffn1_up", FF_STEPS), ("ffn2_up", FF_STEPS)),
    "hidden_silu": (("ffn1_silu", FF_STEPS), ("ffn2_silu", FF_STEPS)),
    "hidden": (("ffn1_h", FF_STEPS), ("ffn2_h", FF_STEPS), ("mlp_sq", MLP_STEPS)),
    "hidden_high": (("ffn1_fh", FF_STEPS), ("ffn2_fh", FF_STEPS), ("mlp_fh", MLP_STEPS)),
    "hidden_low": (("ffn1_fl", FF_STEPS), ("ffn2_fl", FF_STEPS), ("mlp_fl", MLP_STEPS)),
}
SHARED = {}
for _sem, _stages in SEQUENCES.items():
    _n = 0
    for _stage, _count in _stages:
        SHARED[_stage] = (_sem, _n)
        _n += _count

PLAN = slab_plan()
FIRST = {}
for _s, (_phase, _step) in enumerate(PLAN):
    FIRST.setdefault(_phase, _s)
N_SLABS = len(PLAN)
MIX_COL = [1536, 1792, 2048, 2304, 2560, 2816, -1, 512, 768, 1024, 1280, 0, 256, 3072, 3328]
MIX_AB = 6
ADA_AFTER = (4, 8, 12, 14)


def slab_dmas(s):
    phase, step = PLAN[s]
    if phase == "mix" and step == MIX_AB:
        return 2
    if phase == "lat" and step == 2:
        return 3
    return {"uq": 3, "ukv": 2}.get(phase, 1)


def landed(s):
    return 16 * sum(slab_dmas(n) for n in range(s % SLOTS, s + 1, SLOTS))


def two_pi():
    c1 = 6.28125
    c2 = float((np.float32(2 * np.pi - c1).view(np.uint32) & np.uint32(0xFFFFF000)).view(np.float32))
    return c1, c2, float(np.float32(2 * np.pi - c1 - c2))


class Steps:

    def __init__(self, engine, semaphore):
        self.engine, self.semaphore, self.n = engine, semaphore, 0

    def __call__(self, instruction):
        instruction.then_inc(self.semaphore, 1)
        self.n += 1

    def sync(self):
        self.engine.wait_ge(self.semaphore, self.n)


def slab_floats(s):
    phase, step = PLAN[s]
    if phase == "mix" and step == MIX_AB:
        return KT * P
    if phase == "uq":
        return 3 * 512
    return SLAB


def two_blocks(nc, a):
    with ExitStack() as ctx:
        def sem(name):
            return ctx.enter_context(nc.semaphore(name))

        def sb(name, shape, dt=F32, where=ctx):
            return where.enter_context(nc.sbuf_tensor(name, shape, dt))

        con = sb("con", [P, N_CONST])
        raw = sb("raw", [P, SLOTS, SLAB])
        wh = sb("wh", [P, SLOTS, SLAB], F32R)
        wl = sb("wl", [P, SLOTS, SLAB], F32R)
        resid = sb("resid", [P, KT, T])
        xh = sb("xh", [P, KT, T], F32R)
        xl = sb("xl", [P, KT, T], F32R)
        vec = sb("vec", [P, 4, P])
        ada_raw = sb("ada_raw", [P, KT, 256])
        ada_sum = sb("ada_sum", [P, 256])
        ada = sb("ada", [P, ADA_TILES])
        mods = sb("mods", [P, 4, KT])
        c_act = sb("c_act", [P, KT])
        rstd = sb("rstd", [P, T])
        std = sb("std", [P, T])
        zero = sb("zero", [1, 512], BF16)
        fh = sb("fh", [P, 2, T], F32R)
        fl = sb("fl", [P, 2, T], F32R)
        hid = sb("hid", [P, 4, 2 * T])
        a_log = sb("a_log", [4, 2])
        g_cum = sb("g_cum", [4, T])
        beta_row = sb("beta_row", [4, T])
        att_col = sb("att_col", [P, 16])

        with ExitStack() as first:
            work1 = sb("work1", [P, 17600], where=first)
        yh = sb("yh", [P, KT, T], F32R)
        yl = sb("yl", [P, KT, T], F32R)
        work2 = sb("work2", [P, 13560])
        pt_mem = ada_raw[:, :, :].rearrange("p k m -> p (k m)")
        pool_mem = pt_mem[:, 6 * P:6 * P + POOL_TILES * T]
        ps = [ctx.enter_context(nc.psum_tensor(f"ps{i}", [P, 512], F32)) for i in range(8)]

        def const(name, width, rows=P):
            return con[0:rows, C[name]:C[name] + width]

        ident, ones = const("ident", P), const("ones", P)
        eps = const("eps", 1)

        def col(name, t, rows=P):
            g, r = VECS[name]
            return vec[0:rows, g, r + t:r + t + 1]

        def tap(k, t):
            r = k * KT + t
            return vec[:, 2 + r // 124, r % 124:r % 124 + 1]

        def pair(ap):
            return ap.rearrange("p (m t) -> p m t", m=2)

        def spread(ap, n):
            return ap.unsqueeze(1).to_broadcast([ap.shape[0], n, ap.shape[1]])

        used = {"w1": 0, "w2": 0}

        def w1(n):
            used["w1"] += n
            return work1[:, used["w1"] - n:used["w1"]]

        def w2(n):
            used["w2"] += n
            return work2[:, used["w2"] - n:used["w2"]]

        def tiles(ap, n):
            return ap.rearrange("p (n t) -> p n t", n=n)

        QW = T + 3
        w_qkvp = w1(12 * QW)
        qkvp = tiles(w_qkvp, 12)
        t_mat, tt_mat, x_mat = (w_qkvp[:, n * 1024:(n + 1) * 1024] for n in range(3))
        qkv = tiles(w1(12 * T), 12)
        w_sq = w1(2048)
        sq = tiles(w_sq, KT)
        gz = tiles(w1(1024), 4)
        w_cb = w1(1024)
        cb = tiles(w_cb, 4)
        w_cc = w1(1024)
        cc = tiles(w_cc, 4)
        mpad = tiles(w1(4 * (T + 2)), 4)
        g_row = tiles(w1(1024), 4)
        w_kb = w1(1024)
        kb = tiles(w_kb, 4)
        dt_mat = w1(1024)
        lt_mat = w1(1024)
        at_mat = w1(1024)
        q_n, k_n = qkv[:, 0:4, :], qkv[:, 4:8, :]
        v_beta = qkv[:, 8:12, :].rearrange("p n t -> p (n t)")
        k_be = qkv[:, 4:6, :].rearrange("p n t -> p (n t)")
        k_dec = qkv[:, 6:8, :].rearrange("p n t -> p (n t)")
        state = dt_mat[:, 0:512]
        exp_g = tiles(w_sq[:, 0:512], 4)
        o_t = g_row
        v_new = w_kb
        cols = w1(48)
        small = tiles(hid[0:8, :, :].rearrange("p n t -> p (n t)"), 8)
        b_mat = w_sq[:, 0:1024]

        UW = T + PAD
        upad = tiles(w2(KT * UW), KT)
        conv = tiles(w2(2048), KT)
        w_qn = w2(2048)
        qn = tiles(w_qn, KT)
        w_kn = w2(2048)
        kn = tiles(w_kn, KT)
        w_qr = w2(2048)
        qr_raw = tiles(w_qr[:, 0:1024], 4)
        qr = tiles(w_qr[:, 1024:2048], 4)
        w_v = w2(2048)
        v = tiles(w_v, 2)
        kr_raw = w2(T)
        kr = w2(T)
        cosines = w2(T)
        sines = w2(T)

        stage = tiles(lt_mat[:, 0:512], 4)
        lat = tiles(w_v[:, 0:5 * T], 5)
        lat_sq = tiles(w_qr[:, 0:5 * T], 5)
        v_sq = tiles(w_v, KT)
        upad_out = w_qr.rearrange("p (a n) -> p a n", a=2)
        score = [hid[:, n, 0:3 * P] for n in range(2)]
        prob = [hid[:, 2 + n, 0:3 * P] for n in range(2)]

        prob_t = [pt_mem[:, n * 3 * P:(n + 1) * 3 * P] for n in range(2)]
        work_pool = pool_mem
        assert used["w1"] <= 17600 and used["w2"] <= 13560, used

        named = {}

        def S(name):
            name = SHARED.get(name, (name, 0))[0]
            if name not in named:
                named[name] = sem("s_" + name)
            return named[name]

        def at(name, count):
            return S(name), count + SHARED.get(name, (name, 0))[1]

        slot_loaded = [sem(f"slot{i}_loaded") for i in range(SLOTS)]
        high_done = sem("high_done")
        low_done = sem("low_done")
        taken = sem("taken")
        s_vstep, s_astep, s_pstep = sem("vector_step"), sem("scalar_step"), sem("pool_step")

        dram = {n: a[n][0] for n in ("ffn1_w_in", "ffn1_w_out", "ffn2_w_in", "ffn2_w_out", "w_mix_in", "w_mix_out",
                                     "w_ada_2", "w_in_2", "w_conv_out_2", "w_uq_2", "w_ukv_2", "w_attn_out_2",
                                     "w_out_2", "w_mlp_in_2", "w_mlp_out_2")}
        rows = {n: w.rearrange("(k p) n -> p k n", p=P) for n, w in dram.items()}
        x_rows = a["x"][0].rearrange("(k p) n -> p k n", p=P)
        out_rows = a["out"][0].rearrange("(k p) n -> p k n", p=P)
        gu, gq = 0, 2048

        block = ctx.enter_context(nc.Block())

        @block.sync
        def _(sp):
            def slot(s, k):
                n = SLAB if k != 3 else 1536
                return raw[:, s % SLOTS, 0:n].rearrange("p (k m) -> p k m", k=k)

            def free(s):
                if not isinstance(s, int) or s >= SLOTS:
                    sp.wait_ge(low_done, s - SLOTS + 1)

            def wide(s, slot_of, w, c0):
                free(s)
                sp.dma_start(slot(slot_of, KT), rows[w][:, :, bass.ds(c0, 256)]).then_inc(slot_loaded[slot_of % SLOTS], 16)

            def deep(s, slot_of, w, step):
                free(s)
                sp.dma_start(slot(slot_of, 2), rows[w][:, bass.ds(step * 2, 2), :]).then_inc(slot_loaded[slot_of % SLOTS], 16)

            def modulation(step):
                if not isinstance(step, int) or step:
                    sp.wait_ge(*at("ada_free", step))
                sp.dma_start(ada_raw[:, :, :], rows["w_ada_2"][:, :, bass.ds(step * 256, 256)]).then_inc(S("ada_loaded"), 16)

            def ffn(name, w_in, w_out, start):
                s0 = FIRST[name + "_gate"]
                wide(s0, s0, w_in, 0)
                wide(s0 + 1, s0 + 1, w_in, D_FF)
                modulation(0 if name == "ffn1" else FF_STEPS - 1 + ADA_MIX)
                for k in range(1, start):
                    s = s0 + 3 * k - 1
                    wide(s, s, w_in, 256 * k)
                    wide(s + 1, s + 1, w_in, D_FF + 256 * k)
                    deep(s + 2, s + 2, w_out, k - 1)
                with sp.Fori(0, FF_STEPS - start) as i:
                    s = s0 + 3 * start - 1
                    wide(s + i * 3, s, w_in, i * 256 + 256 * start)
                    wide(s + 1 + i * 3, s + 1, w_in, i * 256 + (D_FF + 256 * start))
                    deep(s + 2 + i * 3, s + 2, w_out, i + (start - 1))
                    modulation(i + (1 if name == "ffn1" else FF_STEPS + ADA_MIX))
                s = s0 + 3 * FF_STEPS - 1
                deep(s, s, w_out, FF_STEPS - 1)

            sp.dma_start(sq.rearrange("p (a b) t -> p a (b t)", a=2), x_rows).then_inc(S("x_loaded"), 16)
            ffn("ffn1", "ffn1_w_in", "ffn1_w_out", 2)
            for n, c0 in enumerate(MIX_COL):
                s = FIRST["mix"] + n
                if n == MIX_AB:
                    free(s)
                    dst = raw[:, s % SLOTS, 0:KT * P].rearrange("p (k m) -> p k m", k=KT)
                    for m, c in ((0, 3584), (32, 3588)):
                        sp.dma_start(dst[:, :, m:m + HEADS], rows["w_mix_in"][:, :, c:c + HEADS])\
                            .then_inc(slot_loaded[s % SLOTS], 16)
                else:
                    wide(s, s, "w_mix_in", c0)
                if n % 4 == 3:
                    modulation(FF_STEPS - 1 + n // 4)
            modulation(FF_STEPS - 1 + 3)
            for n in range(4):
                wide(FIRST["mix_out"] + n, FIRST["mix_out"] + n, "w_mix_out", 256 * n)
            ffn("ffn2", "ffn2_w_in", "ffn2_w_out", 2)
            for n in range(4):
                s = FIRST["glu"] + 2 * n
                wide(s, s, "w_in_2", 256 * n)
                wide(s + 1, s + 1, "w_in_2", 1024 + 256 * n)
            sp.wait_ge(*at("ffn2_resid", 4))
            sp.dma_start(cosines.bitcast(I32), a["positions_2"].to_broadcast([P, T])).then_inc(S("pos_loaded"), 16)
            s = FIRST["lat"]
            wide(s, s, "w_in_2", gq)
            wide(s + 1, s + 1, "w_in_2", gq + 256)
            free(s + 2)
            for m, c, n in ((0, gq + 512, 128), (128, gq + 640, ROPE), (192, gq + 640, ROPE)):
                sp.dma_start(slot(s + 2, KT)[:, :, m:m + n], rows["w_in_2"][:, :, c:c + n])\
                    .then_inc(slot_loaded[(s + 2) % SLOTS], 16)
            uq = rows["w_uq_2"].rearrange("p k (h c) -> p k h c", c=NOPE + ROPE)
            for n in range(3):
                s = FIRST["uq"] + n
                free(s)
                for k in range(3):
                    dst = slot(s, 3)[:, k, :]
                    if n < 2:
                        dst, src = dst.rearrange("p (h c) -> p h c", h=4), uq[:, k, 4 * n:4 * n + 4, 0:NOPE]
                    else:
                        dst, src = dst.rearrange("p (h c) -> p h c", h=NH), uq[:, k, :, NOPE:NOPE + ROPE]
                    sp.dma_start(dst, src).then_inc(slot_loaded[s % SLOTS], 16)
            ukv = rows["w_ukv_2"].rearrange("p k (h c) -> p k h c", c=2 * P)
            for n in range(2):
                s = FIRST["ukv"] + n
                free(s)
                for k in range(2):
                    dst = slot(s, 2)[:, k, :].rearrange("p (h c) -> p h c", h=NH)
                    sp.dma_start(dst, ukv[:, k, :, n * P:(n + 1) * P]).then_inc(slot_loaded[s % SLOTS], 16)
            for phase, w, c0 in (("gate_b", "w_in_2", 3776), ("attn_out", "w_attn_out_2", 0), ("gate_a", "w_in_2", 2752),
                                 ("conv_out", "w_conv_out_2", 0), ("w_out", "w_out_2", 0)):
                for n in range(4):
                    wide(FIRST[phase] + n, FIRST[phase] + n, w, c0 + 256 * n)
            s0 = FIRST["mlp_in"]
            wide(s0, s0, "w_mlp_in_2", 0)
            with sp.Fori(0, (MLP_STEPS - 1) // SLOTS) as i:
                for r in range(SLOTS):
                    s = s0 + 1 + 2 * r
                    wide(s + i * 6, s, "w_mlp_in_2", i * 768 + 256 * (r + 1))
                    deep(s + 1 + i * 6, s + 1, "w_mlp_out_2", i * 3 + r)
            deep(N_SLABS - 1, N_SLABS - 1, "w_mlp_out_2", MLP_STEPS - 1)
            for tk in range(2):
                sp.wait_ge(*at("out_ready", 4 * (tk + 1)))
                sp.dma_start(out_rows[:, tk, :], upad_out[:, tk, :]).then_inc(S("stored"), 16)
            sp.wait_ge(*at("stored", 32))

        @block.gpsimd
        def _(pool):
            ps_ = Steps(pool, s_pstep)
            pool.memset(zero[:, :], 0.0).then_inc(S("zero"), 1)
            pool.memset(qkvp[:, :, 0:3], 0.0).then_inc(S("pads"), 1)
            pool.memset(mpad[:, :, 0:2], 0.0).then_inc(S("pads"), 1)
            def modulation(step):
                flat = ada_raw[:, :, :].rearrange("p k m -> p (k m)")
                pool.wait_ge(*at("ada_loaded", step * 16 + 16))
                pool.tensor_tensor(ada_raw[:, :, :], ada_raw[:, :, :], c_act[:, :].unsqueeze(2).to_broadcast([P, KT, 256]),
                                   ALU.mult).then_inc(S("ada_part"), 1)
                pool.wait_ge(*at("ada_part", step * 3 + 1))
                pool.tensor_tensor(flat[:, 0:1024], flat[:, 0:1024], flat[:, 1024:2048], ALU.add).then_inc(S("ada_part"), 1)
                pool.wait_ge(*at("ada_part", step * 3 + 2))
                pool.tensor_tensor(flat[:, 0:512], flat[:, 0:512], flat[:, 512:1024], ALU.add).then_inc(S("ada_part"), 1)
                pool.wait_ge(*at("ada_part", step * 3 + 3))
                if not isinstance(step, int) or step:
                    pool.wait_ge(*at("ada_taken", step))
                pool.tensor_tensor(ada_sum[:, :], flat[:, 0:256], flat[:, 256:512], ALU.add).then_inc(S("ada_free"), 1)

            def squares(n, ready, dst):
                for b in range(4):
                    pool.wait_ge(*at(ready, b + 1))
                    pool.tensor_tensor(dst[:, 2 * b:2 * b + 2, :], resid[:, 2 * b:2 * b + 2, :], resid[:, 2 * b:2 * b + 2, :],
                                       ALU.mult).then_inc(S(n + "_sq"), 1)

            squares("n1", "x_in", sq)
            pool.dma_start(con[:, N_CONST_FIRST:], a["table"][:, N_CONST_FIRST:]).then_inc(S("con_rest"), 16)
            pool.wait_ge(*at("c_act", 1))
            modulation(0)
            with pool.Fori(0, FF_STEPS - 2) as i:
                modulation(i + 1)
            squares("n2", "ffn1_resid", sq)
            for n in range(ADA_MIX - 1):
                modulation(FF_STEPS - 1 + n)
            pool.wait_ge(*at("mix_evac", 13))
            body = mpad[:, :, 2:2 + T]
            ps_(pool.tensor_tensor(body, body, cc[:, :, :], ALU.mult))
            ps_.sync()
            for k in range(3):
                for t in range(4):
                    dst = cc if k == 0 else g_row
                    ins = pool.tensor_scalar(dst[:, t, :], mpad[:, t, k:k + T], col("conv_short_w", 4 * k + t), None, ALU.mult)
                ps_(ins)
                ps_.sync()
                if k:
                    ps_(pool.tensor_tensor(cc[:, :, :], cc[:, :, :], g_row[:, :, :], ALU.add))
                    ps_.sync()
            pool.tensor_tensor(cc[:, :, :], cc[:, :, :], cb[:, :, :], ALU.mult).then_inc(S("short_y"), 1)
            pool.wait_ge(*at("short_y", 1))
            pool.tensor_tensor(sq[:, 4:8, :], cc[:, :, :], cc[:, :, :], ALU.mult).then_inc(S("short_sq"), 1)
            modulation(FF_STEPS + 2)
            squares("n3", "mix_resid", sq)
            with pool.Fori(0, FF_STEPS - 1) as i:
                modulation(i + (FF_STEPS - 1 + ADA_MIX))
            squares("f", "ffn2_resid", kn)
            pool.wait_ge(*at("ffn2_resid", 4))
            pool.memset(upad[:, :, 0:PAD], 0.0).then_inc(S("upads"), 1)
            tmp = tiles(work_pool[:, :], POOL_TILES)
            pool.wait_ge(*at("glu", 4))
            for k in range(TAPS):
                for t in range(DVE_TILES, KT):
                    dst = conv[:, t, :] if k == 0 else tmp[:, t - DVE_TILES, :]
                    if k == 0:
                        ins = pool.tensor_scalar(dst, upad[:, t, k:k + T], tap(k, t), col("conv_b_2", t), ALU.mult, ALU.add)
                    else:
                        ins = pool.tensor_scalar(dst, upad[:, t, k:k + T], tap(k, t), 0.0, ALU.mult, ALU.add)
                ps_(ins)
                ps_.sync()
                if k:
                    ins = pool.tensor_tensor(conv[:, DVE_TILES:KT, :], conv[:, DVE_TILES:KT, :], tmp, ALU.add)
                    if k == TAPS - 1:
                        ins.then_inc(S("long_conv"), 1)
                    else:
                        ps_(ins)
                        ps_.sync()

        @block.scalar
        def _(act):
            st = Steps(act, s_astep)

            def cast(s):
                act.wait_ge(slot_loaded[s % SLOTS], landed(s))
                if s >= SLOTS:
                    act.wait_ge(taken, s - SLOTS + 1)
                n = slab_floats(s)
                act.activation(wh[:, s % SLOTS, 0:n], raw[:, s % SLOTS, 0:n], ACT.Copy).then_inc(high_done, 1)

            def cast_in_loop(s, i, per, count):
                act.wait_ge(slot_loaded[s % SLOTS], i * (16 * count) + landed(s))
                act.wait_ge(taken, i * per + (s - SLOTS + 1))
                act.activation(wh[:, s % SLOTS, :], raw[:, s % SLOTS, :], ACT.Copy).then_inc(high_done, 1)

            def norm_in(n, ready, gain):
                for t in range(KT):
                    if t % 2 == 0:
                        act.wait_ge(*at(ready, t // 2 + 1))
                    act.activation(xh[:, t, :], resid[:, t, :], ACT.Copy, scale=col(gain, t)).then_inc(S(n + "_xh"), 1)

            def root(n, src, dst, width):
                act.wait_ge(*at(n + "_stat", 1))
                act.activation(dst, src, ACT.Sqrt, scale=1.0 / width, bias=eps[0:dst.shape[0], :]).then_inc(S(n + "_std"), 1)

            def ffn(name):
                s0 = FIRST[name + "_gate"]

                def silu(count):
                    act.wait_ge(*at(name + "_gate", count))
                    act.activation(hid[:, 1, :], hid[:, 0, :], ACT.Silu).then_inc(S(name + "_silu"), 1)

                def round_hidden(count):
                    act.wait_ge(*at(name + "_h", count))
                    act.activation(fh[:, :, :], pair(hid[:, 3, :]), ACT.Copy).then_inc(S(name + "_fh"), 1)

                cast(s0 + 3)
                silu(1)
                if name == "ffn1":
                    g, r = VECS["c_2"]
                    act.wait_ge(*at("vec", 2))
                    act.activation(c_act[:, :], vec[:, g, r:r + KT], ACT.Silu).then_inc(S("c_act"), 1)
                cast(s0 + 4)
                round_hidden(1)
                with act.Fori(0, FF_STEPS - 1) as i:
                    s = s0 + 2
                    cast_in_loop(s + 3, i, 3, 1)
                    silu(i + 2)
                    cast_in_loop(s + 4, i, 3, 1)
                    act.wait_ge(taken, i * 3 + (s + 3))
                    round_hidden(i + 2)
                    cast_in_loop(s + 5, i, 3, 1)
                if name == "ffn2":
                    cast(s0 + 3 * FF_STEPS + 2)

            act.dma_start(con[:, 0:N_CONST_FIRST], a["table"][:, 0:N_CONST_FIRST]).then_inc(S("con"), 16)
            n_vec = 0
            for name, (g, r) in VECS.items():
                src = a[name]
                if name == "conv_short_w" or name == "gdn_conv_w":
                    src = src[0].rearrange("k (t p) -> (k t) p", p=P)
                elif name == "final_norm":
                    src = src.rearrange("(t p) -> t p", p=P)
                elif name == "gdn_out_norm":
                    src = src
                else:
                    src = src.rearrange("a (t p) -> (a t) p", p=P)
                act.dma_start(stage[r:r + src.shape[0], g, :], src).then_inc(S(f"vec{g}_loaded"), 16)
                n_vec += 1
            taps = a["conv_w_2"][0].rearrange("k (t p) -> (k t) p", p=P)
            for g in range(2):
                act.dma_start(stage[0:124, 2 + g, :], taps[g * 124:(g + 1) * 124, :]).then_inc(S("vec1_loaded"), 16)
                n_vec += 1
            assert n_vec == N_VEC
            act.dma_start(a_log[:, 0:1], a["gdn_A_log"].rearrange("a h -> h a")).then_inc(S("small_loaded"), 16)
            act.dma_start(a_log[:, 1:2], a["gdn_dt_bias"].rearrange("a h -> h a")).then_inc(S("small_loaded"), 16)
            act.wait_ge(*at("vec", 1))
            norm_in("n1", "x_in", "ffn1_norm")
            for s in range(SLOTS):
                cast(s)
            root("n1", ps[6][:, 0:T], std[:, :], D)
            ffn("ffn1")
            norm_in("n2", "ffn1_resid", "mix_norm")
            cast(FIRST["mix"] + 2)
            root("n2", ps[6][:, 0:T], std[:, :], D)
            s0 = FIRST["mix"]

            def silu_qkv(n):
                act.wait_ge(*at("conv4_done", 2 * (n + 1)))
                act.activation(qkv[:, 2 * n:2 * n + 2, :], qkv[:, 2 * n:2 * n + 2, :], ACT.Silu).then_inc(S("qkv_silu"), 1)
                if n < 4:
                    act.wait_ge(*at("qkv_silu", n + 1))
                    if n == 0:
                        act.wait_ge(*at("n2_stat", 1))
                    act.activation(sq[:, 2 * n:2 * n + 2, :], qkv[:, 2 * n:2 * n + 2, :], ACT.Square).then_inc(S("qk_sq"), 1)

            for n in range(6):
                cast(s0 + n + 3)
                if n:
                    silu_qkv(n - 1)
            cast(s0 + 6 + 3)
            silu_qkv(5)
            root("qk", ps[0][0:8, 0:T], small[0:8, 6, :], 1)
            act.wait_ge(*at("small_loaded", 32))
            act.wait_ge(*at("ab_abs", 1))
            st(act.activation(a_log[:, 0:1], a_log[:, 0:1], ACT.Exp))
            act.activation(small[0:4, 2, :], small[0:4, 1, :], ACT.Exp).then_inc(S("ab_exp"), 1)
            act.wait_ge(*at("ab_one", 1))
            act.activation(small[0:4, 4, :], small[0:4, 3, :], ACT.Ln).then_inc(S("ab_ln"), 1)
            act.activation(beta_row[0:4, :], small[0:4, 5, :], ACT.Sigmoid).then_inc(S("beta"), 1)
            cast(s0 + 7 + 3)
            cast(s0 + 8 + 3)
            for n in range(2):
                act.wait_ge(*at("g_spread", n + 1))
                act.activation(g_row[:, 2 * n:2 * n + 2, :], pair(ps[n][:, :]), ACT.Copy).then_inc(S("g_row"), 1)
            cast(s0 + 9 + 3)
            act.wait_ge(*at("dt_diff", 1))
            act.activation(dt_mat, dt_mat, ACT.Exp).then_inc(S("dt_exp"), 1)
            act.activation(cols[:, 16:20], cols[:, 4:8], ACT.Exp).then_inc(S("g_exp"), 1)
            act.activation(cols[:, 20:24], cols[:, 24:28], ACT.Exp).then_inc(S("g_exp"), 1)
            act.activation(exp_g, g_row[:, :, CH:2 * CH], ACT.Exp).then_inc(S("g_exp"), 1)
            cast(s0 + 10 + 3)
            act.wait_ge(*at("v_turned", 2))
            for u in range(UNITS):
                act.activation(v_beta[:, u * P:(u + 1) * P], ps[2 + u // 4][:, (u % 4) * P:(u % 4 + 1) * P], ACT.Copy,
                               scale=cols[:, 8 + u:9 + u]).then_inc(S("v_nat"), 1)
            cast(s0 + 11 + 3)
            act.wait_ge(*at("cols_ready", 1))
            act.wait_ge(*at("at_done", 1))
            act.wait_ge(*at("k_turned", 2))
            for u in range(UNITS):
                dst = k_dec[:, u * P:(u + 1) * P] if u < 4 else k_be[:, (u - 4) * P:(u - 3) * P]
                scale = cols[:, 20 + u:21 + u] if u < 4 else cols[:, 28 + u - 4:29 + u - 4]
                act.activation(dst, ps[2 + u // 4][:, (u % 4) * P:(u % 4 + 1) * P], ACT.Copy, scale=scale)\
                    .then_inc(S("k_nat"), 1)
            cast(s0 + 12 + 3)
            with act.Fori(0, LEVELS) as i:
                act.wait_ge(*at("inv_x", i * 2 + 2))
                act.activation(x_mat[:, 512:1024], ps[1][:, :], ACT.Copy).then_inc(S("inv_xa"), 1)
            act.wait_ge(*at("w_mm", 1))
            act.activation(x_mat[:, 0:512], ps[1][:, :], ACT.Copy).then_inc(S("w_t"), 1)
            root("short", ps[6][0:8, 0:T], small[0:8, 6, :], 64)
            act.wait_ge(*at("s_mm", 1))
            act.activation(state, ps[2][:, :], ACT.Copy).then_inc(S("state"), 1)
            act.wait_ge(*at("o_mm", 1))
            act.activation(o_t[:, :, 0:CH], tiles(ps[3][:, :], 4), ACT.Copy).then_inc(S("o_t"), 1)
            cast(s0 + 13 + 3)
            act.wait_ge(*at("o_mm", 2))
            act.activation(o_t[:, :, CH:2 * CH], tiles(ps[2][:, :], 4), ACT.Copy).then_inc(S("o_t"), 1)
            act.wait_ge(*at("o_t", 2))
            act.activation(sq[:, 0:4, :], o_t[:, :, :], ACT.Square).then_inc(S("o_sq"), 1)
            cast(s0 + 14 + 3)
            root("o", ps[3][0:8, 0:T], small[0:8, 6, :], DH)
            for n in range(2):
                act.wait_ge(*at("mix_evac", 14 + n))
                act.activation(gz[:, 2 * n:2 * n + 2, :], gz[:, 2 * n:2 * n + 2, :], ACT.Silu).then_inc(S("gz_silu"), 1)
            for n in range(2):
                act.wait_ge(*at("short_out", n + 1))
                act.wait_ge(taken, FIRST["mix_out"])
                act.activation(xh[:, 2 * n:2 * n + 2, :], cb[:, 2 * n:2 * n + 2, :], ACT.Copy).then_inc(S("mo_xh"), 1)
            for n in range(2):
                act.wait_ge(*at("gdn_out", n + 1))
                act.activation(xh[:, 4 + 2 * n:6 + 2 * n, :], o_t[:, 2 * n:2 * n + 2, :], ACT.Copy).then_inc(S("mo_xh"), 1)
            for n in range(4):
                cast(FIRST["mix_out"] + n + 3)

            norm_in("n3", "mix_resid", "ffn2_norm")
            root("n3", ps[6][:, 0:T], std[:, :], D)
            ffn("ffn2")

            for t in range(KT):
                act.wait_ge(*at("ffn2_resid", t // 2 + 1))
                act.activation(qn[:, t, :], resid[:, t, :], ACT.Square, scale=col("final_norm", t)).then_inc(S("fg_sq"), 1)
            root("f", ps[6][:, 0:T], std[:, :], D)
            act.wait_ge(*at("m2", 1))
            act.activation(kr, kr_raw, ACT.Sqrt, scale=1.0 / D, bias=eps).then_inc(S("g_std"), 1)
            for t in range(KT):
                act.wait_ge(*at("h_f", t + 1))
                act.activation(xh[:, t, :], kn[:, t, :], ACT.Identity, bias=ada[:, t:t + 1]).then_inc(S("h_xh"), 1)
            for n in range(4):
                s = FIRST["glu"] + 2 * n
                cast(s + 3)
                act.wait_ge(taken, s + 2)
                if n:
                    act.wait_ge(*at("glu", n))
                act.activation(hid[:, 0, :], ps[5][:, :], ACT.Sigmoid).then_inc(S("glu_sig"), 1)
                cast(s + 4)
            act.wait_ge(*at("angles", 1))
            act.activation(sines, sines, ACT.Sin).then_inc(S("rope_tables"), 1)
            act.activation(cosines, cosines, ACT.Sin).then_inc(S("rope_tables"), 1)
            s = FIRST["lat"]
            for n in range(3):
                cast(s + n + 3)
                act.wait_ge(taken, s + n + 1)
                bank = ps[4 + n % 2]
                if n < 2:
                    act.activation(lat[:, 2 * n:2 * n + 2, :], pair(bank[:, :]), ACT.Copy).then_inc(S("lat"), 1)
                else:
                    act.activation(lat[:, 4, :], bank[:, 0:T], ACT.Copy).then_inc(S("lat"), 1)
                    act.activation(kr_raw, bank[:, T:2 * T], ACT.Copy).then_inc(S("lat"), 1)
            act.wait_ge(*at("lat", 4))
            act.activation(lat_sq, lat[:, :, :], ACT.Square).then_inc(S("lat_sq"), 1)
            act.wait_ge(*at("lat_stat", 1))
            act.activation(hid[:, 0, 0:T], ps[6][:, 0:T], ACT.Sqrt, scale=1.0 / Q_LAT, bias=eps).then_inc(S("lat_std"), 1)
            act.activation(hid[:, 0, T:2 * T], ps[6][:, T:2 * T], ACT.Sqrt, scale=1.0 / KV_LAT, bias=eps).then_inc(S("lat_std"), 1)
            for t in range(5):
                act.wait_ge(*at("lat_n", 1))
                gain = col("q_norm_g_2", t) if t < 3 else col("kv_norm_g_2", t - 3)
                act.activation(yh[:, t, :], lat[:, t, :], ACT.Copy, scale=gain).then_inc(S("lat_yh"), 1)
            for n in range(3):
                s = FIRST["uq"] + n
                cast(s + 3)
                act.wait_ge(taken, s + 1)
                dst = qn[:, 4 * n:4 * n + 4, :] if n < 2 else qr_raw[:, :, :]
                for b in range(2):
                    act.activation(dst[:, 2 * b:2 * b + 2, :], pair(ps[4 + b][:, :]), ACT.Copy).then_inc(S("q"), 1)
            s = FIRST["ukv"]
            cast(s + 3)
            act.wait_ge(taken, s + 1)
            for b in range(4):
                act.activation(kn[:, 2 * b:2 * b + 2, :], pair(ps[b][:, :]), ACT.Copy).then_inc(S("k"), 1)
            cast(s + 4)
            act.wait_ge(taken, s + 2)
            act.wait_ge(*at("lat_yl", 5))
            for b in range(4):
                act.activation(v[:, b // 2, (b % 2) * 512:(b % 2 + 1) * 512], ps[b][:, :], ACT.Copy).then_inc(S("v"), 1)

            def attn_exp(h):
                act.wait_ge(*at("att_max", h + 1))
                if h >= 2:
                    act.wait_ge(*at("att_norm", h - 1))
                for qt in range(2):
                    w = (qt + 1) * P
                    o = qt * P
                    act.activation(prob[h % 2][:, o:o + w], score[h % 2][:, o:o + w], ACT.Exp,
                                   scale=ATT_SCALE, bias=att_col[:, 8 * (h % 2) + 2 + qt:8 * (h % 2) + 3 + qt],
                                   accum_out=att_col[:, 8 * (h % 2) + 4 + qt:8 * (h % 2) + 5 + qt]).then_inc(S("att_exp"), 1)

            def attn_out(h):
                act.wait_ge(*at("att_turned", h + 1))
                act.activation(prob_t[h % 2], ps[2 + h % 2][:, 0:3 * P], ACT.Copy).then_inc(S("att_pt"), 1)
                act.wait_ge(*at("att_o", h + 1))
                if h == 0:
                    act.wait_ge(taken, FIRST["ukv"] + 2)
                act.activation(yh[:, h, :], ps[4 + h % 2][:, 0:T], ACT.Copy).then_inc(S("o_yh"), 1)

            for h in range(NH + 1):
                if h < NH:
                    attn_exp(h)
                if h >= 1:
                    attn_out(h - 1)

            def gate(phase, n):
                s = FIRST[phase] + n
                cast(s + 3)
                act.wait_ge(taken, s + 1)
                if phase == "gate_a":
                    act.wait_ge(*at("mixed_b", n + 1))
                act.activation(qn[:, 2 * n:2 * n + 2, :], pair(ps[4 + n % 2][:, :]), ACT.Sigmoid).then_inc(S(phase), 1)

            for n in range(4):
                gate("gate_b", n)
            for n in range(4):
                cast(FIRST["attn_out"] + n + 3)
            for n in range(4):
                gate("gate_a", n)
            act.wait_ge(*at("ln_cen", 1))
            act.activation(v_sq, conv[:, :, :], ACT.Square).then_inc(S("ln_sq"), 1)
            root("ln", ps[6][:, 0:T], std[:, :], D)
            act.wait_ge(*at("ln_n", 1))
            for t in range(KT):
                act.activation(conv[:, t, :], conv[:, t, :], ACT.Silu, scale=col("conv_norm_g_2", t),
                               bias=col("conv_norm_b_2", t)).then_inc(S("ln_silu"), 1)
                act.wait_ge(*at("ln_silu", t + 1))
                act.activation(yh[:, t, :], conv[:, t, :], ACT.Copy).then_inc(S("c_yh"), 1)
            for n in range(4):
                cast(FIRST["conv_out"] + n + 3)
            for t in range(KT):
                act.wait_ge(*at("mixed", t // 2 + 1))
                act.activation(xh[:, t, :], kn[:, t, :], ACT.Copy).then_inc(S("w_xh"), 1)
            for n in range(4):
                s = FIRST["w_out"] + n
                cast(s + 3)
                act.wait_ge(taken, s + 1)
                act.activation(conv[:, 2 * n:2 * n + 2, :], pair(ps[4 + n % 2][:, :]), ACT.Copy).then_inc(S("y"), 1)
                act.wait_ge(*at("y", n + 1))
                act.activation(v_sq[:, 2 * n:2 * n + 2, :], conv[:, 2 * n:2 * n + 2, :], ACT.Square).then_inc(S("y_sq"), 1)
            root("y", ps[6][:, 0:T], std[:, :], D)
            act.wait_ge(*at("x3", 4))
            act.activation(v_sq, resid[:, :, :], ACT.Square).then_inc(S("x3_sq"), 1)
            root("x3", ps[6][:, T:2 * T], std[:, :], D)
            for t in range(KT):
                act.wait_ge(*at("h2_f", t + 1))
                act.activation(xh[:, t, :], qn[:, t, :], ACT.Identity, bias=ada[:, 24 + t:25 + t]).then_inc(S("h2_xh"), 1)

            s0 = FIRST["mlp_in"]

            def square(count):
                act.wait_ge(*at("mlp_relu", count))
                act.activation(fh[:, :, :], pair(hid[:, 0, :]), ACT.Square).then_inc(S("mlp_fh"), 1)

            cast(s0 + 3)
            square(1)
            with act.Fori(0, (MLP_STEPS - 1) // SLOTS - 1) as i:
                for r in range(SLOTS):
                    s = s0 + 1 + 2 * r
                    cast_in_loop(s + 3, i, 6, 2)
                    act.wait_ge(taken, i * 6 + (s + 2))
                    square(i * 3 + (r + 2))
                    cast_in_loop(s + 4, i, 6, 2)
            for k in range(MLP_STEPS - SLOTS, MLP_STEPS):
                s = s0 + 2 * k - 1
                if s + 3 < N_SLABS:
                    cast(s + 3)
                act.wait_ge(taken, s + 2)
                square(k + 1)
                if s + 4 < N_SLABS:
                    cast(s + 4)
            act.wait_ge(taken, N_SLABS)
            for n in range(4):
                act.activation(v_sq[:, 2 * n:2 * n + 2, :], pair(ps[n][:, :]), ACT.Square).then_inc(S("z_sq"), 1)
            root("z", ps[6][:, 0:T], std[:, :], D)
            for tk in range(2):
                for n in range(0, 2):
                    act.wait_ge(*at("turned", 2 * tk + n + 1))
                    act.activation(upad_out[:, tk, n * 512:(n + 1) * 512], ps[4 + 2 * tk + n][:, :], ACT.Copy)\
                        .then_inc(S("out_ready"), 2)

        @block.vector
        def _(dve):
            st = Steps(dve, s_vstep)

            def sub(s):
                n = slab_floats(s)
                dve.wait_ge(high_done, s + 1)
                dve.tensor_tensor(wl[:, s % SLOTS, 0:n], raw[:, s % SLOTS, 0:n], wh[:, s % SLOTS, 0:n].bitcast(F32),
                                  ALU.subtract).then_inc(low_done, 1)

            def sub_in_loop(s, i, per):
                dve.wait_ge(high_done, i * per + (s + 1))
                dve.tensor_tensor(wl[:, s % SLOTS, :], raw[:, s % SLOTS, :], wh[:, s % SLOTS, :].bitcast(F32),
                                  ALU.subtract).then_inc(low_done, 1)

            def norm_in(n, gain):
                for t in range(KT):
                    dve.wait_ge(*at(n + "_xh", t + 1))
                    dve.scalar_tensor_tensor(xl[:, t, :], resid[:, t, :], col(gain, t), xh[:, t, :].bitcast(F32),
                                             ALU.mult, ALU.subtract).then_inc(S(n + "_xl"), 1)

            def inverse(n, dst, src):
                dve.wait_ge(*at(n + "_std", 1))
                dve.reciprocal(dst, src).then_inc(S(n + "_rstd"), 1)
                dve.wait_ge(*at(n + "_rstd", 1))

            def scaled(dst, bank, r=rstd):
                return dve.tensor_tensor(dst, pair(bank[:, :]), spread(r[:, :], 2), ALU.mult)

            def ffn(name, n):
                s0 = FIRST[name + "_gate"]

                def gate(s, count):
                    dve.wait_ge(taken, s + 1)
                    scaled(pair(hid[:, 0, :]), ps[4]).then_inc(S(name + "_gate"), 1)

                def up(s, count):
                    dve.wait_ge(taken, s + 1)
                    scaled(pair(hid[:, 2, :]), ps[5]).then_inc(S(name + "_up"), 1)

                def hidden(count):
                    dve.wait_ge(*at(name + "_silu", count))
                    dve.wait_ge(*at(name + "_up", count))
                    dve.tensor_tensor(hid[:, 3, :], hid[:, 1, :], hid[:, 2, :], ALU.mult).then_inc(S(name + "_h"), 1)

                def rest(count):
                    dve.wait_ge(*at(name + "_fh", count))
                    dve.tensor_tensor(fl[:, :, :], pair(hid[:, 3, :]), fh[:, :, :].bitcast(F32), ALU.subtract)\
                        .then_inc(S(name + "_fl"), 1)

                inverse(n, rstd[:, :], std[:, :])
                gate(s0, 1)
                sub(s0 + 3)
                up(s0 + 1, 1)
                sub(s0 + 4)
                hidden(1)
                rest(1)
                with dve.Fori(0, FF_STEPS - 1) as i:
                    s = s0 + 2
                    gate(i * 3 + s, i + 2)
                    sub_in_loop(s + 3, i, 3)
                    up(i * 3 + (s + 1), i + 2)
                    sub_in_loop(s + 4, i, 3)
                    hidden(i + 2)
                    rest(i + 2)
                    sub_in_loop(s + 5, i, 3)
                s = s0 + 3 * FF_STEPS - 1
                dve.wait_ge(taken, s + 1)
                for b in range(4):
                    dve.scalar_tensor_tensor(resid[:, 2 * b:2 * b + 2, :], pair(ps[b][:, :]), 0.5,
                                             resid[:, 2 * b:2 * b + 2, :], ALU.mult, ALU.add).then_inc(S(name + "_resid"), 1)
                if name == "ffn2":
                    sub(s + 3)

            dve.wait_ge(*at("x_turned", 4))
            for b in range(4):
                dve.tensor_copy(resid[:, 2 * b:2 * b + 2, :], pair(ps[4 + b][:, :])).then_inc(S("x_in"), 1)
            dve.wait_ge(*at("vec_turned", 1))
            dve.tensor_copy(vec[:, 0, 0:STAGE_ROWS[0]], ps[0][:, 0:STAGE_ROWS[0]]).then_inc(S("vec"), 1)
            dve.wait_ge(*at("vec", 1))
            dve.wait_ge(*at("x_in", 4))
            norm_in("n1", "ffn1_norm")
            for s in range(SLOTS):
                sub(s)
            dve.wait_ge(*at("vec_turned", 2))
            for g in range(1, 4):
                ins = dve.tensor_copy(vec[:, g, 0:STAGE_ROWS[g]], ps[1][:, g * P:g * P + STAGE_ROWS[g]])
            ins.then_inc(S("vec"), 1)
            ffn("ffn1", "n1")

            dve.wait_ge(*at("ffn1_resid", 4))
            norm_in("n2", "mix_norm")
            sub(FIRST["mix"] + 2)
            inverse("n2", rstd[:, :], std[:, :])
            s0 = FIRST["mix"]
            dve.wait_ge(*at("pads", 2))
            dve.wait_ge(*at("con_rest", 16))

            def evac(n, dst):
                dve.wait_ge(taken, s0 + n + 1)
                scaled(dst, ps[4 + n % 2]).then_inc(S("mix_evac"), 1)
                dve.wait_ge(*at("mix_evac", n + 1))

            for n in range(6):
                evac(n, qkvp[:, 2 * n:2 * n + 2, 3:3 + T])
                for k in range(4):
                    for t in (2 * n, 2 * n + 1):
                        if k == 0:
                            ins = dve.tensor_scalar(qkv[:, t, :], qkvp[:, t, 0:T], col("gdn_conv_w", t), None, ALU.mult)
                        else:
                            ins = dve.scalar_tensor_tensor(qkv[:, t, :], qkvp[:, t, k:k + T], col("gdn_conv_w", 12 * k + t),
                                                           qkv[:, t, :], ALU.mult, ALU.add)
                        if k == 3:
                            ins.then_inc(S("conv4_done"), 1)
                    if k < 3:
                        st(ins)
                        st.sync()
                sub(s0 + n + 3)
            dve.wait_ge(taken, s0 + MIX_AB + 1)
            dve.tensor_tensor(small[0:4, 5, :], ps[4][0:4, 0:T], rstd[0:4, :], ALU.mult)
            st(dve.tensor_tensor(small[0:4, 0, :], ps[4][32:36, 0:T], rstd[32:36, :], ALU.mult))
            st.sync()
            dve.wait_ge(*at("small_loaded", 32))
            dve.tensor_scalar(small[0:4, 0, :], small[0:4, 0, :], a_log[:, 1:2], None, ALU.add).then_inc(S("mix_evac"), 1)
            dve.wait_ge(*at("mix_evac", MIX_AB + 1))
            dve.scalar_tensor_tensor(small[0:4, 1, :], small[0:4, 0, :], -1.0, small[0:4, 0, :], ALU.mult, ALU.min)\
                .then_inc(S("ab_abs"), 1)
            inverse("qk", small[0:8, 7, :], small[0:8, 6, :])
            dve.tensor_scalar(small[0:8, 7, :], small[0:8, 7, :], const("qk_scale", 1, 8), None, ALU.mult).then_inc(S("qk_row"), 1)
            sub(s0 + MIX_AB + 3)
            dve.wait_ge(*at("ab_exp", 1))
            dve.tensor_scalar(small[0:4, 3, :], small[0:4, 2, :], 1.0, None, ALU.add).then_inc(S("ab_one"), 1)
            evac(7, cc[:, 0:2, :])
            dve.wait_ge(*at("ab_ln", 1))
            st(dve.tensor_scalar(small[0:4, 3, :], small[0:4, 3, :], 1.0, None, ALU.subtract))
            st.sync()
            st(dve.tensor_scalar(small[0:4, 1, :], small[0:4, 3, :], 0.0, None, ALU.is_equal))
            st.sync()
            dve.tensor_tensor(small[0:4, 4, :], small[0:4, 4, :], small[0:4, 1, :], ALU.add)
            st(dve.tensor_tensor(small[0:4, 3, :], small[0:4, 3, :], small[0:4, 1, :], ALU.add))
            st.sync()
            st(dve.reciprocal(small[0:4, 1, :], small[0:4, 3, :]))
            st.sync()
            st(dve.tensor_tensor(small[0:4, 4, :], small[0:4, 4, :], small[0:4, 1, :], ALU.mult))
            st.sync()
            st(dve.tensor_tensor(small[0:4, 4, :], small[0:4, 4, :], small[0:4, 2, :], ALU.mult))
            st.sync()
            st(dve.scalar_tensor_tensor(small[0:4, 4, :], small[0:4, 0, :], 0.0, small[0:4, 4, :], ALU.max, ALU.add))
            st.sync()
            st(dve.tensor_scalar(small[0:4, 4, :], small[0:4, 4, :], a_log[:, 0:1], -1.0, ALU.mult, ALU.mult))
            st.sync()
            dve.tensor_tensor_scan(g_cum[0:4, :], const("restart", T, 4), small[0:4, 4, :], 0.0, ALU.mult, ALU.add)\
                .then_inc(S("g_cum"), 1)
            sub(s0 + 7 + 3)
            dve.wait_ge(*at("qk_spread", 4))
            for b in range(4):
                dve.tensor_tensor(qkv[:, 2 * b:2 * b + 2, :], qkv[:, 2 * b:2 * b + 2, :], pair(ps[b][:, :]), ALU.mult)\
                    .then_inc(S("qk_n"), 1)
            evac(8, cc[:, 2:4, :])
            sub(s0 + 8 + 3)
            for b in range(2):
                dve.wait_ge(*at("b_spread", b + 1))
                dve.tensor_tensor(kb[:, 2 * b:2 * b + 2, :], k_n[:, 2 * b:2 * b + 2, :], pair(ps[2 + b][:, :]), ALU.mult)\
                    .then_inc(S("kb"), 1)
            evac(9, mpad[:, 0:2, 2:2 + T])
            dve.wait_ge(*at("col_turned", 4))
            dve.wait_ge(*at("g_row", 2))
            st(dve.tensor_copy(cols[:, 0:16], ps[6][:, 0:16]))
            st.sync()
            for u in range(UNITS):
                c, h = u // HEADS, u % HEADS
                ins = dve.tensor_scalar(dt_mat[:, u * P:(u + 1) * P], g_row[:, h, c * CH:(c + 1) * CH], cols[:, u:u + 1], 0.0,
                                        ALU.subtract, ALU.min)
            st(ins)
            dve.tensor_tensor(cols[:, 24:28], g_row[:, :, CH - 1], cols[:, 0:4], ALU.subtract).then_inc(S("dt_diff"), 1)
            sub(s0 + 9 + 3)
            evac(10, mpad[:, 2:4, 2:2 + T])
            dve.wait_ge(*at("g_exp", 3))
            dve.wait_ge(*at("dt_exp", 1))
            dve.scalar_tensor_tensor(cols[:, 28:32], cols[:, 12:16], -1.0, cols[:, 16:20], ALU.mult, ALU.mult)\
                .then_inc(S("cols_ready"), 1)
            for b in range(2):
                dve.wait_ge(*at("lt_mm", b + 1))
                dve.tensor_tensor(lt_mat[:, b * 512:(b + 1) * 512], ps[b][:, :], dt_mat[:, b * 512:(b + 1) * 512], ALU.mult)\
                    .then_inc(S("lt"), 1)
            dve.wait_ge(*at("lt", 2))
            st(dve.tensor_tensor(tiles(dt_mat, UNITS), tiles(dt_mat, UNITS), spread(const("upper", P), UNITS), ALU.mult))
            sub(s0 + 10 + 3)
            st.sync()
            for b in range(2):
                dve.wait_ge(*at("at_mm", b + 1))
                ins = dve.tensor_tensor(at_mat[:, b * 512:(b + 1) * 512], ps[b][:, :], dt_mat[:, b * 512:(b + 1) * 512], ALU.mult)
            ins.then_inc(S("at_done"), 1)
            dve.wait_ge(*at("at_done", 1))
            st(dve.tensor_tensor(q_n[:, :, CH:2 * CH], q_n[:, :, CH:2 * CH], exp_g, ALU.mult))
            st.sync()
            evac(11, cb[:, 0:2, :])
            sub(s0 + 11 + 3)
            for b in range(2):
                for m in (t_mat, tt_mat):
                    dve.tensor_copy(tiles(m[:, b * 512:(b + 1) * 512], 4), spread(ident, 4)).then_inc(S("inv_t"), 1)

            def between_halves(mask):
                dve.tensor_tensor(tiles(b_mat, UNITS), tiles(lt_mat, UNITS), spread(mask, UNITS), ALU.mult)\
                    .then_inc(S("inv_b"), 1)

            def level(i, last=False):
                dve.wait_ge(*at("inv_x", i * 2 + 1))
                dve.tensor_copy(x_mat[:, 0:512], ps[0][:, :]).then_inc(S("inv_xv"), 1)
                if not last:
                    dve.wait_ge(*at("inv_x", i * 2 + 2))
                    between_halves(con[:, bass.ds(i * P + (C["levels"] + P), P)])
                dve.wait_ge(*at("inv_t", i * 4 + 4))
                for b in range(2):
                    for n, m in enumerate((t_mat, tt_mat)):
                        dve.wait_ge(*at("inv_y", i * 4 + (2 * b + n + 1)))
                        dve.tensor_tensor(m[:, b * 512:(b + 1) * 512], m[:, b * 512:(b + 1) * 512], ps[2 + b + 2 * n][:, :],
                                          ALU.subtract).then_inc(S("inv_t"), 1)

            between_halves(con[:, C["levels"]:C["levels"] + P])
            evac(12, cb[:, 2:4, :])
            sub(s0 + 12 + 3)
            with dve.Fori(0, LEVELS - 1) as i:
                level(i)
            level(LEVELS - 1, last=True)
            dve.wait_ge(*at("v_mm", 1))
            dve.tensor_copy(v_new[:, 0:512], ps[0][:, :]).then_inc(S("v_new"), 1)
            inverse("short", small[0:8, 7, :], small[0:8, 6, :])
            evac(13, gz[:, 0:2, :])
            dve.wait_ge(*at("v_mm", 2))
            dve.tensor_copy(v_new[:, 512:1024], ps[1][:, :]).then_inc(S("v_new"), 1)
            sub(s0 + 13 + 3)
            for b in range(2):
                dve.wait_ge(*at("short_spread", b + 1))
                bank = ps[(6, 0)[b]]
                for t in (2 * b, 2 * b + 1):
                    ins = dve.scalar_tensor_tensor(cb[:, t, :], cc[:, t, :], col("conv_out_norm", t),
                                                   bank[:, (t % 2) * T:(t % 2 + 1) * T], ALU.mult, ALU.mult)
                ins.then_inc(S("short_out"), 1)
            evac(14, gz[:, 2:4, :])
            sub(s0 + 14 + 3)
            for b in range(2):
                dve.wait_ge(*at("mo_xh", b + 1))
                dve.tensor_tensor(xl[:, 2 * b:2 * b + 2, :], cb[:, 2 * b:2 * b + 2, :], xh[:, 2 * b:2 * b + 2, :].bitcast(F32),
                                  ALU.subtract).then_inc(S("mo_xl"), 1)
            inverse("o", small[0:8, 7, :], small[0:8, 6, :])
            dve.wait_ge(*at("gz_silu", 2))
            for b in range(2):
                dve.wait_ge(*at("o_spread", b + 1))
                st(dve.scalar_tensor_tensor(o_t[:, 2 * b:2 * b + 2, :], o_t[:, 2 * b:2 * b + 2, :], col("gdn_out_norm", 0),
                                            pair(ps[b][:, :]), ALU.mult, ALU.mult))
                st.sync()
                dve.tensor_tensor(o_t[:, 2 * b:2 * b + 2, :], o_t[:, 2 * b:2 * b + 2, :], gz[:, 2 * b:2 * b + 2, :], ALU.mult)\
                    .then_inc(S("gdn_out"), 1)
            for b in range(2):
                dve.wait_ge(*at("mo_xh", b + 3))
                dve.tensor_tensor(xl[:, 4 + 2 * b:6 + 2 * b, :], o_t[:, 2 * b:2 * b + 2, :],
                                  xh[:, 4 + 2 * b:6 + 2 * b, :].bitcast(F32), ALU.subtract).then_inc(S("mo_xl"), 1)
            for n in range(4):
                s = FIRST["mix_out"] + n
                dve.wait_ge(taken, s + 1)
                dve.tensor_tensor(resid[:, 2 * n:2 * n + 2, :], pair(ps[4 + n % 2][:, :]), resid[:, 2 * n:2 * n + 2, :],
                                  ALU.add).then_inc(S("mix_resid"), 1)
                sub(s + 3)
            dve.wait_ge(*at("mix_resid", 4))
            norm_in("n3", "ffn2_norm")
            ffn("ffn2", "n3")

            dve.wait_ge(*at("ffn2_resid", 4))
            for t in range(KT):
                dve.wait_ge(*at("ffn2_resid", t // 2 + 1))
                dve.wait_ge(*at("fg_sq", t + 1))
                if t % 2 == 0:
                    dve.wait_ge(*at("f_sq", t // 2 + 1))
                dve.tensor_scalar(resid[:, t, :], resid[:, t, :], col("final_norm", t), None, ALU.mult).then_inc(S("x2_scaled"), 1)
            dve.wait_ge(*at("ada_taken", ADA_STEPS))
            g, r = VECS["b_ada_2"]
            st(dve.tensor_tensor(ada[:, :], ps[7][:, 0:ADA_TILES], vec[:, g, r:r + ADA_TILES], ALU.add))
            st.sync()

            def vecs(name):
                g, r = VECS[name]
                return vec[:, g, r:r + KT]

            dve.scalar_tensor_tensor(mods[:, 0, :], ada[:, 8:16], 1.0, vecs("g_pre_mix_2"), ALU.add, ALU.mult)
            dve.tensor_tensor(mods[:, 1, :], ada[:, 16:24], vecs("g_post_mix_2"), ALU.mult)
            dve.scalar_tensor_tensor(mods[:, 2, :], ada[:, 32:40], 1.0, vecs("g_pre_mlp_2"), ALU.add, ALU.mult)
            st(dve.tensor_tensor(mods[:, 3, :], ada[:, 40:48], vecs("g_post_mlp_2"), ALU.mult))
            st.sync()
            inverse("f", rstd[:, :], std[:, :])
            dve.wait_ge(*at("f_stat", 2))
            st(dve.tensor_tensor(kr_raw, ps[5][:, 0:T], rstd[:, :], ALU.mult))
            st.sync()
            dve.tensor_tensor(kr_raw, kr_raw, rstd[:, :], ALU.mult).then_inc(S("m2"), 1)
            inverse("g", hid[:, 0, 0:T], kr)
            st(dve.tensor_tensor(hid[:, 0, 0:T], hid[:, 0, 0:T], rstd[:, :], ALU.mult))
            st.sync()
            dve.wait_ge(*at("x2_scaled", KT))
            for t in range(KT):
                dve.scalar_tensor_tensor(kn[:, t, :], resid[:, t, :], mods[:, 0, t:t + 1], hid[:, 0, 0:T], ALU.mult, ALU.mult)\
                    .then_inc(S("h_f"), 1)
            for t in range(KT):
                dve.wait_ge(*at("h_xh", t + 1))
                dve.scalar_tensor_tensor(xl[:, t, :], kn[:, t, :], ada[:, t:t + 1], xh[:, t, :].bitcast(F32), ALU.add,
                                         ALU.subtract).then_inc(S("h_xl"), 1)
            st(dve.tensor_tensor(resid[:, :, :], resid[:, :, :], spread(rstd[:, :], KT), ALU.mult))
            dve.wait_ge(*at("upads", 1))
            for n in range(4):
                s = FIRST["glu"] + 2 * n
                sub(s + 3)
                dve.wait_ge(*at("glu_sig", n + 1))
                dve.tensor_tensor(upad[:, 2 * n:2 * n + 2, PAD:PAD + T], pair(ps[4][:, :]), pair(hid[:, 0, :]), ALU.mult)\
                    .then_inc(S("glu"), 1)
                sub(s + 4)
            dve.wait_ge(*at("glu", 4))
            dve.wait_ge(*at("pos_loaded", 16))
            c1, c2, c3 = two_pi()
            magic = 12582912.0
            lim = 3.1415925
            ang, turns = hid[:, 1, 0:T], hid[:, 1, T:2 * T]
            st(dve.tensor_copy(ang, cosines.bitcast(I32)))
            st.sync()
            st(dve.tensor_scalar(ang, ang, const("inv_freq", 1), None, ALU.mult))
            st.sync()
            for dst, quarter, shift in ((sines, 0.0, 0.0), (cosines, 0.25, float(np.float32(np.pi / 2)))):
                st(dve.tensor_scalar(turns, ang, float(np.float32(1 / (2 * np.pi))), quarter, ALU.mult, ALU.add))
                st.sync()
                st(dve.tensor_scalar(turns, turns, magic, None, ALU.add))
                st.sync()
                st(dve.tensor_scalar(turns, turns, magic, None, ALU.subtract))
                st.sync()
                src = ang
                for c in (c1, c2, c3):
                    st(dve.scalar_tensor_tensor(dst, turns, -c, src, ALU.mult, ALU.add))
                    st.sync()
                    src = dst
                st(dve.tensor_scalar(dst, dst, shift, lim, ALU.add, ALU.min))
                st.sync()
                ins = dve.tensor_scalar(dst, dst, -lim, None, ALU.max)
                if quarter:
                    ins.then_inc(S("angles"), 1)
                else:
                    st(ins)

            taps_left = list(range(TAPS))

            def convolve(n):
                for _ in range(n):
                    if not taps_left:
                        return
                    k = taps_left.pop(0)
                    for t in range(DVE_TILES):
                        if k == 0:
                            ins = dve.tensor_scalar(conv[:, t, :], upad[:, t, 0:T], tap(0, t), col("conv_b_2", t),
                                                    ALU.mult, ALU.add)
                        else:
                            ins = dve.scalar_tensor_tensor(conv[:, t, :], upad[:, t, k:k + T], tap(k, t), conv[:, t, :],
                                                           ALU.mult, ALU.add)
                    st(ins)
                    st.sync()

            for n in range(3):
                sub(FIRST["lat"] + n + 3)
                convolve(1)
            dve.wait_ge(*at("lat_std", 2))
            st(dve.reciprocal(hid[:, 1, :], hid[:, 0, :]))
            st.sync()
            st(dve.tensor_tensor(lat[:, 0:3, :], lat[:, 0:3, :], spread(hid[:, 1, 0:T], 3), ALU.mult))
            dve.tensor_tensor(lat[:, 3:5, :], lat[:, 3:5, :], spread(hid[:, 1, T:2 * T], 2), ALU.mult).then_inc(S("lat_n"), 1)
            dve.wait_ge(*at("lat_n", 1))
            for t in range(5):
                gain = col("q_norm_g_2", t) if t < 3 else col("kv_norm_g_2", t - 3)
                dve.wait_ge(*at("lat_yh", t + 1))
                dve.scalar_tensor_tensor(yl[:, t, :], lat[:, t, :], gain, yh[:, t, :].bitcast(F32), ALU.mult, ALU.subtract)\
                    .then_inc(S("lat_yl"), 1)
            dve.wait_ge(*at("rope_tables", 2))
            dve.wait_ge(*at("kr_swap", 1))
            dve.wait_ge(*at("lat", 4))
            st(dve.tensor_tensor(kr, kr_raw, cosines, ALU.mult))
            st(dve.tensor_tensor(hid[:, 2, 0:T], ps[7][:, 0:T], sines, ALU.mult))
            st.sync()
            dve.tensor_tensor(kr, kr, hid[:, 2, 0:T], ALU.add).then_inc(S("kr"), 1)
            for n in range(3):
                sub(FIRST["uq"] + n + 3)
                convolve(1)
            dve.wait_ge(*at("q", 6))
            st(dve.tensor_tensor(qr[:, :, :], qr_raw[:, :, :], spread(cosines, 4), ALU.mult))
            for b in range(2):
                dve.wait_ge(*at("q_swap", b + 1))
                st(dve.tensor_tensor(pair(hid[:, 2 + b, :]), pair(ps[6 + b][:, :]), spread(sines, 2), ALU.mult))
            st.sync()
            dve.tensor_tensor(qr[:, :, :], qr[:, :, :], tiles(hid[:, 2:4, :].rearrange("p a t -> p (a t)"), 4), ALU.add)\
                .then_inc(S("qr"), 1)
            sub(FIRST["ukv"] + 3)
            sub(FIRST["ukv"] + 4)

            def attn_max(h):
                c = 8 * (h % 2)
                dve.wait_ge(*at("att_s", h + 1))
                st(dve.tensor_tensor(score[h % 2], ps[h % 2][:, 0:3 * P], const("causal", 3 * P), ALU.add))
                st.sync()
                dve.tensor_reduce(att_col[:, c:c + 1], score[h % 2][:, 0:P], AX_X, ALU.max)
                st(dve.tensor_reduce(att_col[:, c + 1:c + 2], score[h % 2][:, P:3 * P], AX_X, ALU.max))
                st.sync()
                dve.tensor_scalar(att_col[:, c + 2:c + 4], att_col[:, c:c + 2], -ATT_SCALE, None, ALU.mult)\
                    .then_inc(S("att_max"), 1)

            def attn_norm(h):
                c = 8 * (h % 2)
                dve.wait_ge(*at("att_exp", 2 * (h + 1)))
                st(dve.reciprocal(att_col[:, c + 6:c + 8], att_col[:, c + 4:c + 6]))
                st.sync()
                st(dve.tensor_scalar(prob[h % 2][:, 0:P], prob[h % 2][:, 0:P], att_col[:, c + 6:c + 7], None, ALU.mult))
                dve.tensor_scalar(prob[h % 2][:, P:3 * P], prob[h % 2][:, P:3 * P], att_col[:, c + 7:c + 8], None, ALU.mult)\
                    .then_inc(S("att_norm"), 1)

            def attn_rest(h):
                dve.wait_ge(*at("o_yh", h + 1))
                dve.tensor_tensor(yl[:, h, :], ps[4 + h % 2][:, 0:T], yh[:, h, :].bitcast(F32), ALU.subtract)\
                    .then_inc(S("o_yl"), 1)

            for h in range(NH + 2):
                if h < NH:
                    attn_max(h)
                convolve(1)
                if 1 <= h <= NH:
                    attn_norm(h - 1)
                if h >= 2:
                    attn_rest(h - 2)
            for n in range(4):
                sub(FIRST["gate_b"] + n + 3)
                convolve(2)
            for n in range(4):
                s = FIRST["attn_out"] + n
                dve.wait_ge(taken, s + 1)
                dve.wait_ge(*at("gate_b", n + 1))
                dve.tensor_tensor(kn[:, 2 * n:2 * n + 2, :], pair(ps[4 + n % 2][:, :]), qn[:, 2 * n:2 * n + 2, :], ALU.mult)\
                    .then_inc(S("mixed_b"), 1)
                sub(s + 3)
                convolve(1)
            for n in range(4):
                sub(FIRST["gate_a"] + n + 3)
                if n == 0:
                    convolve(TAPS)
                    dve.wait_ge(*at("long_conv", 1))
                    dve.tensor_copy(att_col[:, 0:1], att_col[:, 0:1]).then_inc(S("conv_done"), 1)
                if n == 2:
                    dve.wait_ge(*at("ln_mean", 1))
                    st(dve.tensor_scalar(hid[:, 0, 0:T], ps[7][:, 0:T], 1.0 / D, None, ALU.mult))
                    st.sync()
                    dve.tensor_tensor(conv[:, :, :], conv[:, :, :], spread(hid[:, 0, 0:T], KT), ALU.subtract)\
                        .then_inc(S("ln_cen"), 1)
            inverse("ln", rstd[:, :], std[:, :])
            dve.wait_ge(*at("ln_cen", 1))
            dve.tensor_tensor(conv[:, :, :], conv[:, :, :], spread(rstd[:, :], KT), ALU.mult).then_inc(S("ln_n"), 1)
            for t in range(KT):
                dve.wait_ge(*at("c_yh", t + 1))
                dve.tensor_tensor(yl[:, t, :], conv[:, t, :], yh[:, t, :].bitcast(F32), ALU.subtract).then_inc(S("c_yl"), 1)
            for n in range(4):
                s = FIRST["conv_out"] + n
                dve.wait_ge(taken, s + 1)
                dve.wait_ge(*at("gate_a", n + 1))
                st(dve.tensor_tensor(pair(hid[:, n, :]), pair(ps[4 + n % 2][:, :]), qn[:, 2 * n:2 * n + 2, :], ALU.mult))
                st.sync()
                dve.wait_ge(*at("mixed_b", 4))
                dve.tensor_tensor(kn[:, 2 * n:2 * n + 2, :], kn[:, 2 * n:2 * n + 2, :], pair(hid[:, n, :]), ALU.add)\
                    .then_inc(S("mixed"), 1)
                sub(s + 3)
            dve.wait_ge(*at("mixed", 4))
            for t in range(KT):
                dve.wait_ge(*at("w_xh", t + 1))
                dve.tensor_tensor(xl[:, t, :], kn[:, t, :], xh[:, t, :].bitcast(F32), ALU.subtract).then_inc(S("w_xl"), 1)
            for n in range(4):
                sub(FIRST["w_out"] + n + 3)

            def add_normed(tag, src, gain):
                for b in range(4):
                    for t in (2 * b, 2 * b + 1):
                        ins = dve.scalar_tensor_tensor(qn[:, t, :], src(t), mods[:, gain, t:t + 1], rstd[:, :], ALU.mult, ALU.mult)
                    st(ins)
                    st.sync()
                    dve.tensor_tensor(resid[:, 2 * b:2 * b + 2, :], resid[:, 2 * b:2 * b + 2, :], qn[:, 2 * b:2 * b + 2, :],
                                      ALU.add).then_inc(S(tag), 1)

            inverse("y", rstd[:, :], std[:, :])
            add_normed("x3", lambda t: conv[:, t, :], 1)
            inverse("x3", rstd[:, :], std[:, :])
            dve.wait_ge(*at("x3", 4))
            for t in range(KT):
                dve.scalar_tensor_tensor(qn[:, t, :], resid[:, t, :], mods[:, 2, t:t + 1], rstd[:, :], ALU.mult, ALU.mult)\
                    .then_inc(S("h2_f"), 1)
            for t in range(KT):
                dve.wait_ge(*at("h2_xh", t + 1))
                dve.scalar_tensor_tensor(xl[:, t, :], qn[:, t, :], ada[:, 24 + t:25 + t], xh[:, t, :].bitcast(F32), ALU.add,
                                         ALU.subtract).then_inc(S("h2_xl"), 1)

            s0 = FIRST["mlp_in"]

            def relu(s):
                dve.wait_ge(taken, s + 1)
                dve.tensor_scalar(hid[:, 0, :], ps[4][:, :], 0.0, None, ALU.max).then_inc(S("mlp_relu"), 1)

            def rest(count):
                dve.wait_ge(*at("mlp_relu", count))
                dve.tensor_tensor(hid[:, 1, :], hid[:, 0, :], hid[:, 0, :], ALU.mult).then_inc(S("mlp_sq"), 1)
                dve.wait_ge(*at("mlp_sq", count))
                dve.wait_ge(*at("mlp_fh", count))
                dve.tensor_tensor(fl[:, :, :], pair(hid[:, 1, :]), fh[:, :, :].bitcast(F32), ALU.subtract)\
                    .then_inc(S("mlp_fl"), 1)

            relu(s0)
            sub(s0 + 3)
            rest(1)
            with dve.Fori(0, (MLP_STEPS - 1) // SLOTS - 1) as i:
                for r in range(SLOTS):
                    s = s0 + 1 + 2 * r
                    relu(i * 6 + s)
                    sub_in_loop(s + 3, i, 6)
                    rest(i * 3 + (r + 2))
                    sub_in_loop(s + 4, i, 6)
            for k in range(MLP_STEPS - SLOTS, MLP_STEPS):
                s = s0 + 2 * k - 1
                relu(s)
                if s + 3 < N_SLABS:
                    sub(s + 3)
                rest(k + 1)
                if s + 4 < N_SLABS:
                    sub(s + 4)
            inverse("z", rstd[:, :], std[:, :])
            add_normed("x4", lambda t: ps[t // 2][:, (t % 2) * T:(t % 2 + 1) * T], 3)

        @block.tensor
        def _(pe):
            def wide(s, bank, x, y, tile_ready=None, tile_base=0, slab=None, m_tiles=2):
                slab = s if slab is None else slab
                pe.wait_ge(low_done, s + 1)
                n = KT * P * m_tiles
                h, l = (w[:, slab % SLOTS, 0:n].rearrange("p (k m) -> p k m", k=KT) for w in (wh, wl))
                for m in range(m_tiles):
                    for k in range(KT):
                        if tile_ready is not None and m == 0:
                            pe.wait_ge(*at(tile_ready, tile_base(k)))
                        for j, (w, r) in enumerate(((h, x), (h, y), (l, x))):
                            mm = pe.matmul(bank[:, m * T:(m + 1) * T], w[:, k, m * P:(m + 1) * P], r[:, k, :],
                                           start=(m == 0 and k == 0 and j == 0), stop=(k == KT - 1 and j == 2),
                                           skip_group_check=True)
                mm.then_inc(taken, 1)

            def deep(s, slab=None):
                slab = s if slab is None else slab
                pe.wait_ge(low_done, s + 1)
                h, l = (w[:, slab % SLOTS, :].rearrange("p (k m) -> p k m", k=2) for w in (wh, wl))
                for k in range(2):
                    for m in range(KT):
                        for w, r in ((h, fh), (h, fl), (l, fh)):
                            mm = pe.matmul(ps[m // 2][:, (m % 2) * T:(m % 2 + 1) * T], w[:, k, m * P:(m + 1) * P], r[:, k, :],
                                           start=False, stop=False, skip_group_check=True)
                mm.then_inc(taken, 1)

            def clear_sums():
                for b in range(4):
                    pe.matmul(ps[b][:, :], zero[0:1, 0:P], zero[0:1, :], start=True, stop=True, skip_group_check=True)

            def column_sums(n, src, k_tiles, out, ready, signal=True, by_pair=False):
                pe.wait_ge(*at(*ready))
                for k in range(k_tiles):
                    if by_pair and k % 2 == 0 and k:
                        pe.wait_ge(*at(ready[0], ready[1] + k // 2))
                    mm = pe.matmul(out, ones, src(k), start=(k == 0), stop=(k == k_tiles - 1), skip_group_check=True)
                if signal:
                    mm.then_inc(S(n + "_stat"), 1)

            def one(k):
                return k + 1

            def modulate(step):
                pe.wait_ge(*at("ada_free", step + 1))
                for m in range(2):
                    mm = pe.matmul(ps[7][:, bass.ds(step * 2 + m, 1)], ada_sum[:, m * P:(m + 1) * P], ones[:, 0:1], start=True,
                                   stop=True, skip_group_check=True)
                mm.then_inc(S("ada_taken"), 1)

            def ffn(name, n, prev_free):
                s0 = FIRST[name + "_gate"]
                column_sums(n, lambda k: sq[:, k, :], KT, ps[6][:, 0:T], (n + "_sq", 1), by_pair=True)
                wide(s0, ps[4], xh, xl, n + "_xl", one)
                if prev_free:
                    pe.wait_ge(*at(*prev_free))
                wide(s0 + 1, ps[5], xh, xl)
                if name == "ffn1":
                    pe.wait_ge(*at("vec", 2))
                clear_sums()
                with pe.Fori(0, FF_STEPS - 1) as i:
                    s = s0 + 2
                    pe.wait_ge(*at(name + "_gate", i + 1))
                    wide(i * 3 + s, ps[4], xh, xl, slab=s)
                    pe.wait_ge(*at(name + "_up", i + 1))
                    wide(i * 3 + (s + 1), ps[5], xh, xl, slab=s + 1)
                    pe.wait_ge(*at(name + "_fl", i + 1))
                    deep(i * 3 + (s + 2), slab=s + 2)
                    modulate(i + (0 if name == "ffn1" else FF_STEPS - 1 + ADA_MIX))
                pe.wait_ge(*at(name + "_fl", FF_STEPS))
                deep(s0 + 3 * FF_STEPS - 1)

            pe.wait_ge(*at("con", 16))
            pe.wait_ge(*at("zero", 1))
            pe.wait_ge(*at("x_loaded", 16))
            xin = sq.rearrange("p (a b) t -> p a (b t)", a=2)
            for b in range(4):
                for t in (2 * b, 2 * b + 1):
                    for tk in range(2):
                        mm = pe.transpose(ps[4 + b][:, (t % 2) * T + tk * P:(t % 2) * T + (tk + 1) * P],
                                          xin[:, tk, t * P:(t + 1) * P], ident)
                mm.then_inc(S("x_turned"), 1)
            pe.wait_ge(*at("vec0_loaded", 16 * N_VEC_0))
            n = STAGE_ROWS[0]
            pe.transpose(ps[0][:, 0:n], stage[0:n, 0, :], ident[0:n, 0:n]).then_inc(S("vec_turned"), 1)
            pe.wait_ge(*at("vec1_loaded", 16 * (N_VEC - N_VEC_0)))
            for g in range(1, 4):
                n = STAGE_ROWS[g]
                mm = pe.transpose(ps[1][:, g * P:g * P + n], stage[0:n, g, :], ident[0:n, 0:n])
            mm.then_inc(S("vec_turned"), 1)
            pe.wait_ge(*at("x_in", 4))
            ffn("ffn1", "n1", None)

            s0 = FIRST["mix"]

            def mix(n, **kw):
                if n >= 2:
                    pe.wait_ge(*at("mix_evac", n - 1))
                wide(s0 + n, ps[4 + n % 2], xh, xl, m_tiles=1 if n == MIX_AB else 2, **kw)
                if n in ADA_AFTER:
                    modulate(FF_STEPS - 1 + ADA_AFTER.index(n))

            column_sums("n2", lambda k: sq[:, k, :], KT, ps[6][:, 0:T], ("n2_sq", 1), by_pair=True)
            mix(0, tile_ready="n2_xl", tile_base=one)
            for n in range(1, 6):
                mix(n)

            def row_sums(n, name, tile_of, count, bank, ready):
                pe.wait_ge(*at(*ready))
                sel = const(name, 8 * count).rearrange("p (t r) -> p t r", r=8)
                for t in range(count):
                    mm = pe.matmul(bank[0:8, 0:T], sel[:, t, :], sq[:, tile_of + t, :], start=(t == 0), stop=(t == count - 1),
                                   skip_group_check=True)
                mm.then_inc(S(n + "_stat"), 1)

            def spread_rows(n, name, src, count, k_rows, banks):
                sel = const(name, P * count, k_rows).rearrange("p (t m) -> p t m", m=P)
                for t in range(count):
                    mm = pe.matmul(ps[banks[t // 2]][:, (t % 2) * T:(t % 2 + 1) * T], sel[:, t, :], src,
                                   start=(t % 2 == 0), stop=True, skip_group_check=True)
                    if t % 2:
                        mm.then_inc(S(n), 1)

            def unit(m, u):
                return m[:, u * P:(u + 1) * P]

            def chan(m, u):
                c, h = u // HEADS, u % HEADS
                return m[:, h, c * CH:(c + 1) * CH]

            def four_units(bank, name, half, lhs, rhs):
                for u in range(4 * half, 4 * half + 4):
                    mm = pe.matmul(unit(bank, u % 4), lhs(u), rhs(u), start=(u % 4 == 0), stop=True, skip_group_check=True)
                mm.then_inc(S(name), 1)

            def turn_units(name, src):
                for u in range(UNITS):
                    mm = pe.transpose(unit(ps[2 + u // 4], u % 4), chan(src, u), ident)
                    if u % 4 == 3:
                        mm.then_inc(S(name), 1)

            pe.wait_ge(*at("con_rest", 16))
            row_sums("qk", "row_of", 0, 8, ps[0], ("qk_sq", 4))
            mix(6)
            mix(7)
            pe.wait_ge(*at("qk_row", 1))
            spread_rows("qk_spread", "row_sel", small[0:8, 7, :], 8, 8, (0, 1, 2, 3))
            mix(8)
            pe.wait_ge(*at("g_cum", 1))
            pe.wait_ge(*at("qk_n", 4))
            pe.wait_ge(*at("beta", 1))
            spread_rows("g_spread", "row_sel", g_cum[0:4, :], 4, 4, (0, 1))
            spread_rows("b_spread", "row_sel", beta_row[0:4, :], 4, 4, (2, 3))
            for q, src in enumerate((g_cum, beta_row)):
                for c in range(2):
                    pe.transpose(ps[6][:, 8 * q + 4 * c:8 * q + 4 * c + 4], src[0:4, c * CH:(c + 1) * CH], ident[0:4, 0:4])\
                        .then_inc(S("col_turned"), 1)
            mix(9)
            pe.wait_ge(*at("g_row", 2))
            pe.wait_ge(*at("kb", 2))
            for half in range(2):
                four_units(ps[half], "lt_mm", half, lambda u: chan(k_n, u), lambda u: chan(kb, u))
            pe.wait_ge(*at("qkv_silu", 6))
            turn_units("v_turned", qkv[:, 8:12, :])
            mix(10)
            pe.wait_ge(*at("lt", 2))
            for half in range(2):
                four_units(ps[half], "at_mm", half, lambda u: chan(k_n, u), lambda u: chan(q_n, u))
            mix(11)
            pe.wait_ge(*at("v_nat", 8))
            turn_units("k_turned", k_n)
            mix(12)
            pe.wait_ge(*at("mix_evac", 13))
            pe.wait_ge(*at("at_done", 1))
            pe.wait_ge(*at("k_nat", 8))
            with pe.Fori(0, LEVELS) as i:
                pe.wait_ge(*at("inv_b", i + 1))
                pe.wait_ge(*at("inv_t", i * 4 + 1))
                four_units(ps[0], "inv_x", 0, lambda u: unit(b_mat, u), lambda u: unit(t_mat, u))
                pe.wait_ge(*at("inv_t", i * 4 + 3))
                four_units(ps[1], "inv_x", 1, lambda u: unit(b_mat, u), lambda u: unit(t_mat, u))
                pe.wait_ge(*at("inv_xv", i + 1))
                four_units(ps[2], "inv_y", 0, lambda u: unit(tt_mat, u), lambda u: unit(x_mat, u))
                four_units(ps[4], "inv_y", 0, lambda u: unit(x_mat, u), lambda u: unit(tt_mat, u))
                pe.wait_ge(*at("inv_t", i * 4 + 4))
                pe.wait_ge(*at("inv_xa", i + 1))
                four_units(ps[3], "inv_y", 1, lambda u: unit(tt_mat, u), lambda u: unit(x_mat, u))
                four_units(ps[5], "inv_y", 1, lambda u: unit(x_mat, u), lambda u: unit(tt_mat, u))
            pe.wait_ge(*at("inv_t", 4 * LEVELS + 2))
            four_units(ps[0], "v_mm", 0, lambda u: unit(tt_mat, u), lambda u: unit(v_beta, u))
            pe.wait_ge(*at("inv_t", 4 * LEVELS + 4))
            for h in range(HEADS):
                mm = pe.matmul(unit(ps[1], h), unit(k_be, h), unit(tt_mat, HEADS + h), start=(h == 0), stop=True,
                               skip_group_check=True)
            mm.then_inc(S("w_mm"), 1)
            row_sums("short", "grp_row_of", 4, 4, ps[6], ("short_sq", 1))
            mix(13)
            pe.wait_ge(*at("v_new", 1))
            four_units(ps[2], "s_mm", 0, lambda u: unit(k_dec, u), lambda u: unit(v_new, u))
            four_units(ps[3], "o_mm", 0, lambda u: unit(v_new, u), lambda u: unit(at_mat, u))
            pe.wait_ge(*at("short_rstd", 1))
            spread_rows("short_spread", "grp_sel", small[0:8, 7, :], 4, 8, (6, 0))
            pe.wait_ge(*at("w_t", 1))
            pe.wait_ge(*at("state", 1))
            for h in range(HEADS):
                pe.matmul(unit(ps[1], h), unit(tt_mat, HEADS + h), unit(v_beta, HEADS + h), start=(h == 0), stop=False,
                          skip_group_check=True)
                mm = pe.matmul(unit(ps[1], h), unit(x_mat, h), unit(state, h), start=False, stop=True, skip_group_check=True)
            mm.then_inc(S("v_mm"), 1)
            mix(14)
            pe.wait_ge(*at("v_new", 2))
            for h in range(HEADS):
                pe.matmul(unit(ps[2], h), unit(state, h), q_n[:, h, CH:2 * CH], start=(h == 0), stop=False, skip_group_check=True)
                mm = pe.matmul(unit(ps[2], h), unit(v_new, HEADS + h), unit(at_mat, HEADS + h), start=False, stop=True,
                               skip_group_check=True)
            mm.then_inc(S("o_mm"), 1)
            row_sums("o", "row_of", 0, 4, ps[3], ("o_sq", 1))
            pe.wait_ge(*at("o_rstd", 1))
            pe.wait_ge(*at("short_out", 2))
            spread_rows("o_spread", "row_sel", small[0:8, 7, :], 4, 8, (0, 1))
            pe.wait_ge(*at("mix_evac", 15))
            for n in range(4):
                if n >= 2:
                    pe.wait_ge(*at("mix_resid", n - 1))
                wide(FIRST["mix_out"] + n, ps[4 + n % 2], xh, xl, "mo_xl" if n == 0 else None, lambda k: k // 2 + 1)
            pe.wait_ge(*at("mix_resid", 3))
            ffn("ffn2", "n3", ("mix_resid", 4))

            column_sums("f", lambda k: kn[:, k, :], KT, ps[6][:, 0:T], ("f_sq", 1), by_pair=True)
            column_sums("f", lambda k: qn[:, k, :], KT, ps[5][:, 0:T], ("fg_sq", 8))
            for n in range(4):
                s = FIRST["glu"] + 2 * n
                if n:
                    pe.wait_ge(*at("glu", n))
                wide(s, ps[4], xh, xl, "h_xl" if n == 0 else None, one)
                wide(s + 1, ps[5], xh, xl)
            s = FIRST["lat"]
            pe.wait_ge(*at("glu", 4))
            for n in range(3):
                if n == 2:
                    pe.wait_ge(*at("lat", 1))
                wide(s + n, ps[4 + n % 2], xh, xl)
            pe.wait_ge(*at("m2", 1))
            pe.wait_ge(*at("lat_sq", 1))
            for k in range(3):
                pe.matmul(ps[6][:, 0:T], ones, lat_sq[:, k, :], start=(k == 0), stop=(k == 2), skip_group_check=True)
            for k in range(2):
                mm = pe.matmul(ps[6][:, T:2 * T], ones, lat_sq[:, 3 + k, :], start=(k == 0), stop=(k == 1), skip_group_check=True)
            mm.then_inc(S("lat_stat"), 1)
            pe.wait_ge(*at("lat", 4))
            swap = const("swap", P)
            pe.matmul(ps[7][:, 0:T], swap, kr_raw, start=True, stop=True).then_inc(S("kr_swap"), 1)
            for n in range(3):
                s = FIRST["uq"] + n
                pe.wait_ge(low_done, s + 1)
                if n:
                    pe.wait_ge(*at("q", 2 * n))
                h, l = (w[:, s % SLOTS, 0:1536].rearrange("p (k m) -> p k m", k=3) for w in (wh, wl))
                for m in range(4):
                    for k in range(3):
                        if n == 0 and m == 0:
                            pe.wait_ge(*at("lat_yl", k + 1))
                        for j, (w, r) in enumerate(((h, yh), (h, yl), (l, yh))):
                            mm = pe.matmul(ps[4 + m // 2][:, (m % 2) * T:(m % 2 + 1) * T], w[:, k, m * P:(m + 1) * P], r[:, k, :],
                                           start=(m % 2 == 0 and k == 0 and j == 0), stop=(k == 2 and j == 2),
                                           skip_group_check=True)
                mm.then_inc(taken, 1)
            s = FIRST["ukv"]
            pe.wait_ge(low_done, s + 1)
            pe.wait_ge(*at("lat_yl", 5))
            h, l = (w[:, s % SLOTS, :].rearrange("p (k m) -> p k m", k=2) for w in (wh, wl))
            for m in range(NH):
                for k in range(2):
                    for j, (w, r) in enumerate(((h, yh), (h, yl), (l, yh))):
                        mm = pe.matmul(ps[m // 2][:, (m % 2) * T:(m % 2 + 1) * T], w[:, k, m * P:(m + 1) * P], r[:, 3 + k, :],
                                       start=(m % 2 == 0 and k == 0 and j == 0), stop=(k == 1 and j == 2), skip_group_check=True)
            mm.then_inc(taken, 1)
            pe.wait_ge(*at("q", 6))
            pe.wait_ge(*at("kr", 1))
            for b in range(2):
                pe.matmul(pair(ps[6 + b][:, :]), swap, qr_raw[:, 2 * b:2 * b + 2, :], start=True, stop=True).then_inc(S("q_swap"), 1)
            pe.wait_ge(low_done, s + 2)
            pe.wait_ge(*at("k", 4))
            h, l = (w[:, (s + 1) % SLOTS, :].rearrange("p (k m) -> p k m", k=2) for w in (wh, wl))
            for tk in range(2):
                for half in range(2):
                    for k in range(2):
                        for j, (w, r) in enumerate(((h, yh), (h, yl), (l, yh))):
                            mm = pe.matmul(ps[2 * tk + half][:, :], r[:, 3 + k, tk * P:(tk + 1) * P],
                                           w[:, k, half * 512:(half + 1) * 512], start=(k == 0 and j == 0),
                                           stop=(k == 1 and j == 2), skip_group_check=True)
            mm.then_inc(taken, 1)

            def scores(h):
                if h >= 2:
                    pe.wait_ge(*at("att_max", h - 1))
                bank, off = ps[h % 2], ROPE * (h % 2)
                for qt in range(2):
                    out = bank[:, qt * P:qt * P + (qt + 1) * P]
                    n = (qt + 1) * P
                    pe.matmul(out, qn[:, h, qt * P:(qt + 1) * P], kn[:, h, 0:n], start=(qt == 0), stop=False, skip_group_check=True)
                    mm = pe.matmul(out, qr[off:off + ROPE, h // 2, qt * P:(qt + 1) * P], kr[off:off + ROPE, 0:n], start=False,
                                   stop=True, skip_group_check=True)
                mm.then_inc(S("att_s"), 1)

            def turn(h):
                pe.wait_ge(*at("att_norm", h + 1))
                if h >= 2:
                    pe.wait_ge(*at("att_pt", h - 1))
                for j in range(3):
                    mm = pe.transpose(ps[2 + h % 2][:, j * P:(j + 1) * P], prob[h % 2][:, j * P:(j + 1) * P], ident)
                mm.then_inc(S("att_turned"), 1)

            def weigh(h):
                pe.wait_ge(*at("att_pt", h + 1))
                if h >= 2:
                    pe.wait_ge(*at("o_yl", h - 1))
                bank = ps[4 + h % 2]
                pe.matmul(bank[:, 0:T], v[:, 0, h * P:(h + 1) * P], prob_t[h % 2][:, 0:T], start=True, stop=False,
                          skip_group_check=True)
                pe.matmul(bank[:, P:T], v[:, 1, h * P:(h + 1) * P], prob_t[h % 2][:, T:T + P], start=False, stop=True,
                          skip_group_check=True).then_inc(S("att_o"), 1)

            pe.wait_ge(*at("v", 4))
            pe.wait_ge(*at("qr", 1))
            for h in range(NH + 2):
                if h < NH:
                    scores(h)
                if 1 <= h <= NH:
                    turn(h - 1)
                if h >= 2:
                    weigh(h - 2)

            def four(phase, x, y, freed, first=None, base=one, start_free=None):
                for n in range(4):
                    if n < 2 and start_free:
                        pe.wait_ge(*at(*start_free[n]))
                    if n >= 2:
                        pe.wait_ge(*at(freed, n - 1))
                    wide(FIRST[phase] + n, ps[4 + n % 2], x, y, first if n == 0 else None, base)

            four("gate_b", xh, xl, "gate_b", start_free=(("o_yl", 7), ("o_yl", 8)))
            four("attn_out", yh, yl, "mixed_b", start_free=(("gate_b", 3), ("gate_b", 4)))
            four("gate_a", xh, xl, "gate_a", start_free=(("mixed_b", 3), ("mixed_b", 4)))
            pe.wait_ge(*at("conv_done", 1))
            for k in range(KT):
                mm = pe.matmul(ps[7][:, 0:T], ones, conv[:, k, :], start=(k == 0), stop=(k == KT - 1), skip_group_check=True)
            mm.then_inc(S("ln_mean"), 1)
            column_sums("ln", lambda k: v_sq[:, k, :], KT, ps[6][:, 0:T], ("ln_sq", 1))
            four("conv_out", yh, yl, "mixed", "c_yl", one, start_free=(("gate_a", 3), ("gate_a", 4)))
            four("w_out", xh, xl, "y", "w_xl", one, start_free=(("mixed", 3), ("mixed", 4)))
            column_sums("y", lambda k: v_sq[:, k, :], KT, ps[6][:, 0:T], ("y_sq", 4))
            column_sums("x3", lambda k: v_sq[:, k, :], KT, ps[6][:, T:2 * T], ("x3_sq", 1))

            s0 = FIRST["mlp_in"]
            pe.wait_ge(*at("y", 4))
            clear_sums()
            wide(s0, ps[4], xh, xl, "h2_xl", one)
            with pe.Fori(0, (MLP_STEPS - 1) // SLOTS) as i:
                for r in range(SLOTS):
                    s = s0 + 1 + 2 * r
                    pe.wait_ge(*at("mlp_relu", i * 3 + (r + 1)))
                    wide(i * 6 + s, ps[4], xh, xl, slab=s)
                    pe.wait_ge(*at("mlp_fl", i * 3 + (r + 1)))
                    deep(i * 6 + (s + 1), slab=s + 1)
            pe.wait_ge(*at("mlp_fl", MLP_STEPS))
            deep(N_SLABS - 1)
            column_sums("z", lambda k: v_sq[:, k, :], KT, ps[6][:, 0:T], ("z_sq", 4))
            for tk in range(2):
                for half in range(2):
                    for t in range(4 * half, 4 * half + 4):
                        pe.wait_ge(*at("x4", t // 2 + 1))
                        if tk == 1:
                            pe.wait_ge(*at("z_std", 1))
                        mm = pe.transpose(ps[4 + 2 * tk + half][:, (t % 4) * P:(t % 4 + 1) * P],
                                          resid[:, t, tk * P:(tk + 1) * P], ident)
                    mm.then_inc(S("turned"), 1)


_INS = ["x", "ffn1_norm", "ffn1_w_in", "ffn1_w_out", "mix_norm", "w_mix_in", "conv_short_w", "conv_out_norm",
        "gdn_conv_w", "gdn_A_log", "gdn_dt_bias", "gdn_out_norm", "w_mix_out", "ffn2_norm", "ffn2_w_in", "ffn2_w_out",
        "final_norm", "c_2", "positions_2", "w_ada_2", "b_ada_2", "g_pre_mix_2", "g_post_mix_2", "g_pre_mlp_2",
        "g_post_mlp_2", "w_in_2", "conv_w_2", "conv_b_2", "conv_norm_g_2", "conv_norm_b_2", "w_conv_out_2",
        "q_norm_g_2", "w_uq_2", "kv_norm_g_2", "w_ukv_2", "w_attn_out_2", "w_out_2", "w_mlp_in_2", "w_mlp_out_2"]


def kernel(**inputs):
    import concourse.bacc as bacc
    from concourse.bass_utils import run_bass_kernel_spmd

    nc = bacc.Bacc("TRN2", target_bir_lowering=False, num_devices=1)
    arrays = {f"in_{n}": np.ascontiguousarray(inputs[n]) for n in _INS}
    arrays["in_table"] = constants()
    aps = {n[3:]: nc.dram_tensor(n, v.shape, mybir.dt.from_np(v.dtype), kind="ExternalInput").ap()
           for n, v in arrays.items()}
    aps["out"] = nc.dram_tensor("out", (1, T, D), F32, kind="ExternalOutput").ap()
    two_blocks(nc, aps)
    return run_bass_kernel_spmd(nc, [arrays], core_ids=[0]).results[0]["out"]
```

```python
from contextlib import ExitStack

import numpy as np

import concourse.bass as bass
from concourse import mybir

F32 = mybir.dt.float32
F32R = mybir.dt.float32r
BF16 = mybir.dt.bfloat16
I32 = mybir.dt.int32
ACT = mybir.ActivationFunctionType
ALU = mybir.AluOpType
AX_X = mybir.AxisListType.X

P = 128
T = 256
D = 1024
KT = D // P
EPS = 1e-6

D_FF = 2816
FF_STEPS = D_FF // 256
D_CONV = 512
HEADS = 4
DH = 128
CH = 128
UNITS = HEADS * (T // CH)
LEVELS = 7
MIX_COLS = 3592

TAPS = 31
PAD = TAPS - 1
NH = 8
NOPE = 128
ROPE = 64
Q_LAT = 384
KV_LAT = 256
D_MLP = 4096
MLP_STEPS = D_MLP // 256
POOL_TILES = ((0, 1), (6, 7))
DVE_TILES = ((2, 3), (4, 5))
GATE_AT_HEAD = {0: ("gate_b", 2), 1: ("gate_b", 3), 2: ("gate_a", 0), 4: ("gate_a", 1), 6: ("gate_a", 2), 8: ("gate_a", 3)}

N_VEC_0 = 8
N_VEC = 21
ATT_SCALE = float((NOPE + ROPE) ** -0.5)
SLOTS = 3
SLAB = 2048
ADA_TILES = 6 * KT
ADA_STEPS = ADA_TILES // 2
ADA_MIX = 4

_at = 0
C = {}
for _name, _width in (("ident", P), ("ones", P), ("eps", 1), ("inv_freq", 1), ("qk_scale", 1), ("swap", P),
                      ("causal", 3 * P), ("upper", P), ("levels", LEVELS * P), ("row_of", 64), ("grp_row_of", 32),
                      ("row_sel", 8 * P), ("grp_sel", 4 * P), ("restart", T)):
    C[_name] = _at
    _at += _width
N_CONST = _at
N_CONST_FIRST = C["swap"]
N_CONST_BOTH = C["upper"]

VECS = {}
_rows = [0, 0, 0, 0]
for _g, _name, _n in ((0, "ffn1_norm", 8), (0, "mix_norm", 8), (0, "conv_out_norm", 4), (0, "gdn_out_norm", 1),
                      (0, "ffn2_norm", 8), (0, "final_norm", 8), (0, "conv_short_w", 12), (0, "gdn_conv_w", 48),
                      (1, "g_pre_mix_2", 8), (1, "g_post_mix_2", 8), (1, "g_pre_mlp_2", 8), (1, "g_post_mlp_2", 8),
                      (1, "conv_b_2", 8), (1, "conv_norm_g_2", 8), (1, "conv_norm_b_2", 8), (1, "q_norm_g_2", 3),
                      (1, "kv_norm_g_2", 2), (1, "c_2", 8), (1, "b_ada_2", 48)):
    VECS[_name] = (_g, _rows[_g])
    _rows[_g] += _n
_rows[2] = _rows[3] = 124
STAGE_ROWS = tuple(_rows)


def constants():
    t = np.zeros((P, N_CONST), np.float32)
    p = np.arange(P)

    def put(name, a):
        t[:a.shape[0], C[name]:C[name] + a.shape[1]] = a

    put("ident", np.eye(P))
    put("ones", np.ones((P, P)))
    swap = np.zeros((P, P))
    for m in range(P):
        if m % ROPE < ROPE // 2:
            swap[m + ROPE // 2, m] = -1
        else:
            swap[m - ROPE // 2, m] = 1
    put("swap", swap)
    j, i = p[:, None], p[None, :]
    put("upper", (i >= j) * 1.0)
    for lev in range(LEVELS):
        s = 1 << lev
        m = (i // (2 * s) == j // (2 * s)) & ((i // s) % 2 == 1) & ((j // s) % 2 == 0)
        t[:, C["levels"] + lev * P:C["levels"] + (lev + 1) * P] = m
    diag = np.where(p[:, None] >= p[None, :], 0.0, -1e30)
    put("causal", np.concatenate([diag, np.zeros((P, P)), diag], 1))
    row_of = np.zeros((P, 8, 8))
    for r in range(8):
        row_of[:, r, r] = 1
    put("row_of", row_of.reshape(P, 64))
    grp = np.zeros((P, 4, 8))
    sel = np.zeros((8, 4, P))
    for r in range(4):
        grp[:64, r, 2 * r] = 1
        grp[64:, r, 2 * r + 1] = 1
        sel[2 * r, r, :64] = 1
        sel[2 * r + 1, r, 64:] = 1
    put("grp_row_of", grp.reshape(P, 32))
    put("grp_sel", sel.reshape(8, 512))
    rs = np.zeros((8, 8, P))
    for r in range(8):
        rs[r, r, :] = 1
    put("row_sel", rs.reshape(8, 1024))
    restart = np.ones((8, T))
    restart[:, ::CH] = 0
    put("restart", restart)
    freq = 1.0 / np.power(np.float32(10000.0), np.arange(0, ROPE, 2, dtype=np.float32) / np.float32(ROPE)).astype(np.float32)
    put("inv_freq", freq.astype(np.float32)[p % (ROPE // 2)][:, None])
    put("eps", np.full((P, 1), EPS))
    qk = np.ones((8, 1))
    qk[:HEADS] = DH ** -0.5
    put("qk_scale", qk)
    return t


def slab_plan():
    plan = []

    def ffn(name):
        plan.extend([(name + "_gate", 0), (name + "_up", 0)])
        for k in range(1, FF_STEPS):
            plan.extend([(name + "_gate", k), (name + "_up", k), (name + "_down", k - 1)])
        plan.append((name + "_down", FF_STEPS - 1))

    ffn("ffn1")
    plan.extend([("mix", n) for n in range(15)])
    plan.extend([("mix_out", n) for n in range(4)])
    ffn("ffn2")
    plan.extend([("glu", n) for n in range(8)] + [("lat", n) for n in range(3)])
    plan.extend([("gate_b", 0), ("gate_b", 1)])
    plan.extend([("uq", n) for n in range(3)] + [("ukv", n) for n in range(2)])
    plan.extend([("gate_b", 2), ("gate_b", 3)] + [("gate_a", n) for n in range(4)])
    for phase in ("attn_out", "conv_out", "w_out"):
        plan.extend([(phase, n) for n in range(4)])
    plan.append(("mlp_in", 0))
    for k in range(1, MLP_STEPS):
        plan.extend([("mlp_in", k), ("mlp_out", k - 1)])
    plan.append(("mlp_out", MLP_STEPS - 1))
    return plan


SEQUENCES = {
    "x_high": (("n1_xh", 8), ("n2_xh", 8), ("mo_xh", 4), ("n3_xh", 8), ("h_xh", 8), ("c_xh", 8), ("h2_xh", 8)),
    "x_low": (("n1_xl", 8), ("n2_xl", 8), ("mo_xl", 4), ("n3_xl", 8), ("h_xl", 8), ("c_xl", 8), ("h2_xl", 8)),
    "y_high": (("lat_yh", 5), ("o_yh", 8), ("w_yh", 4)),
    "y_low": (("lat_yl", 5), ("o_yl", 8), ("w_yl", 4)),
    "squares": (("n1_sq", 4), ("n2_sq", 4), ("n3_sq", 4), ("f_sq", 4)),
    "sums": (("n1_stat", 1), ("n2_stat", 1), ("qk_stat", 1), ("short_stat", 1), ("o_stat", 1), ("n3_stat", 1),
             ("f_stat", 2), ("lat_stat", 1), ("ln_stat", 1), ("y_stat", 1), ("x3_stat", 1), ("z_stat", 1)),
    "roots": (("n1_std", 1), ("n2_std", 1), ("qk_std", 1), ("short_std", 1), ("o_std", 1), ("n3_std", 1), ("f_std", 1),
              ("g_std", 1), ("lat_std", 2), ("ln_std", 1), ("y_std", 1), ("x3_std", 1), ("z_std", 1)),
    "inverses": (("n1_rstd", 1), ("n2_rstd", 1), ("qk_rstd", 1), ("short_rstd", 1), ("o_rstd", 1), ("n3_rstd", 1),
                 ("f_rstd", 1), ("g_rstd", 1), ("ln_rstd", 1), ("y_rstd", 1), ("x3_rstd", 1), ("z_rstd", 1)),
    "resid_ready": (("x_in", 4), ("ffn1_resid", 4), ("mix_resid", 4), ("ffn2_resid", 4), ("x3", 4), ("x4", 4)),
    "hidden_gate": (("ffn1_gate", FF_STEPS), ("ffn2_gate", FF_STEPS), ("mlp_relu", MLP_STEPS)),
    "hidden_up": (("ffn1_up", FF_STEPS), ("ffn2_up", FF_STEPS)),
    "hidden_silu": (("ffn1_silu", FF_STEPS), ("ffn2_silu", FF_STEPS)),
    "hidden": (("ffn1_h", FF_STEPS), ("ffn2_h", FF_STEPS), ("mlp_sq", MLP_STEPS)),
    "hidden_high": (("ffn1_fh", FF_STEPS), ("ffn2_fh", FF_STEPS), ("mlp_fh", MLP_STEPS)),
    "hidden_low": (("ffn1_fl", FF_STEPS), ("ffn2_fl", FF_STEPS), ("mlp_fl", MLP_STEPS)),
}
SHARED = {}
for _sem, _stages in SEQUENCES.items():
    _n = 0
    for _stage, _count in _stages:
        SHARED[_stage] = (_sem, _n)
        _n += _count

PLAN = slab_plan()
SLAB_OF = {entry: s for s, entry in enumerate(PLAN)}
FIRST = {}
for _s, (_phase, _step) in enumerate(PLAN):
    FIRST.setdefault(_phase, _s)
N_SLABS = len(PLAN)
MIX_COL = [1536, 1792, 2048, 2304, 2560, 2816, -1, 512, 768, 1024, 1280, 0, 256, 3072, 3328]
KEY_BANKS, VALUE_BANKS = (0, 1, 6, 7), (4, 5, 0, 1)
MIX_AB = 6
OUT_ORDER = ((0, 0), (0, 1), (1, 0), (1, 1))
ADA_AFTER = (4, 8, 12, 14)


def slab_dmas(s):
    phase, step = PLAN[s]
    if phase == "mix" and step == MIX_AB:
        return 2
    if phase == "lat" and step == 2:
        return 3
    return {"uq": 3, "ukv": 2}.get(phase, 1)


def landed(s):
    return 16 * sum(slab_dmas(n) for n in range(s % SLOTS, s + 1, SLOTS))


def two_pi():
    c1 = 6.28125
    c2 = float((np.float32(2 * np.pi - c1).view(np.uint32) & np.uint32(0xFFFFF000)).view(np.float32))
    return c1, c2, float(np.float32(2 * np.pi - c1 - c2))


class Steps:

    def __init__(self, engine, semaphore):
        self.engine, self.semaphore, self.n = engine, semaphore, 0

    def __call__(self, instruction):
        instruction.then_inc(self.semaphore, 1)
        self.n += 1

    def sync(self):
        self.engine.wait_ge(self.semaphore, self.n)


def slab_floats(s):
    phase, step = PLAN[s]
    if phase == "mix" and step == MIX_AB:
        return KT * P
    if phase == "uq":
        return 3 * 512
    return SLAB


def two_blocks(nc, a):
    with ExitStack() as ctx:
        def sem(name):
            return ctx.enter_context(nc.semaphore(name))

        def sb(name, shape, dt=F32, where=ctx):
            return where.enter_context(nc.sbuf_tensor(name, shape, dt))

        con = sb("con", [P, N_CONST])
        raw = sb("raw", [P, SLOTS, SLAB])
        wh = sb("wh", [P, SLOTS, SLAB], F32R)
        wl = sb("wl", [P, SLOTS, SLAB], F32R)
        resid = sb("resid", [P, KT, T])
        xh = sb("xh", [P, KT, T], F32R)
        xl = sb("xl", [P, KT, T], F32R)
        vec = sb("vec", [P, 4, P])
        ada_raw = sb("ada_raw", [P, KT, 256])
        ada_sum = sb("ada_sum", [P, 256])
        ada = sb("ada", [P, ADA_TILES])
        mods = sb("mods", [P, 4, KT])
        c_act = sb("c_act", [P, KT])
        rstd = sb("rstd", [P, T])
        std = sb("std", [P, T])
        zero = sb("zero", [1, 512], BF16)
        fh = sb("fh", [P, 2, T], F32R)
        fl = sb("fl", [P, 2, T], F32R)
        hid = sb("hid", [P, 4, 2 * T])
        a_log = sb("a_log", [4, 2])
        g_cum = sb("g_cum", [4, T])
        beta_row = sb("beta_row", [4, T])
        att_col = sb("att_col", [P, 16])

        with ExitStack() as first:
            work1 = sb("work1", [P, 17600], where=first)
        yh = sb("yh", [P, KT, T], F32R)
        yl = sb("yl", [P, KT, T], F32R)
        work2 = sb("work2", [P, 13560])
        def tiles(ap, n):
            return ap.rearrange("p (n t) -> p n t", n=n)

        pt_mem = ada_raw[:, :, :].rearrange("p k m -> p (k m)")
        tap_mem = tiles(pt_mem[:, 6 * P:6 * P + 2 * T], 2)
        ps = [ctx.enter_context(nc.psum_tensor(f"ps{i}", [P, 512], F32)) for i in range(8)]

        def const(name, width, rows=P):
            return con[0:rows, C[name]:C[name] + width]

        ident, ones = const("ident", P), const("ones", P)
        eps = const("eps", 1)

        def col(name, t, rows=P):
            g, r = VECS[name]
            return vec[0:rows, g, r + t:r + t + 1]

        def tap(k, t):
            r = k * KT + t
            return vec[:, 2 + r // 124, r % 124:r % 124 + 1]

        def pair(ap):
            return ap.rearrange("p (m t) -> p m t", m=2)

        def spread(ap, n):
            return ap.unsqueeze(1).to_broadcast([ap.shape[0], n, ap.shape[1]])

        used = {"w1": 0, "w2": 0}

        def w1(n):
            used["w1"] += n
            return work1[:, used["w1"] - n:used["w1"]]

        def w2(n):
            used["w2"] += n
            return work2[:, used["w2"] - n:used["w2"]]

        QW = T + 3
        w_qkvp = w1(12 * QW)
        qkvp = tiles(w_qkvp, 12)
        t_mat, tt_mat, x_mat = (w_qkvp[:, n * 1024:(n + 1) * 1024] for n in range(3))
        qkv = tiles(w1(12 * T), 12)
        w_sq = w1(2048)
        sq = tiles(w_sq, KT)
        gz = tiles(w1(1024), 4)
        w_cb = w1(1024)
        cb = tiles(w_cb, 4)
        w_cc = w1(1024)
        cc = tiles(w_cc, 4)
        mpad = tiles(w1(4 * (T + 2)), 4)
        g_row = tiles(w1(1024), 4)
        w_kb = w1(1024)
        kb = tiles(w_kb, 4)
        dt_mat = w1(1024)
        lt_mat = w1(1024)
        at_mat = w1(1024)
        q_n, k_n = qkv[:, 0:4, :], qkv[:, 4:8, :]
        v_beta = qkv[:, 8:12, :].rearrange("p n t -> p (n t)")
        k_be = qkv[:, 4:6, :].rearrange("p n t -> p (n t)")
        k_dec = qkv[:, 6:8, :].rearrange("p n t -> p (n t)")
        state = dt_mat[:, 0:512]
        exp_g = tiles(w_sq[:, 0:512], 4)
        o_t = g_row
        v_new = w_kb
        cols = w1(48)
        small = tiles(hid[0:8, :, :].rearrange("p n t -> p (n t)"), 8)
        b_mat = w_sq[:, 0:1024]

        UW = T + PAD
        upad = tiles(w2(KT * UW), KT)
        conv = tiles(w2(2048), KT)
        w_qn = w2(2048)
        qn = tiles(w_qn, KT)
        w_kn = w2(2048)
        kn = tiles(w_kn, KT)
        w_qr = w2(2048)
        qr_raw = tiles(w_qr[:, 0:1024], 4)
        qr = tiles(w_qr[:, 1024:2048], 4)
        w_v = w2(2048)
        v = tiles(w_v, 2)
        kr_raw = w2(T)
        kr = w2(T)
        cosines = w2(T)
        sines = w2(T)

        stage = tiles(lt_mat[:, 0:512], 4)
        lat = tiles(w_v[:, 0:5 * T], 5)
        lat_sq = tiles(w_qr[:, 0:5 * T], 5)
        v_sq = tiles(w_v, KT)
        ln_squares = tiles(w_qr, KT)
        upad_out = w_qr.rearrange("p (a n) -> p a n", a=2)
        score = [hid[:, n, 0:3 * P] for n in range(2)]
        prob = [hid[:, 2 + n, 0:3 * P] for n in range(2)]

        prob_t = [pt_mem[:, n * 3 * P:(n + 1) * 3 * P] for n in range(2)]
        gate_mem = {"gate_b": tiles(con[:, N_CONST_BOTH:N_CONST_BOTH + KT * T], KT), "gate_a": qn}
        assert used["w1"] <= 17600 and used["w2"] <= 13560, used

        named = {}

        def S(name):
            name = SHARED.get(name, (name, 0))[0]
            if name not in named:
                named[name] = sem("s_" + name)
            return named[name]

        def at(name, count):
            return S(name), count + SHARED.get(name, (name, 0))[1]

        slot_loaded = [sem(f"slot{i}_loaded") for i in range(SLOTS)]
        high_done = sem("high_done")
        low_done = sem("low_done")
        taken = sem("taken")
        s_vstep, s_astep, s_pstep = sem("vector_step"), sem("scalar_step"), sem("pool_step")

        dram = {n: a[n][0] for n in ("ffn1_w_in", "ffn1_w_out", "ffn2_w_in", "ffn2_w_out", "w_mix_in", "w_mix_out",
                                     "w_ada_2", "w_in_2", "w_conv_out_2", "w_uq_2", "w_ukv_2", "w_attn_out_2",
                                     "w_out_2", "w_mlp_in_2", "w_mlp_out_2")}
        rows = {n: w.rearrange("(k p) n -> p k n", p=P) for n, w in dram.items()}
        x_rows = a["x"][0].rearrange("(k p) n -> p k n", p=P)
        out_rows = a["out"][0].rearrange("(k p) n -> p k n", p=P)
        gu, gq = 0, 2048

        block = ctx.enter_context(nc.Block())

        @block.sync
        def _(sp):
            def slot(s, k):
                n = SLAB if k != 3 else 1536
                return raw[:, s % SLOTS, 0:n].rearrange("p (k m) -> p k m", k=k)

            def free(s):
                if not isinstance(s, int) or s >= SLOTS:
                    sp.wait_ge(low_done, s - SLOTS + 1)

            def wide(s, slot_of, w, c0):
                free(s)
                sp.dma_start(slot(slot_of, KT), rows[w][:, :, bass.ds(c0, 256)]).then_inc(slot_loaded[slot_of % SLOTS], 16)

            def deep(s, slot_of, w, step):
                free(s)
                sp.dma_start(slot(slot_of, 2), rows[w][:, bass.ds(step * 2, 2), :]).then_inc(slot_loaded[slot_of % SLOTS], 16)

            def modulation(step):
                if not isinstance(step, int) or step:
                    sp.wait_ge(*at("ada_free", step))
                sp.dma_start(ada_raw[:, :, :], rows["w_ada_2"][:, :, bass.ds(step * 256, 256)]).then_inc(S("ada_loaded"), 16)

            def ffn(name, w_in, w_out, start):
                s0 = FIRST[name + "_gate"]
                wide(s0, s0, w_in, 0)
                wide(s0 + 1, s0 + 1, w_in, D_FF)
                modulation(0 if name == "ffn1" else FF_STEPS - 1 + ADA_MIX)
                for k in range(1, start):
                    s = s0 + 3 * k - 1
                    wide(s, s, w_in, 256 * k)
                    wide(s + 1, s + 1, w_in, D_FF + 256 * k)
                    deep(s + 2, s + 2, w_out, k - 1)
                with sp.Fori(0, FF_STEPS - start) as i:
                    s = s0 + 3 * start - 1
                    wide(s + i * 3, s, w_in, i * 256 + 256 * start)
                    wide(s + 1 + i * 3, s + 1, w_in, i * 256 + (D_FF + 256 * start))
                    deep(s + 2 + i * 3, s + 2, w_out, i + (start - 1))
                    modulation(i + (1 if name == "ffn1" else FF_STEPS + ADA_MIX))
                s = s0 + 3 * FF_STEPS - 1
                deep(s, s, w_out, FF_STEPS - 1)

            sp.dma_start(sq.rearrange("p (a b) t -> p a (b t)", a=2), x_rows).then_inc(S("x_loaded"), 16)
            ffn("ffn1", "ffn1_w_in", "ffn1_w_out", 2)
            for n, c0 in enumerate(MIX_COL):
                s = FIRST["mix"] + n
                if n == MIX_AB:
                    free(s)
                    dst = raw[:, s % SLOTS, 0:KT * P].rearrange("p (k m) -> p k m", k=KT)
                    for m, c in ((0, 3584), (32, 3588)):
                        sp.dma_start(dst[:, :, m:m + HEADS], rows["w_mix_in"][:, :, c:c + HEADS])\
                            .then_inc(slot_loaded[s % SLOTS], 16)
                else:
                    wide(s, s, "w_mix_in", c0)
                if n % 4 == 3:
                    modulation(FF_STEPS - 1 + n // 4)
            modulation(FF_STEPS - 1 + 3)
            for n in range(4):
                wide(FIRST["mix_out"] + n, FIRST["mix_out"] + n, "w_mix_out", 256 * n)
            ffn("ffn2", "ffn2_w_in", "ffn2_w_out", 2)
            uq = rows["w_uq_2"].rearrange("p k (h c) -> p k h c", c=NOPE + ROPE)
            ukv = rows["w_ukv_2"].rearrange("p k (h c) -> p k h c", c=2 * P)
            column = {"gate_b": ("w_in_2", 3776), "gate_a": ("w_in_2", 2752), "attn_out": ("w_attn_out_2", 0),
                      "conv_out": ("w_conv_out_2", 0), "w_out": ("w_out_2", 0)}
            for s in range(FIRST["glu"], FIRST["mlp_in"]):
                phase, n = PLAN[s]
                if phase == "glu":
                    wide(s, s, "w_in_2", 1024 * (n % 2) + 256 * (n // 2))
                elif phase in column:
                    w, c0 = column[phase]
                    wide(s, s, w, c0 + 256 * n)
                elif phase == "lat" and n < 2:
                    wide(s, s, "w_in_2", gq + 256 * n)
                elif phase == "lat":
                    free(s)
                    for m, c, width in ((0, gq + 512, 128), (128, gq + 640, ROPE), (192, gq + 640, ROPE)):
                        sp.dma_start(slot(s, KT)[:, :, m:m + width], rows["w_in_2"][:, :, c:c + width])\
                            .then_inc(slot_loaded[s % SLOTS], 16)
                elif phase == "uq":
                    free(s)
                    for k in range(3):
                        dst = slot(s, 3)[:, k, :]
                        if n < 2:
                            dst, src = dst.rearrange("p (h c) -> p h c", h=4), uq[:, k, 4 * n:4 * n + 4, 0:NOPE]
                        else:
                            dst, src = dst.rearrange("p (h c) -> p h c", h=NH), uq[:, k, :, NOPE:NOPE + ROPE]
                        sp.dma_start(dst, src).then_inc(slot_loaded[s % SLOTS], 16)
                else:
                    free(s)
                    for k in range(2):
                        dst = slot(s, 2)[:, k, :].rearrange("p (h c) -> p h c", h=NH)
                        sp.dma_start(dst, ukv[:, k, :, n * P:(n + 1) * P]).then_inc(slot_loaded[s % SLOTS], 16)
            s0 = FIRST["mlp_in"]
            wide(s0, s0, "w_mlp_in_2", 0)
            with sp.Fori(0, (MLP_STEPS - 1) // SLOTS) as i:
                for r in range(SLOTS):
                    s = s0 + 1 + 2 * r
                    wide(s + i * 6, s, "w_mlp_in_2", i * 768 + 256 * (r + 1))
                    deep(s + 1 + i * 6, s + 1, "w_mlp_out_2", i * 3 + r)
            deep(N_SLABS - 1, N_SLABS - 1, "w_mlp_out_2", MLP_STEPS - 1)
            for n, (half, tk) in enumerate(OUT_ORDER):
                sp.wait_ge(*at("out_ready", n + 1))
                sp.dma_start(out_rows[:, tk, half * 512:(half + 1) * 512], upad_out[:, tk, half * 512:(half + 1) * 512])\
                    .then_inc(S("stored"), 16)
            sp.wait_ge(*at("stored", 64))

        @block.gpsimd
        def _(pool):
            ps_ = Steps(pool, s_pstep)
            pool.memset(zero[:, :], 0.0).then_inc(S("zero"), 1)
            pool.memset(qkvp[:, :, 0:3], 0.0).then_inc(S("pads"), 1)
            pool.memset(mpad[:, :, 0:2], 0.0).then_inc(S("pads"), 1)
            def modulation(step):
                flat = ada_raw[:, :, :].rearrange("p k m -> p (k m)")
                pool.wait_ge(*at("ada_loaded", step * 16 + 16))
                pool.tensor_tensor(ada_raw[:, :, :], ada_raw[:, :, :], c_act[:, :].unsqueeze(2).to_broadcast([P, KT, 256]),
                                   ALU.mult).then_inc(S("ada_part"), 1)
                pool.wait_ge(*at("ada_part", step * 3 + 1))
                pool.tensor_tensor(flat[:, 0:1024], flat[:, 0:1024], flat[:, 1024:2048], ALU.add).then_inc(S("ada_part"), 1)
                pool.wait_ge(*at("ada_part", step * 3 + 2))
                pool.tensor_tensor(flat[:, 0:512], flat[:, 0:512], flat[:, 512:1024], ALU.add).then_inc(S("ada_part"), 1)
                pool.wait_ge(*at("ada_part", step * 3 + 3))
                if not isinstance(step, int) or step:
                    pool.wait_ge(*at("ada_taken", step))
                pool.tensor_tensor(ada_sum[:, :], flat[:, 0:256], flat[:, 256:512], ALU.add).then_inc(S("ada_free"), 1)

            def squares(n, ready, dst):
                for b in range(4):
                    pool.wait_ge(*at(ready, b + 1))
                    pool.tensor_tensor(dst[:, 2 * b:2 * b + 2, :], resid[:, 2 * b:2 * b + 2, :], resid[:, 2 * b:2 * b + 2, :],
                                       ALU.mult).then_inc(S(n + "_sq"), 1)

            squares("n1", "x_in", sq)
            pool.dma_start(con[:, N_CONST_FIRST:], a["table"][:, N_CONST_FIRST:]).then_inc(S("con_rest"), 16)
            pool.wait_ge(*at("c_act", 1))
            modulation(0)
            with pool.Fori(0, FF_STEPS - 2) as i:
                modulation(i + 1)
            squares("n2", "ffn1_resid", sq)
            for n in range(ADA_MIX - 1):
                modulation(FF_STEPS - 1 + n)
            pool.wait_ge(*at("mix_evac", 13))
            body = mpad[:, :, 2:2 + T]
            ps_(pool.tensor_tensor(body, body, cc[:, :, :], ALU.mult))
            ps_.sync()
            for k in range(3):
                for t in range(4):
                    dst = cc if k == 0 else g_row
                    ins = pool.tensor_scalar(dst[:, t, :], mpad[:, t, k:k + T], col("conv_short_w", 4 * k + t), 0.0, ALU.mult,
                                             ALU.add)
                ps_(ins)
                ps_.sync()
                if k:
                    ps_(pool.tensor_tensor(cc[:, :, :], cc[:, :, :], g_row[:, :, :], ALU.add))
                    ps_.sync()
            pool.tensor_tensor(cc[:, :, :], cc[:, :, :], cb[:, :, :], ALU.mult).then_inc(S("short_y"), 1)
            pool.wait_ge(*at("short_y", 1))
            pool.tensor_tensor(sq[:, 4:8, :], cc[:, :, :], cc[:, :, :], ALU.mult).then_inc(S("short_sq"), 1)
            modulation(FF_STEPS + 2)
            squares("n3", "mix_resid", sq)
            with pool.Fori(0, FF_STEPS - 1) as i:
                modulation(i + (FF_STEPS - 1 + ADA_MIX))
            squares("f", "ffn2_resid", kn)
            pool.wait_ge(*at("ffn2_resid", 4))
            pool.memset(upad[:, :, 0:PAD], 0.0).then_inc(S("upads"), 1)
            pool.dma_start(cosines.bitcast(I32), a["positions_2"].to_broadcast([P, T])).then_inc(S("pos_loaded"), 16)
            c1, c2, c3 = two_pi()
            magic = 12582912.0
            lim = 3.1415925
            ang, turns, part = tap_mem[:, 0, :], tap_mem[:, 1, :], w_v[:, 0:T]

            def step(ins):
                ps_(ins)
                ps_.sync()

            pool.wait_ge(*at("pos_loaded", 16))
            pool.wait_ge(*at("ada_taken", ADA_STEPS))
            step(pool.tensor_copy(ang, cosines.bitcast(I32)))
            step(pool.tensor_scalar(ang, ang, const("inv_freq", 1), 0.0, ALU.mult, ALU.add))
            for dst, quarter, shift in ((sines, 0.0, 0.0), (cosines, 0.25, float(np.float32(np.pi / 2)))):
                step(pool.tensor_scalar(turns, ang, float(np.float32(1 / (2 * np.pi))), quarter, ALU.mult, ALU.add))
                step(pool.tensor_scalar(turns, turns, magic, 0.0, ALU.add, ALU.add))
                step(pool.tensor_scalar(turns, turns, -magic, 0.0, ALU.add, ALU.add))
                src = ang
                for c in (c1, c2, c3):
                    step(pool.tensor_scalar(part, turns, -c, 0.0, ALU.mult, ALU.add))
                    step(pool.tensor_tensor(dst, part, src, ALU.add))
                    src = dst
                step(pool.tensor_scalar(dst, dst, shift, lim, ALU.add, ALU.min))
                ins = pool.tensor_scalar(dst, dst, -lim, 0.0, ALU.max, ALU.add)
                if quarter:
                    ins.then_inc(S("angles"), 1)
                else:
                    step(ins)
            pool.wait_ge(*at("angles", 1))
            for group in POOL_TILES:
                pool.wait_ge(*at("glu", group[-1] // 2 + 1))
                sums = conv[:, group[0]:group[-1] + 1, :]
                for k in range(TAPS):
                    for n, t in enumerate(group):
                        if k == 0:
                            ins = pool.tensor_scalar(conv[:, t, :], upad[:, t, 0:T], tap(0, t), col("conv_b_2", t), ALU.mult,
                                                     ALU.add)
                        else:
                            ins = pool.tensor_scalar(tap_mem[:, n, :], upad[:, t, k:k + T], tap(k, t), 0.0, ALU.mult, ALU.add)
                    ps_(ins)
                    ps_.sync()
                    if k:
                        ins = pool.tensor_tensor(sums, sums, tap_mem[:, :, :], ALU.add)
                        if k < TAPS - 1:
                            ps_(ins)
                            ps_.sync()
                        else:
                            ins.then_inc(S("long_conv"), 1)

        @block.scalar
        def _(act):
            st = Steps(act, s_astep)

            def cast(s):
                act.wait_ge(slot_loaded[s % SLOTS], landed(s))
                if s >= SLOTS:
                    act.wait_ge(taken, s - SLOTS + 1)
                n = slab_floats(s)
                act.activation(wh[:, s % SLOTS, 0:n], raw[:, s % SLOTS, 0:n], ACT.Copy).then_inc(high_done, 1)

            def cast_in_loop(s, i, per, count):
                act.wait_ge(slot_loaded[s % SLOTS], i * (16 * count) + landed(s))
                act.wait_ge(taken, i * per + (s - SLOTS + 1))
                act.activation(wh[:, s % SLOTS, :], raw[:, s % SLOTS, :], ACT.Copy).then_inc(high_done, 1)

            def norm_in(n, ready, gain):
                for t in range(KT):
                    if t % 2 == 0:
                        act.wait_ge(*at(ready, t // 2 + 1))
                    act.activation(xh[:, t, :], resid[:, t, :], ACT.Copy, scale=col(gain, t)).then_inc(S(n + "_xh"), 1)

            def root(n, src, dst, width):
                act.wait_ge(*at(n + "_stat", 1))
                act.activation(dst, src, ACT.Sqrt, scale=1.0 / width, bias=eps[0:dst.shape[0], :]).then_inc(S(n + "_std"), 1)

            def ffn(name):
                s0 = FIRST[name + "_gate"]

                def silu(count):
                    act.wait_ge(*at(name + "_gate", count))
                    act.activation(hid[:, 1, :], hid[:, 0, :], ACT.Silu).then_inc(S(name + "_silu"), 1)

                def round_hidden(count):
                    act.wait_ge(*at(name + "_h", count))
                    act.activation(fh[:, :, :], pair(hid[:, 3, :]), ACT.Copy).then_inc(S(name + "_fh"), 1)

                cast(s0 + 3)
                silu(1)
                if name == "ffn1":
                    g, r = VECS["c_2"]
                    act.wait_ge(*at("vec", 2))
                    act.activation(c_act[:, :], vec[:, g, r:r + KT], ACT.Silu).then_inc(S("c_act"), 1)
                cast(s0 + 4)
                round_hidden(1)
                with act.Fori(0, FF_STEPS - 1) as i:
                    s = s0 + 2
                    cast_in_loop(s + 3, i, 3, 1)
                    silu(i + 2)
                    cast_in_loop(s + 4, i, 3, 1)
                    act.wait_ge(taken, i * 3 + (s + 3))
                    round_hidden(i + 2)
                    cast_in_loop(s + 5, i, 3, 1)
                if name == "ffn2":
                    cast(s0 + 3 * FF_STEPS + 2)

            act.dma_start(con[:, 0:N_CONST_FIRST], a["table"][:, 0:N_CONST_FIRST]).then_inc(S("con"), 16)
            n_vec = 0
            for name, (g, r) in VECS.items():
                src = a[name]
                if name == "conv_short_w" or name == "gdn_conv_w":
                    src = src[0].rearrange("k (t p) -> (k t) p", p=P)
                elif name == "final_norm":
                    src = src.rearrange("(t p) -> t p", p=P)
                elif name == "gdn_out_norm":
                    src = src
                else:
                    src = src.rearrange("a (t p) -> (a t) p", p=P)
                act.dma_start(stage[r:r + src.shape[0], g, :], src).then_inc(S(f"vec{g}_loaded"), 16)
                n_vec += 1
            taps = a["conv_w_2"][0].rearrange("k (t p) -> (k t) p", p=P)
            for g in range(2):
                act.dma_start(stage[0:124, 2 + g, :], taps[g * 124:(g + 1) * 124, :]).then_inc(S("vec1_loaded"), 16)
                n_vec += 1
            assert n_vec == N_VEC
            act.dma_start(a_log[:, 0:1], a["gdn_A_log"].rearrange("a h -> h a")).then_inc(S("small_loaded"), 16)
            act.dma_start(a_log[:, 1:2], a["gdn_dt_bias"].rearrange("a h -> h a")).then_inc(S("small_loaded"), 16)
            act.wait_ge(*at("vec", 1))
            norm_in("n1", "x_in", "ffn1_norm")
            for s in range(SLOTS):
                cast(s)
            root("n1", ps[6][:, 0:T], std[:, :], D)
            ffn("ffn1")
            norm_in("n2", "ffn1_resid", "mix_norm")
            cast(FIRST["mix"] + 2)
            root("n2", ps[6][:, 0:T], std[:, :], D)
            s0 = FIRST["mix"]

            def silu_qkv(n):
                act.wait_ge(*at("conv4_done", 2 * (n + 1)))
                act.activation(qkv[:, 2 * n:2 * n + 2, :], qkv[:, 2 * n:2 * n + 2, :], ACT.Silu).then_inc(S("qkv_silu"), 1)
                if n < 4:
                    act.wait_ge(*at("qkv_silu", n + 1))
                    if n == 0:
                        act.wait_ge(*at("n2_stat", 1))
                    act.activation(sq[:, 2 * n:2 * n + 2, :], qkv[:, 2 * n:2 * n + 2, :], ACT.Square).then_inc(S("qk_sq"), 1)

            for n in range(6):
                cast(s0 + n + 3)
                if n:
                    silu_qkv(n - 1)
            cast(s0 + 6 + 3)
            silu_qkv(5)
            root("qk", ps[0][0:8, 0:T], small[0:8, 6, :], 1)
            act.wait_ge(*at("small_loaded", 32))
            act.wait_ge(*at("ab_abs", 1))
            st(act.activation(a_log[:, 0:1], a_log[:, 0:1], ACT.Exp))
            act.activation(small[0:4, 2, :], small[0:4, 1, :], ACT.Exp).then_inc(S("ab_exp"), 1)
            act.wait_ge(*at("ab_one", 1))
            act.activation(small[0:4, 4, :], small[0:4, 3, :], ACT.Ln).then_inc(S("ab_ln"), 1)
            act.activation(beta_row[0:4, :], small[0:4, 5, :], ACT.Sigmoid).then_inc(S("beta"), 1)
            cast(s0 + 7 + 3)
            cast(s0 + 8 + 3)
            for n in range(2):
                act.wait_ge(*at("g_spread", n + 1))
                act.activation(g_row[:, 2 * n:2 * n + 2, :], pair(ps[n][:, :]), ACT.Copy).then_inc(S("g_row"), 1)
            cast(s0 + 9 + 3)
            act.wait_ge(*at("dt_diff", 1))
            act.activation(dt_mat, dt_mat, ACT.Exp).then_inc(S("dt_exp"), 1)
            act.activation(cols[:, 16:20], cols[:, 4:8], ACT.Exp).then_inc(S("g_exp"), 1)
            act.activation(cols[:, 20:24], cols[:, 24:28], ACT.Exp).then_inc(S("g_exp"), 1)
            act.activation(exp_g, g_row[:, :, CH:2 * CH], ACT.Exp).then_inc(S("g_exp"), 1)
            cast(s0 + 10 + 3)
            act.wait_ge(*at("v_turned", 2))
            for u in range(UNITS):
                act.activation(v_beta[:, u * P:(u + 1) * P], ps[2 + u // 4][:, (u % 4) * P:(u % 4 + 1) * P], ACT.Copy,
                               scale=cols[:, 8 + u:9 + u]).then_inc(S("v_nat"), 1)
            cast(s0 + 11 + 3)
            act.wait_ge(*at("cols_ready", 1))
            act.wait_ge(*at("at_done", 1))
            act.wait_ge(*at("k_turned", 2))
            for u in range(UNITS):
                dst = k_dec[:, u * P:(u + 1) * P] if u < 4 else k_be[:, (u - 4) * P:(u - 3) * P]
                scale = cols[:, 20 + u:21 + u] if u < 4 else cols[:, 28 + u - 4:29 + u - 4]
                act.activation(dst, ps[2 + u // 4][:, (u % 4) * P:(u % 4 + 1) * P], ACT.Copy, scale=scale)\
                    .then_inc(S("k_nat"), 1)
            cast(s0 + 12 + 3)
            with act.Fori(0, LEVELS) as i:
                act.wait_ge(*at("inv_x", i * 2 + 2))
                act.activation(x_mat[:, 512:1024], ps[1][:, :], ACT.Copy).then_inc(S("inv_xa"), 1)
            act.wait_ge(*at("w_mm", 1))
            act.activation(x_mat[:, 0:512], ps[1][:, :], ACT.Copy).then_inc(S("w_t"), 1)
            root("short", ps[6][0:8, 0:T], small[0:8, 6, :], 64)
            act.wait_ge(*at("s_mm", 1))
            act.activation(state, ps[2][:, :], ACT.Copy).then_inc(S("state"), 1)
            act.wait_ge(*at("o_mm", 1))
            act.activation(o_t[:, :, 0:CH], tiles(ps[3][:, :], 4), ACT.Copy).then_inc(S("o_t"), 1)
            cast(s0 + 13 + 3)
            act.wait_ge(*at("o_mm", 2))
            act.activation(o_t[:, :, CH:2 * CH], tiles(ps[2][:, :], 4), ACT.Copy).then_inc(S("o_t"), 1)
            act.wait_ge(*at("o_t", 2))
            act.activation(sq[:, 0:4, :], o_t[:, :, :], ACT.Square).then_inc(S("o_sq"), 1)
            cast(s0 + 14 + 3)
            root("o", ps[3][0:8, 0:T], small[0:8, 6, :], DH)
            for n in range(2):
                act.wait_ge(*at("mix_evac", 14 + n))
                act.activation(gz[:, 2 * n:2 * n + 2, :], gz[:, 2 * n:2 * n + 2, :], ACT.Silu).then_inc(S("gz_silu"), 1)
            for n in range(2):
                act.wait_ge(*at("short_out", n + 1))
                act.wait_ge(taken, FIRST["mix_out"])
                act.activation(xh[:, 2 * n:2 * n + 2, :], cb[:, 2 * n:2 * n + 2, :], ACT.Copy).then_inc(S("mo_xh"), 1)
            for n in range(2):
                act.wait_ge(*at("gdn_out", n + 1))
                act.activation(xh[:, 4 + 2 * n:6 + 2 * n, :], o_t[:, 2 * n:2 * n + 2, :], ACT.Copy).then_inc(S("mo_xh"), 1)
            for n in range(4):
                cast(FIRST["mix_out"] + n + 3)

            norm_in("n3", "mix_resid", "ffn2_norm")
            root("n3", ps[6][:, 0:T], std[:, :], D)
            ffn("ffn2")

            for t in range(KT):
                act.wait_ge(*at("ffn2_resid", t // 2 + 1))
                act.activation(qn[:, t, :], resid[:, t, :], ACT.Square, scale=col("final_norm", t)).then_inc(S("fg_sq"), 1)
            root("f", ps[6][:, 0:T], std[:, :], D)
            act.wait_ge(*at("m2", 1))
            act.activation(kr, kr_raw, ACT.Sqrt, scale=1.0 / D, bias=eps).then_inc(S("g_std"), 1)
            for t in range(KT):
                act.wait_ge(*at("h_f", t + 1))
                act.activation(xh[:, t, :], kn[:, t, :], ACT.Identity, bias=ada[:, t:t + 1]).then_inc(S("h_xh"), 1)
            for n in range(4):
                s = FIRST["glu"] + 2 * n
                cast(s + 3)
                act.wait_ge(taken, s + 2)
                if n:
                    act.wait_ge(*at("glu", n))
                act.activation(hid[:, 0, :], ps[5 + 2 * (n % 2)][:, :], ACT.Sigmoid).then_inc(S("glu_sig"), 1)
                cast(s + 4)
            act.wait_ge(*at("angles", 1))
            act.activation(sines, sines, ACT.Sin).then_inc(S("rope_tables"), 1)
            act.activation(cosines, cosines, ACT.Sin).then_inc(S("rope_tables"), 1)
            s = FIRST["lat"]
            for n in range(3):
                cast(s + n + 3)
                act.wait_ge(taken, s + n + 1)
                bank = ps[4 + n % 2]
                if n < 2:
                    act.activation(lat[:, 2 * n:2 * n + 2, :], pair(bank[:, :]), ACT.Copy).then_inc(S("lat"), 1)
                else:
                    act.activation(lat[:, 4, :], bank[:, 0:T], ACT.Copy).then_inc(S("lat"), 1)
                    act.activation(kr_raw, bank[:, T:2 * T], ACT.Copy).then_inc(S("lat"), 1)
            act.wait_ge(*at("lat", 4))
            act.activation(lat_sq, lat[:, :, :], ACT.Square).then_inc(S("lat_sq"), 1)

            def gate_logits(phase, n, bank):
                s = SLAB_OF[phase, n]
                cast(s + 3)
                act.wait_ge(taken, s + 1)
                act.activation(gate_mem[phase][:, 2 * n:2 * n + 2, :], pair(bank[:, :]), ACT.Copy).then_inc(S("logits"), 1)

            gate_logits("gate_b", 0, ps[5])
            act.wait_ge(*at("lat_stat", 1))
            act.activation(hid[:, 0, 0:T], ps[6][:, 0:T], ACT.Sqrt, scale=1.0 / Q_LAT, bias=eps).then_inc(S("lat_std"), 1)
            act.activation(hid[:, 0, T:2 * T], ps[6][:, T:2 * T], ACT.Sqrt, scale=1.0 / KV_LAT, bias=eps).then_inc(S("lat_std"), 1)
            for t in range(5):
                act.wait_ge(*at("lat_n", 1))
                gain = col("q_norm_g_2", t) if t < 3 else col("kv_norm_g_2", t - 3)
                act.activation(yh[:, t, :], lat[:, t, :], ACT.Copy, scale=gain).then_inc(S("lat_yh"), 1)
            gate_logits("gate_b", 1, ps[4])
            for n in range(3):
                s = FIRST["uq"] + n
                cast(s + 3)
                act.wait_ge(taken, s + 1)
                dst = qn[:, 4 * n:4 * n + 4, :] if n < 2 else qr_raw[:, :, :]
                for b in range(2):
                    act.activation(dst[:, 2 * b:2 * b + 2, :], pair(ps[2 * n + b][:, :]), ACT.Copy).then_inc(S("q"), 1)
            s = FIRST["ukv"]
            cast(s + 3)
            act.wait_ge(taken, s + 1)
            for b, bank in enumerate(KEY_BANKS):
                act.activation(kn[:, 2 * b:2 * b + 2, :], pair(ps[bank][:, :]), ACT.Copy).then_inc(S("k"), 1)
            cast(s + 4)
            act.wait_ge(taken, s + 2)
            act.wait_ge(*at("lat_yl", 5))
            for b, bank in enumerate(VALUE_BANKS):
                act.activation(v[:, b // 2, (b % 2) * 512:(b % 2 + 1) * 512], ps[bank][:, :], ACT.Copy).then_inc(S("v"), 1)

            def attn_exp(h):
                act.wait_ge(*at("att_max", h + 1))
                if h >= 2:
                    act.wait_ge(*at("att_norm", h - 1))
                for qt in range(2):
                    w = (qt + 1) * P
                    o = qt * P
                    act.activation(prob[h % 2][:, o:o + w], score[h % 2][:, o:o + w], ACT.Exp,
                                   scale=ATT_SCALE, bias=att_col[:, 8 * (h % 2) + 2 + qt:8 * (h % 2) + 3 + qt],
                                   accum_out=att_col[:, 8 * (h % 2) + 4 + qt:8 * (h % 2) + 5 + qt]).then_inc(S("att_exp"), 1)

            def attn_probs(h):
                act.wait_ge(*at("att_turned", h + 1))
                act.activation(prob_t[h % 2], ps[2 + h % 2][:, 0:3 * P], ACT.Copy).then_inc(S("att_pt"), 1)

            def attn_out(h):
                act.wait_ge(*at("att_o", h + 1))
                if h == 0:
                    act.wait_ge(taken, FIRST["ukv"] + 2)
                act.activation(yh[:, h, :], ps[4 + h % 2][:, 0:T], ACT.Copy).then_inc(S("o_yh"), 1)

            attn_exp(0)
            for h in range(NH + 2):
                if h in GATE_AT_HEAD:
                    gate_logits(*GATE_AT_HEAD[h], ps[6 + GATE_AT_HEAD[h][1] % 2])
                if 1 <= h <= NH:
                    attn_probs(h - 1)
                if h >= 2:
                    attn_out(h - 2)
                if h + 1 < NH:
                    attn_exp(h + 1)

            for b in range(4):
                act.wait_ge(*at("ln_cen", b + 1))
                act.activation(ln_squares[:, 2 * b:2 * b + 2, :], conv[:, 2 * b:2 * b + 2, :], ACT.Square).then_inc(S("ln_sq"), 1)
            act.wait_ge(*at("logits", 8))
            act.activation(gate_mem["gate_b"], gate_mem["gate_b"], ACT.Sigmoid).then_inc(S("gates"), 1)
            act.activation(gate_mem["gate_a"], gate_mem["gate_a"], ACT.Sigmoid).then_inc(S("gates"), 1)
            s = FIRST["attn_out"]
            cast(s + 3)
            root("ln", ps[1][:, 0:T], std[:, :], D)
            cast(s + 4)
            for t in range(KT):
                act.wait_ge(*at("ln_n", t // 2 + 1))
                act.activation(conv[:, t, :], conv[:, t, :], ACT.Silu, scale=col("conv_norm_g_2", t),
                               bias=col("conv_norm_b_2", t)).then_inc(S("ln_silu"), 1)
                act.wait_ge(*at("ln_silu", t + 1))
                act.activation(xh[:, t, :], conv[:, t, :], ACT.Copy).then_inc(S("c_xh"), 1)
                if t == 3:
                    cast(s + 5)
            cast(s + 6)
            for n in range(4):
                cast(FIRST["conv_out"] + n + 3)
                act.wait_ge(*at("mixed", n + 1))
                act.activation(yh[:, 2 * n:2 * n + 2, :], kn[:, 2 * n:2 * n + 2, :], ACT.Copy).then_inc(S("w_yh"), 1)
            for n in range(4):
                s = FIRST["w_out"] + n
                act.wait_ge(taken, s + 1)
                act.activation(conv[:, 2 * n:2 * n + 2, :], pair(ps[4 + n % 2][:, :]), ACT.Copy).then_inc(S("y"), 1)
                act.wait_ge(*at("y", n + 1))
                act.activation(v_sq[:, 2 * n:2 * n + 2, :], conv[:, 2 * n:2 * n + 2, :], ACT.Square).then_inc(S("y_sq"), 1)
                if n < 3:
                    cast(s + 3)
            root("y", ps[6][:, 0:T], std[:, :], D)
            for b in range(4):
                act.wait_ge(*at("x3", b + 1))
                act.activation(v_sq[:, 2 * b:2 * b + 2, :], resid[:, 2 * b:2 * b + 2, :], ACT.Square).then_inc(S("x3_sq"), 1)
            root("x3", ps[7][:, 0:T], std[:, :], D)
            cast(FIRST["w_out"] + 3 + 3)
            for t in range(KT):
                act.wait_ge(*at("h2_f", t + 1))
                act.activation(xh[:, t, :], qn[:, t, :], ACT.Identity, bias=ada[:, 24 + t:25 + t]).then_inc(S("h2_xh"), 1)

            s0 = FIRST["mlp_in"]

            def square(count):
                act.wait_ge(*at("mlp_relu", count))
                act.activation(fh[:, :, :], pair(hid[:, 0, :]), ACT.Square).then_inc(S("mlp_fh"), 1)

            cast(s0 + 3)
            square(1)
            with act.Fori(0, (MLP_STEPS - 1) // SLOTS - 1) as i:
                for r in range(SLOTS):
                    s = s0 + 1 + 2 * r
                    cast_in_loop(s + 3, i, 6, 2)
                    act.wait_ge(taken, i * 6 + (s + 2))
                    square(i * 3 + (r + 2))
                    cast_in_loop(s + 4, i, 6, 2)
            for k in range(MLP_STEPS - SLOTS, MLP_STEPS):
                s = s0 + 2 * k - 1
                if s + 3 < N_SLABS:
                    cast(s + 3)
                act.wait_ge(taken, s + 2)
                square(k + 1)
                if s + 4 < N_SLABS:
                    cast(s + 4)
            act.wait_ge(taken, N_SLABS)
            for n in range(4):
                act.activation(v_sq[:, 2 * n:2 * n + 2, :], pair(ps[n][:, :]), ACT.Square).then_inc(S("z_sq"), 1)
            root("z", ps[6][:, 0:T], std[:, :], D)
            for n, (half, tk) in enumerate(OUT_ORDER):
                act.wait_ge(*at("turned", n + 1))
                act.activation(upad_out[:, tk, half * 512:(half + 1) * 512], ps[4 + n % 2 + 2 * (n // 2)][:, :], ACT.Copy)\
                    .then_inc(S("out_ready"), 1)

        @block.vector
        def _(dve):
            st = Steps(dve, s_vstep)

            def sub(s):
                n = slab_floats(s)
                dve.wait_ge(high_done, s + 1)
                dve.tensor_tensor(wl[:, s % SLOTS, 0:n], raw[:, s % SLOTS, 0:n], wh[:, s % SLOTS, 0:n].bitcast(F32),
                                  ALU.subtract).then_inc(low_done, 1)

            def sub_in_loop(s, i, per):
                dve.wait_ge(high_done, i * per + (s + 1))
                dve.tensor_tensor(wl[:, s % SLOTS, :], raw[:, s % SLOTS, :], wh[:, s % SLOTS, :].bitcast(F32),
                                  ALU.subtract).then_inc(low_done, 1)

            def norm_in(n, gain):
                for t in range(KT):
                    dve.wait_ge(*at(n + "_xh", t + 1))
                    dve.scalar_tensor_tensor(xl[:, t, :], resid[:, t, :], col(gain, t), xh[:, t, :].bitcast(F32),
                                             ALU.mult, ALU.subtract).then_inc(S(n + "_xl"), 1)

            def inverse(n, dst, src):
                dve.wait_ge(*at(n + "_std", 1))
                dve.reciprocal(dst, src).then_inc(S(n + "_rstd"), 1)
                dve.wait_ge(*at(n + "_rstd", 1))

            def scaled(dst, bank, r=rstd):
                return dve.tensor_tensor(dst, pair(bank[:, :]), spread(r[:, :], 2), ALU.mult)

            def ffn(name, n):
                s0 = FIRST[name + "_gate"]

                def gate(s, count):
                    dve.wait_ge(taken, s + 1)
                    scaled(pair(hid[:, 0, :]), ps[4]).then_inc(S(name + "_gate"), 1)

                def up(s, count):
                    dve.wait_ge(taken, s + 1)
                    scaled(pair(hid[:, 2, :]), ps[5]).then_inc(S(name + "_up"), 1)

                def hidden(count):
                    dve.wait_ge(*at(name + "_silu", count))
                    dve.wait_ge(*at(name + "_up", count))
                    dve.tensor_tensor(hid[:, 3, :], hid[:, 1, :], hid[:, 2, :], ALU.mult).then_inc(S(name + "_h"), 1)

                def rest(count):
                    dve.wait_ge(*at(name + "_fh", count))
                    dve.tensor_tensor(fl[:, :, :], pair(hid[:, 3, :]), fh[:, :, :].bitcast(F32), ALU.subtract)\
                        .then_inc(S(name + "_fl"), 1)

                inverse(n, rstd[:, :], std[:, :])
                gate(s0, 1)
                sub(s0 + 3)
                up(s0 + 1, 1)
                sub(s0 + 4)
                hidden(1)
                rest(1)
                with dve.Fori(0, FF_STEPS - 1) as i:
                    s = s0 + 2
                    gate(i * 3 + s, i + 2)
                    sub_in_loop(s + 3, i, 3)
                    up(i * 3 + (s + 1), i + 2)
                    sub_in_loop(s + 4, i, 3)
                    hidden(i + 2)
                    rest(i + 2)
                    sub_in_loop(s + 5, i, 3)
                s = s0 + 3 * FF_STEPS - 1
                dve.wait_ge(taken, s + 1)
                for b in range(4):
                    dve.scalar_tensor_tensor(resid[:, 2 * b:2 * b + 2, :], pair(ps[b][:, :]), 0.5,
                                             resid[:, 2 * b:2 * b + 2, :], ALU.mult, ALU.add).then_inc(S(name + "_resid"), 1)
                if name == "ffn2":
                    sub(s + 3)

            dve.wait_ge(*at("x_turned", 4))
            for b in range(4):
                dve.tensor_copy(resid[:, 2 * b:2 * b + 2, :], pair(ps[4 + b][:, :])).then_inc(S("x_in"), 1)
            dve.wait_ge(*at("vec_turned", 1))
            dve.tensor_copy(vec[:, 0, 0:STAGE_ROWS[0]], ps[0][:, 0:STAGE_ROWS[0]]).then_inc(S("vec"), 1)
            dve.wait_ge(*at("vec", 1))
            dve.wait_ge(*at("x_in", 4))
            norm_in("n1", "ffn1_norm")
            for s in range(SLOTS):
                sub(s)
            dve.wait_ge(*at("vec_turned", 2))
            for g in range(1, 4):
                ins = dve.tensor_copy(vec[:, g, 0:STAGE_ROWS[g]], ps[1][:, g * P:g * P + STAGE_ROWS[g]])
            ins.then_inc(S("vec"), 1)
            ffn("ffn1", "n1")

            dve.wait_ge(*at("ffn1_resid", 4))
            norm_in("n2", "mix_norm")
            sub(FIRST["mix"] + 2)
            inverse("n2", rstd[:, :], std[:, :])
            s0 = FIRST["mix"]
            dve.wait_ge(*at("pads", 2))
            dve.wait_ge(*at("con_rest", 16))

            def evac(n, dst):
                dve.wait_ge(taken, s0 + n + 1)
                scaled(dst, ps[4 + n % 2]).then_inc(S("mix_evac"), 1)
                dve.wait_ge(*at("mix_evac", n + 1))

            for n in range(6):
                evac(n, qkvp[:, 2 * n:2 * n + 2, 3:3 + T])
                for k in range(4):
                    for t in (2 * n, 2 * n + 1):
                        if k == 0:
                            ins = dve.tensor_scalar(qkv[:, t, :], qkvp[:, t, 0:T], col("gdn_conv_w", t), None, ALU.mult)
                        else:
                            ins = dve.scalar_tensor_tensor(qkv[:, t, :], qkvp[:, t, k:k + T], col("gdn_conv_w", 12 * k + t),
                                                           qkv[:, t, :], ALU.mult, ALU.add)
                        if k == 3:
                            ins.then_inc(S("conv4_done"), 1)
                    if k < 3:
                        st(ins)
                        st.sync()
                sub(s0 + n + 3)
            dve.wait_ge(taken, s0 + MIX_AB + 1)
            dve.tensor_tensor(small[0:4, 5, :], ps[4][0:4, 0:T], rstd[0:4, :], ALU.mult)
            st(dve.tensor_tensor(small[0:4, 0, :], ps[4][32:36, 0:T], rstd[32:36, :], ALU.mult))
            st.sync()
            dve.wait_ge(*at("small_loaded", 32))
            dve.tensor_scalar(small[0:4, 0, :], small[0:4, 0, :], a_log[:, 1:2], None, ALU.add).then_inc(S("mix_evac"), 1)
            dve.wait_ge(*at("mix_evac", MIX_AB + 1))
            dve.scalar_tensor_tensor(small[0:4, 1, :], small[0:4, 0, :], -1.0, small[0:4, 0, :], ALU.mult, ALU.min)\
                .then_inc(S("ab_abs"), 1)
            inverse("qk", small[0:8, 7, :], small[0:8, 6, :])
            dve.tensor_scalar(small[0:8, 7, :], small[0:8, 7, :], const("qk_scale", 1, 8), None, ALU.mult).then_inc(S("qk_row"), 1)
            sub(s0 + MIX_AB + 3)
            dve.wait_ge(*at("ab_exp", 1))
            dve.tensor_scalar(small[0:4, 3, :], small[0:4, 2, :], 1.0, None, ALU.add).then_inc(S("ab_one"), 1)
            evac(7, cc[:, 0:2, :])
            dve.wait_ge(*at("ab_ln", 1))
            st(dve.tensor_scalar(small[0:4, 3, :], small[0:4, 3, :], 1.0, None, ALU.subtract))
            st.sync()
            st(dve.tensor_scalar(small[0:4, 1, :], small[0:4, 3, :], 0.0, None, ALU.is_equal))
            st.sync()
            dve.tensor_tensor(small[0:4, 4, :], small[0:4, 4, :], small[0:4, 1, :], ALU.add)
            st(dve.tensor_tensor(small[0:4, 3, :], small[0:4, 3, :], small[0:4, 1, :], ALU.add))
            st.sync()
            st(dve.reciprocal(small[0:4, 1, :], small[0:4, 3, :]))
            st.sync()
            st(dve.tensor_tensor(small[0:4, 4, :], small[0:4, 4, :], small[0:4, 1, :], ALU.mult))
            st.sync()
            st(dve.tensor_tensor(small[0:4, 4, :], small[0:4, 4, :], small[0:4, 2, :], ALU.mult))
            st.sync()
            st(dve.scalar_tensor_tensor(small[0:4, 4, :], small[0:4, 0, :], 0.0, small[0:4, 4, :], ALU.max, ALU.add))
            st.sync()
            st(dve.tensor_scalar(small[0:4, 4, :], small[0:4, 4, :], a_log[:, 0:1], -1.0, ALU.mult, ALU.mult))
            st.sync()
            dve.tensor_tensor_scan(g_cum[0:4, :], const("restart", T, 4), small[0:4, 4, :], 0.0, ALU.mult, ALU.add)\
                .then_inc(S("g_cum"), 1)
            sub(s0 + 7 + 3)
            dve.wait_ge(*at("qk_spread", 4))
            for b in range(4):
                dve.tensor_tensor(qkv[:, 2 * b:2 * b + 2, :], qkv[:, 2 * b:2 * b + 2, :], pair(ps[b][:, :]), ALU.mult)\
                    .then_inc(S("qk_n"), 1)
            evac(8, cc[:, 2:4, :])
            sub(s0 + 8 + 3)
            for b in range(2):
                dve.wait_ge(*at("b_spread", b + 1))
                dve.tensor_tensor(kb[:, 2 * b:2 * b + 2, :], k_n[:, 2 * b:2 * b + 2, :], pair(ps[2 + b][:, :]), ALU.mult)\
                    .then_inc(S("kb"), 1)
            evac(9, mpad[:, 0:2, 2:2 + T])
            dve.wait_ge(*at("col_turned", 4))
            dve.wait_ge(*at("g_row", 2))
            st(dve.tensor_copy(cols[:, 0:16], ps[6][:, 0:16]))
            st.sync()
            for u in range(UNITS):
                c, h = u // HEADS, u % HEADS
                ins = dve.tensor_scalar(dt_mat[:, u * P:(u + 1) * P], g_row[:, h, c * CH:(c + 1) * CH], cols[:, u:u + 1], 0.0,
                                        ALU.subtract, ALU.min)
            st(ins)
            dve.tensor_tensor(cols[:, 24:28], g_row[:, :, CH - 1], cols[:, 0:4], ALU.subtract).then_inc(S("dt_diff"), 1)
            sub(s0 + 9 + 3)
            evac(10, mpad[:, 2:4, 2:2 + T])
            dve.wait_ge(*at("g_exp", 3))
            dve.wait_ge(*at("dt_exp", 1))
            dve.scalar_tensor_tensor(cols[:, 28:32], cols[:, 12:16], -1.0, cols[:, 16:20], ALU.mult, ALU.mult)\
                .then_inc(S("cols_ready"), 1)
            for b in range(2):
                dve.wait_ge(*at("lt_mm", b + 1))
                dve.tensor_tensor(lt_mat[:, b * 512:(b + 1) * 512], ps[b][:, :], dt_mat[:, b * 512:(b + 1) * 512], ALU.mult)\
                    .then_inc(S("lt"), 1)
            dve.wait_ge(*at("lt", 2))
            st(dve.tensor_tensor(tiles(dt_mat, UNITS), tiles(dt_mat, UNITS), spread(const("upper", P), UNITS), ALU.mult))
            sub(s0 + 10 + 3)
            st.sync()
            for b in range(2):
                dve.wait_ge(*at("at_mm", b + 1))
                ins = dve.tensor_tensor(at_mat[:, b * 512:(b + 1) * 512], ps[b][:, :], dt_mat[:, b * 512:(b + 1) * 512], ALU.mult)
            ins.then_inc(S("at_done"), 1)
            dve.wait_ge(*at("at_done", 1))
            st(dve.tensor_tensor(q_n[:, :, CH:2 * CH], q_n[:, :, CH:2 * CH], exp_g, ALU.mult))
            st.sync()
            evac(11, cb[:, 0:2, :])
            sub(s0 + 11 + 3)
            for b in range(2):
                for m in (t_mat, tt_mat):
                    dve.tensor_copy(tiles(m[:, b * 512:(b + 1) * 512], 4), spread(ident, 4)).then_inc(S("inv_t"), 1)

            def between_halves(mask):
                dve.tensor_tensor(tiles(b_mat, UNITS), tiles(lt_mat, UNITS), spread(mask, UNITS), ALU.mult)\
                    .then_inc(S("inv_b"), 1)

            def level(i, last=False):
                dve.wait_ge(*at("inv_x", i * 2 + 1))
                dve.tensor_copy(x_mat[:, 0:512], ps[0][:, :]).then_inc(S("inv_xv"), 1)
                if not last:
                    dve.wait_ge(*at("inv_x", i * 2 + 2))
                    between_halves(con[:, bass.ds(i * P + (C["levels"] + P), P)])
                dve.wait_ge(*at("inv_t", i * 4 + 4))
                for b in range(2):
                    for n, m in enumerate((t_mat, tt_mat)):
                        dve.wait_ge(*at("inv_y", i * 4 + (2 * b + n + 1)))
                        dve.tensor_tensor(m[:, b * 512:(b + 1) * 512], m[:, b * 512:(b + 1) * 512], ps[2 + b + 2 * n][:, :],
                                          ALU.subtract).then_inc(S("inv_t"), 1)

            between_halves(con[:, C["levels"]:C["levels"] + P])
            evac(12, cb[:, 2:4, :])
            sub(s0 + 12 + 3)
            with dve.Fori(0, LEVELS - 1) as i:
                level(i)
            level(LEVELS - 1, last=True)
            dve.wait_ge(*at("v_mm", 1))
            dve.tensor_copy(v_new[:, 0:512], ps[0][:, :]).then_inc(S("v_new"), 1)
            inverse("short", small[0:8, 7, :], small[0:8, 6, :])
            evac(13, gz[:, 0:2, :])
            dve.wait_ge(*at("v_mm", 2))
            dve.tensor_copy(v_new[:, 512:1024], ps[1][:, :]).then_inc(S("v_new"), 1)
            sub(s0 + 13 + 3)
            for b in range(2):
                dve.wait_ge(*at("short_spread", b + 1))
                bank = ps[(6, 0)[b]]
                for t in (2 * b, 2 * b + 1):
                    ins = dve.scalar_tensor_tensor(cb[:, t, :], cc[:, t, :], col("conv_out_norm", t),
                                                   bank[:, (t % 2) * T:(t % 2 + 1) * T], ALU.mult, ALU.mult)
                ins.then_inc(S("short_out"), 1)
            evac(14, gz[:, 2:4, :])
            sub(s0 + 14 + 3)
            for b in range(2):
                dve.wait_ge(*at("mo_xh", b + 1))
                dve.tensor_tensor(xl[:, 2 * b:2 * b + 2, :], cb[:, 2 * b:2 * b + 2, :], xh[:, 2 * b:2 * b + 2, :].bitcast(F32),
                                  ALU.subtract).then_inc(S("mo_xl"), 1)
            inverse("o", small[0:8, 7, :], small[0:8, 6, :])
            dve.wait_ge(*at("gz_silu", 2))
            for b in range(2):
                dve.wait_ge(*at("o_spread", b + 1))
                st(dve.scalar_tensor_tensor(o_t[:, 2 * b:2 * b + 2, :], o_t[:, 2 * b:2 * b + 2, :], col("gdn_out_norm", 0),
                                            pair(ps[b][:, :]), ALU.mult, ALU.mult))
                st.sync()
                dve.tensor_tensor(o_t[:, 2 * b:2 * b + 2, :], o_t[:, 2 * b:2 * b + 2, :], gz[:, 2 * b:2 * b + 2, :], ALU.mult)\
                    .then_inc(S("gdn_out"), 1)
            for b in range(2):
                dve.wait_ge(*at("mo_xh", b + 3))
                dve.tensor_tensor(xl[:, 4 + 2 * b:6 + 2 * b, :], o_t[:, 2 * b:2 * b + 2, :],
                                  xh[:, 4 + 2 * b:6 + 2 * b, :].bitcast(F32), ALU.subtract).then_inc(S("mo_xl"), 1)
            for n in range(4):
                s = FIRST["mix_out"] + n
                dve.wait_ge(taken, s + 1)
                dve.tensor_tensor(resid[:, 2 * n:2 * n + 2, :], pair(ps[4 + n % 2][:, :]), resid[:, 2 * n:2 * n + 2, :],
                                  ALU.add).then_inc(S("mix_resid"), 1)
                sub(s + 3)
            dve.wait_ge(*at("mix_resid", 4))
            norm_in("n3", "ffn2_norm")
            ffn("ffn2", "n3")

            dve.wait_ge(*at("ffn2_resid", 4))
            for t in range(KT):
                dve.wait_ge(*at("ffn2_resid", t // 2 + 1))
                dve.wait_ge(*at("fg_sq", t + 1))
                if t % 2 == 0:
                    dve.wait_ge(*at("f_sq", t // 2 + 1))
                dve.tensor_scalar(resid[:, t, :], resid[:, t, :], col("final_norm", t), None, ALU.mult).then_inc(S("x2_scaled"), 1)
            dve.wait_ge(*at("ada_taken", ADA_STEPS))
            g, r = VECS["b_ada_2"]
            st(dve.tensor_tensor(ada[:, :], ps[7][:, 0:ADA_TILES], vec[:, g, r:r + ADA_TILES], ALU.add))
            st.sync()

            def vecs(name):
                g, r = VECS[name]
                return vec[:, g, r:r + KT]

            dve.scalar_tensor_tensor(mods[:, 0, :], ada[:, 8:16], 1.0, vecs("g_pre_mix_2"), ALU.add, ALU.mult)
            dve.tensor_tensor(mods[:, 1, :], ada[:, 16:24], vecs("g_post_mix_2"), ALU.mult)
            dve.scalar_tensor_tensor(mods[:, 2, :], ada[:, 32:40], 1.0, vecs("g_pre_mlp_2"), ALU.add, ALU.mult)
            st(dve.tensor_tensor(mods[:, 3, :], ada[:, 40:48], vecs("g_post_mlp_2"), ALU.mult))
            st.sync()
            inverse("f", rstd[:, :], std[:, :])
            dve.wait_ge(*at("f_stat", 2))
            st(dve.tensor_tensor(kr_raw, ps[5][:, 0:T], rstd[:, :], ALU.mult))
            st.sync()
            dve.tensor_tensor(kr_raw, kr_raw, rstd[:, :], ALU.mult).then_inc(S("m2"), 1)
            inverse("g", hid[:, 0, 0:T], kr)
            st(dve.tensor_tensor(hid[:, 0, 0:T], hid[:, 0, 0:T], rstd[:, :], ALU.mult))
            st.sync()
            dve.wait_ge(*at("x2_scaled", KT))
            for n in range(KT + 2):
                if n < KT:
                    dve.scalar_tensor_tensor(kn[:, n, :], resid[:, n, :], mods[:, 0, n:n + 1], hid[:, 0, 0:T], ALU.mult,
                                             ALU.mult).then_inc(S("h_f"), 1)
                t = n - 2
                if t < 0:
                    continue
                dve.wait_ge(*at("h_xh", t + 1))
                dve.scalar_tensor_tensor(xl[:, t, :], kn[:, t, :], ada[:, t:t + 1], xh[:, t, :].bitcast(F32), ALU.add,
                                         ALU.subtract).then_inc(S("h_xl"), 1)
            st(dve.tensor_tensor(resid[:, :, :], resid[:, :, :], spread(rstd[:, :], KT), ALU.mult))
            dve.wait_ge(*at("upads", 1))
            taps_left = [(group, k) for group in DVE_TILES for k in range(TAPS)]

            def convolve(n):
                for _ in range(min(n, len(taps_left))):
                    group, k = taps_left.pop(0)
                    for t in group:
                        if k == 0:
                            ins = dve.tensor_scalar(conv[:, t, :], upad[:, t, 0:T], tap(0, t), col("conv_b_2", t),
                                                    ALU.mult, ALU.add)
                        else:
                            ins = dve.scalar_tensor_tensor(conv[:, t, :], upad[:, t, k:k + T], tap(k, t), conv[:, t, :],
                                                           ALU.mult, ALU.add)
                    st(ins)
                    st.sync()

            for n in range(4):
                s = FIRST["glu"] + 2 * n
                sub(s + 3)
                dve.wait_ge(*at("glu_sig", n + 1))
                dve.tensor_tensor(upad[:, 2 * n:2 * n + 2, PAD:PAD + T], pair(ps[4 + 2 * (n % 2)][:, :]), pair(hid[:, 0, :]),
                                  ALU.mult).then_inc(S("glu"), 1)
                if n >= 2:
                    dve.wait_ge(*at("glu", n))
                    convolve(4)
                sub(s + 4)
            dve.wait_ge(*at("glu", 4))
            for n in range(3):
                sub(FIRST["lat"] + n + 3)
                convolve(3)
            sub(SLAB_OF["gate_b", 0] + 3)
            convolve(3)
            dve.wait_ge(*at("lat_std", 2))
            st(dve.reciprocal(hid[:, 1, :], hid[:, 0, :]))
            st.sync()
            st(dve.tensor_tensor(lat[:, 0:3, :], lat[:, 0:3, :], spread(hid[:, 1, 0:T], 3), ALU.mult))
            dve.tensor_tensor(lat[:, 3:5, :], lat[:, 3:5, :], spread(hid[:, 1, T:2 * T], 2), ALU.mult).then_inc(S("lat_n"), 1)
            dve.wait_ge(*at("lat_n", 1))
            for t in range(5):
                gain = col("q_norm_g_2", t) if t < 3 else col("kv_norm_g_2", t - 3)
                dve.wait_ge(*at("lat_yh", t + 1))
                dve.scalar_tensor_tensor(yl[:, t, :], lat[:, t, :], gain, yh[:, t, :].bitcast(F32), ALU.mult, ALU.subtract)\
                    .then_inc(S("lat_yl"), 1)
            dve.wait_ge(*at("rope_tables", 2))
            dve.wait_ge(*at("kr_swap", 1))
            dve.wait_ge(*at("lat", 4))
            st(dve.tensor_tensor(kr, kr_raw, cosines, ALU.mult))
            st(dve.tensor_tensor(hid[:, 2, 0:T], ps[7][:, 0:T], sines, ALU.mult))
            st.sync()
            dve.tensor_tensor(kr, kr, hid[:, 2, 0:T], ALU.add).then_inc(S("kr"), 1)
            sub(SLAB_OF["gate_b", 1] + 3)
            for n in range(3):
                sub(FIRST["uq"] + n + 3)
                convolve(3)
            sub(FIRST["ukv"] + 3)
            convolve(3)
            dve.wait_ge(*at("q", 6))
            st(dve.tensor_tensor(qr[:, :, :], qr_raw[:, :, :], spread(cosines, 4), ALU.mult))
            for b in range(2):
                dve.wait_ge(*at("q_swap", b + 1))
                st(dve.tensor_tensor(pair(hid[:, 2 + b, :]), pair(ps[2 + b][:, :]), spread(sines, 2), ALU.mult))
            st.sync()
            dve.tensor_tensor(qr[:, :, :], qr[:, :, :], tiles(hid[:, 2:4, :].rearrange("p a t -> p (a t)"), 4), ALU.add)\
                .then_inc(S("qr"), 1)
            sub(FIRST["ukv"] + 4)

            def attn_max(h):
                c = 8 * (h % 2)
                dve.wait_ge(*at("att_s", h + 1))
                st(dve.tensor_tensor(score[h % 2], ps[h % 2][:, 0:3 * P], const("causal", 3 * P), ALU.add))
                st.sync()
                dve.tensor_reduce(att_col[:, c:c + 1], score[h % 2][:, 0:P], AX_X, ALU.max)
                st(dve.tensor_reduce(att_col[:, c + 1:c + 2], score[h % 2][:, P:3 * P], AX_X, ALU.max))
                st.sync()
                dve.tensor_scalar(att_col[:, c + 2:c + 4], att_col[:, c:c + 2], -ATT_SCALE, None, ALU.mult)\
                    .then_inc(S("att_max"), 1)

            def attn_norm(h):
                c = 8 * (h % 2)
                dve.wait_ge(*at("att_exp", 2 * (h + 1)))
                st(dve.reciprocal(att_col[:, c + 6:c + 8], att_col[:, c + 4:c + 6]))
                st.sync()
                st(dve.tensor_scalar(prob[h % 2][:, 0:P], prob[h % 2][:, 0:P], att_col[:, c + 6:c + 7], None, ALU.mult))
                dve.tensor_scalar(prob[h % 2][:, P:3 * P], prob[h % 2][:, P:3 * P], att_col[:, c + 7:c + 8], None, ALU.mult)\
                    .then_inc(S("att_norm"), 1)

            def attn_rest(h):
                dve.wait_ge(*at("o_yh", h + 1))
                dve.tensor_tensor(yl[:, h, :], ps[4 + h % 2][:, 0:T], yh[:, h, :].bitcast(F32), ALU.subtract)\
                    .then_inc(S("o_yl"), 1)

            def centre():
                dve.wait_ge(*at("ln_mean", 1))
                st(dve.tensor_scalar(rstd[:, :], ps[0][:, 0:T], 1.0 / D, None, ALU.mult))
                st.sync()
                for b in range(4):
                    dve.tensor_tensor(conv[:, 2 * b:2 * b + 2, :], conv[:, 2 * b:2 * b + 2, :], spread(rstd[:, :], 2),
                                      ALU.subtract).then_inc(S("ln_cen"), 1)

            attn_max(0)
            for h in range(NH + 3):
                if h + 1 < NH:
                    attn_max(h + 1)
                if h < NH:
                    attn_norm(h)
                if h >= 3:
                    attn_rest(h - 3)
                if h < NH - 1:
                    convolve(4 if h in GATE_AT_HEAD else 6)
                if h == NH - 1:
                    convolve(2 * TAPS)
                    dve.wait_ge(*at("long_conv", len(POOL_TILES)))
                    dve.tensor_copy(att_col[:, 0:1], att_col[:, 0:1]).then_inc(S("conv_done"), 1)
                if h == NH + 1:
                    centre()
                if h in GATE_AT_HEAD:
                    sub(SLAB_OF[GATE_AT_HEAD[h]] + 3)

            def mix_b(n):
                dve.wait_ge(taken, FIRST["attn_out"] + n + 1)
                dve.wait_ge(*at("gates", 2))
                dve.tensor_tensor(kn[:, 2 * n:2 * n + 2, :], pair(ps[4 + n % 2][:, :]), gate_mem["gate_b"][:, 2 * n:2 * n + 2, :],
                                  ALU.mult).then_inc(S("mixed_b"), 1)

            s = FIRST["attn_out"]
            mix_b(0)
            sub(s + 3)
            inverse("ln", rstd[:, :], std[:, :])
            dve.wait_ge(*at("ln_cen", 4))
            for b in range(4):
                dve.tensor_tensor(conv[:, 2 * b:2 * b + 2, :], conv[:, 2 * b:2 * b + 2, :], spread(rstd[:, :], 2), ALU.mult)\
                    .then_inc(S("ln_n"), 1)
            mix_b(1)
            sub(s + 4)
            mix_b(2)
            for t in range(KT):
                dve.wait_ge(*at("c_xh", t + 1))
                dve.tensor_tensor(xl[:, t, :], conv[:, t, :], xh[:, t, :].bitcast(F32), ALU.subtract).then_inc(S("c_xl"), 1)
                if t == 3:
                    sub(s + 5)
                if t == 5:
                    mix_b(3)
            sub(s + 6)

            def low_mixed(n):
                dve.wait_ge(*at("w_yh", n + 1))
                dve.tensor_tensor(yl[:, 2 * n:2 * n + 2, :], kn[:, 2 * n:2 * n + 2, :], yh[:, 2 * n:2 * n + 2, :].bitcast(F32),
                                  ALU.subtract).then_inc(S("w_yl"), 1)

            for n in range(4):
                s = FIRST["conv_out"] + n
                dve.wait_ge(taken, s + 1)
                st(dve.tensor_tensor(pair(hid[:, n, :]), pair(ps[4 + n % 2][:, :]), gate_mem["gate_a"][:, 2 * n:2 * n + 2, :],
                                     ALU.mult))
                st.sync()
                dve.wait_ge(*at("mixed_b", 4))
                dve.tensor_tensor(kn[:, 2 * n:2 * n + 2, :], kn[:, 2 * n:2 * n + 2, :], pair(hid[:, n, :]), ALU.add)\
                    .then_inc(S("mixed"), 1)
                if n < 3:
                    sub(s + 3)
                dve.wait_ge(*at("mixed", n + 1))
                low_mixed(n)
            sub(FIRST["conv_out"] + 3 + 3)
            for n in range(3):
                sub(FIRST["w_out"] + n + 3)

            def add_normed(tag, src, gain):
                for b in range(4):
                    for t in (2 * b, 2 * b + 1):
                        ins = dve.scalar_tensor_tensor(qn[:, t, :], src(t), mods[:, gain, t:t + 1], rstd[:, :], ALU.mult, ALU.mult)
                    st(ins)
                    st.sync()
                    dve.tensor_tensor(resid[:, 2 * b:2 * b + 2, :], resid[:, 2 * b:2 * b + 2, :], qn[:, 2 * b:2 * b + 2, :],
                                      ALU.add).then_inc(S(tag), 1)

            inverse("y", rstd[:, :], std[:, :])
            add_normed("x3", lambda t: conv[:, t, :], 1)
            inverse("x3", rstd[:, :], std[:, :])
            dve.wait_ge(*at("x3", 4))
            for n in range(KT + 2):
                if n < KT:
                    dve.scalar_tensor_tensor(qn[:, n, :], resid[:, n, :], mods[:, 2, n:n + 1], rstd[:, :], ALU.mult, ALU.mult)\
                        .then_inc(S("h2_f"), 1)
                t = n - 2
                if t < 0:
                    continue
                dve.wait_ge(*at("h2_xh", t + 1))
                dve.scalar_tensor_tensor(xl[:, t, :], qn[:, t, :], ada[:, 24 + t:25 + t], xh[:, t, :].bitcast(F32), ALU.add,
                                         ALU.subtract).then_inc(S("h2_xl"), 1)
            sub(FIRST["w_out"] + 3 + 3)

            s0 = FIRST["mlp_in"]

            def relu(s):
                dve.wait_ge(taken, s + 1)
                dve.tensor_scalar(hid[:, 0, :], ps[4][:, :], 0.0, None, ALU.max).then_inc(S("mlp_relu"), 1)

            def rest(count):
                dve.wait_ge(*at("mlp_relu", count))
                dve.tensor_tensor(hid[:, 1, :], hid[:, 0, :], hid[:, 0, :], ALU.mult).then_inc(S("mlp_sq"), 1)
                dve.wait_ge(*at("mlp_sq", count))
                dve.wait_ge(*at("mlp_fh", count))
                dve.tensor_tensor(fl[:, :, :], pair(hid[:, 1, :]), fh[:, :, :].bitcast(F32), ALU.subtract)\
                    .then_inc(S("mlp_fl"), 1)

            relu(s0)
            sub(s0 + 3)
            rest(1)
            with dve.Fori(0, (MLP_STEPS - 1) // SLOTS - 1) as i:
                for r in range(SLOTS):
                    s = s0 + 1 + 2 * r
                    relu(i * 6 + s)
                    sub_in_loop(s + 3, i, 6)
                    rest(i * 3 + (r + 2))
                    sub_in_loop(s + 4, i, 6)
            for k in range(MLP_STEPS - SLOTS, MLP_STEPS):
                s = s0 + 2 * k - 1
                relu(s)
                if s + 3 < N_SLABS:
                    sub(s + 3)
                rest(k + 1)
                if s + 4 < N_SLABS:
                    sub(s + 4)
            inverse("z", rstd[:, :], std[:, :])
            add_normed("x4", lambda t: ps[t // 2][:, (t % 2) * T:(t % 2 + 1) * T], 3)

        @block.tensor
        def _(pe):
            def wide(s, bank, x, y, tile_ready=None, tile_base=0, slab=None, m_tiles=2):
                slab = s if slab is None else slab
                pe.wait_ge(low_done, s + 1)
                n = KT * P * m_tiles
                h, l = (w[:, slab % SLOTS, 0:n].rearrange("p (k m) -> p k m", k=KT) for w in (wh, wl))
                for m in range(m_tiles):
                    for k in range(KT):
                        if tile_ready is not None and m == 0:
                            pe.wait_ge(*at(tile_ready, tile_base(k)))
                        for j, (w, r) in enumerate(((h, x), (h, y), (l, x))):
                            mm = pe.matmul(bank[:, m * T:(m + 1) * T], w[:, k, m * P:(m + 1) * P], r[:, k, :],
                                           start=(m == 0 and k == 0 and j == 0), stop=(k == KT - 1 and j == 2),
                                           skip_group_check=True)
                mm.then_inc(taken, 1)

            def deep(s, slab=None):
                slab = s if slab is None else slab
                pe.wait_ge(low_done, s + 1)
                h, l = (w[:, slab % SLOTS, :].rearrange("p (k m) -> p k m", k=2) for w in (wh, wl))
                for k in range(2):
                    for m in range(KT):
                        for w, r in ((h, fh), (h, fl), (l, fh)):
                            mm = pe.matmul(ps[m // 2][:, (m % 2) * T:(m % 2 + 1) * T], w[:, k, m * P:(m + 1) * P], r[:, k, :],
                                           start=False, stop=False, skip_group_check=True)
                mm.then_inc(taken, 1)

            def clear_sums():
                for b in range(4):
                    pe.matmul(ps[b][:, :], zero[0:1, 0:P], zero[0:1, :], start=True, stop=True, skip_group_check=True)

            def column_sums(n, src, k_tiles, out, ready, signal=True, by_pair=False):
                pe.wait_ge(*at(*ready))
                for k in range(k_tiles):
                    if by_pair and k % 2 == 0 and k:
                        pe.wait_ge(*at(ready[0], ready[1] + k // 2))
                    mm = pe.matmul(out, ones, src(k), start=(k == 0), stop=(k == k_tiles - 1), skip_group_check=True)
                if signal:
                    mm.then_inc(S(n + "_stat"), 1)

            def one(k):
                return k + 1

            def modulate(step):
                pe.wait_ge(*at("ada_free", step + 1))
                for m in range(2):
                    mm = pe.matmul(ps[7][:, bass.ds(step * 2 + m, 1)], ada_sum[:, m * P:(m + 1) * P], ones[:, 0:1], start=True,
                                   stop=True, skip_group_check=True)
                mm.then_inc(S("ada_taken"), 1)

            def ffn(name, n, prev_free):
                s0 = FIRST[name + "_gate"]
                column_sums(n, lambda k: sq[:, k, :], KT, ps[6][:, 0:T], (n + "_sq", 1), by_pair=True)
                wide(s0, ps[4], xh, xl, n + "_xl", one)
                if prev_free:
                    pe.wait_ge(*at(*prev_free))
                wide(s0 + 1, ps[5], xh, xl)
                if name == "ffn1":
                    pe.wait_ge(*at("vec", 2))
                clear_sums()
                with pe.Fori(0, FF_STEPS - 1) as i:
                    s = s0 + 2
                    pe.wait_ge(*at(name + "_gate", i + 1))
                    wide(i * 3 + s, ps[4], xh, xl, slab=s)
                    pe.wait_ge(*at(name + "_up", i + 1))
                    wide(i * 3 + (s + 1), ps[5], xh, xl, slab=s + 1)
                    pe.wait_ge(*at(name + "_fl", i + 1))
                    deep(i * 3 + (s + 2), slab=s + 2)
                    modulate(i + (0 if name == "ffn1" else FF_STEPS - 1 + ADA_MIX))
                pe.wait_ge(*at(name + "_fl", FF_STEPS))
                deep(s0 + 3 * FF_STEPS - 1)

            pe.wait_ge(*at("con", 16))
            pe.wait_ge(*at("zero", 1))
            pe.wait_ge(*at("x_loaded", 16))
            xin = sq.rearrange("p (a b) t -> p a (b t)", a=2)
            for b in range(4):
                for t in (2 * b, 2 * b + 1):
                    for tk in range(2):
                        mm = pe.transpose(ps[4 + b][:, (t % 2) * T + tk * P:(t % 2) * T + (tk + 1) * P],
                                          xin[:, tk, t * P:(t + 1) * P], ident)
                mm.then_inc(S("x_turned"), 1)
            pe.wait_ge(*at("vec0_loaded", 16 * N_VEC_0))
            n = STAGE_ROWS[0]
            pe.transpose(ps[0][:, 0:n], stage[0:n, 0, :], ident[0:n, 0:n]).then_inc(S("vec_turned"), 1)
            pe.wait_ge(*at("vec1_loaded", 16 * (N_VEC - N_VEC_0)))
            for g in range(1, 4):
                n = STAGE_ROWS[g]
                mm = pe.transpose(ps[1][:, g * P:g * P + n], stage[0:n, g, :], ident[0:n, 0:n])
            mm.then_inc(S("vec_turned"), 1)
            pe.wait_ge(*at("x_in", 4))
            ffn("ffn1", "n1", None)

            s0 = FIRST["mix"]

            def mix(n, **kw):
                if n >= 2:
                    pe.wait_ge(*at("mix_evac", n - 1))
                wide(s0 + n, ps[4 + n % 2], xh, xl, m_tiles=1 if n == MIX_AB else 2, **kw)
                if n in ADA_AFTER:
                    modulate(FF_STEPS - 1 + ADA_AFTER.index(n))

            column_sums("n2", lambda k: sq[:, k, :], KT, ps[6][:, 0:T], ("n2_sq", 1), by_pair=True)
            mix(0, tile_ready="n2_xl", tile_base=one)
            for n in range(1, 6):
                mix(n)

            def row_sums(n, name, tile_of, count, bank, ready):
                pe.wait_ge(*at(*ready))
                sel = const(name, 8 * count).rearrange("p (t r) -> p t r", r=8)
                for t in range(count):
                    mm = pe.matmul(bank[0:8, 0:T], sel[:, t, :], sq[:, tile_of + t, :], start=(t == 0), stop=(t == count - 1),
                                   skip_group_check=True)
                mm.then_inc(S(n + "_stat"), 1)

            def spread_rows(n, name, src, count, k_rows, banks):
                sel = const(name, P * count, k_rows).rearrange("p (t m) -> p t m", m=P)
                for t in range(count):
                    mm = pe.matmul(ps[banks[t // 2]][:, (t % 2) * T:(t % 2 + 1) * T], sel[:, t, :], src,
                                   start=(t % 2 == 0), stop=True, skip_group_check=True)
                    if t % 2:
                        mm.then_inc(S(n), 1)

            def unit(m, u):
                return m[:, u * P:(u + 1) * P]

            def chan(m, u):
                c, h = u // HEADS, u % HEADS
                return m[:, h, c * CH:(c + 1) * CH]

            def four_units(bank, name, half, lhs, rhs):
                for u in range(4 * half, 4 * half + 4):
                    mm = pe.matmul(unit(bank, u % 4), lhs(u), rhs(u), start=(u % 4 == 0), stop=True, skip_group_check=True)
                mm.then_inc(S(name), 1)

            def turn_units(name, src):
                for u in range(UNITS):
                    mm = pe.transpose(unit(ps[2 + u // 4], u % 4), chan(src, u), ident)
                    if u % 4 == 3:
                        mm.then_inc(S(name), 1)

            pe.wait_ge(*at("con_rest", 16))
            row_sums("qk", "row_of", 0, 8, ps[0], ("qk_sq", 4))
            mix(6)
            mix(7)
            pe.wait_ge(*at("qk_row", 1))
            spread_rows("qk_spread", "row_sel", small[0:8, 7, :], 8, 8, (0, 1, 2, 3))
            mix(8)
            pe.wait_ge(*at("g_cum", 1))
            pe.wait_ge(*at("qk_n", 4))
            pe.wait_ge(*at("beta", 1))
            spread_rows("g_spread", "row_sel", g_cum[0:4, :], 4, 4, (0, 1))
            spread_rows("b_spread", "row_sel", beta_row[0:4, :], 4, 4, (2, 3))
            for q, src in enumerate((g_cum, beta_row)):
                for c in range(2):
                    pe.transpose(ps[6][:, 8 * q + 4 * c:8 * q + 4 * c + 4], src[0:4, c * CH:(c + 1) * CH], ident[0:4, 0:4])\
                        .then_inc(S("col_turned"), 1)
            mix(9)
            pe.wait_ge(*at("g_row", 2))
            pe.wait_ge(*at("kb", 2))
            for half in range(2):
                four_units(ps[half], "lt_mm", half, lambda u: chan(k_n, u), lambda u: chan(kb, u))
            pe.wait_ge(*at("qkv_silu", 6))
            turn_units("v_turned", qkv[:, 8:12, :])
            mix(10)
            pe.wait_ge(*at("lt", 2))
            for half in range(2):
                four_units(ps[half], "at_mm", half, lambda u: chan(k_n, u), lambda u: chan(q_n, u))
            mix(11)
            pe.wait_ge(*at("v_nat", 8))
            turn_units("k_turned", k_n)
            mix(12)
            pe.wait_ge(*at("mix_evac", 13))
            pe.wait_ge(*at("at_done", 1))
            pe.wait_ge(*at("k_nat", 8))
            with pe.Fori(0, LEVELS) as i:
                pe.wait_ge(*at("inv_b", i + 1))
                pe.wait_ge(*at("inv_t", i * 4 + 1))
                four_units(ps[0], "inv_x", 0, lambda u: unit(b_mat, u), lambda u: unit(t_mat, u))
                pe.wait_ge(*at("inv_t", i * 4 + 3))
                four_units(ps[1], "inv_x", 1, lambda u: unit(b_mat, u), lambda u: unit(t_mat, u))
                pe.wait_ge(*at("inv_xv", i + 1))
                four_units(ps[2], "inv_y", 0, lambda u: unit(tt_mat, u), lambda u: unit(x_mat, u))
                four_units(ps[4], "inv_y", 0, lambda u: unit(x_mat, u), lambda u: unit(tt_mat, u))
                pe.wait_ge(*at("inv_t", i * 4 + 4))
                pe.wait_ge(*at("inv_xa", i + 1))
                four_units(ps[3], "inv_y", 1, lambda u: unit(tt_mat, u), lambda u: unit(x_mat, u))
                four_units(ps[5], "inv_y", 1, lambda u: unit(x_mat, u), lambda u: unit(tt_mat, u))
            pe.wait_ge(*at("inv_t", 4 * LEVELS + 2))
            four_units(ps[0], "v_mm", 0, lambda u: unit(tt_mat, u), lambda u: unit(v_beta, u))
            pe.wait_ge(*at("inv_t", 4 * LEVELS + 4))
            for h in range(HEADS):
                mm = pe.matmul(unit(ps[1], h), unit(k_be, h), unit(tt_mat, HEADS + h), start=(h == 0), stop=True,
                               skip_group_check=True)
            mm.then_inc(S("w_mm"), 1)
            row_sums("short", "grp_row_of", 4, 4, ps[6], ("short_sq", 1))
            mix(13)
            pe.wait_ge(*at("v_new", 1))
            four_units(ps[2], "s_mm", 0, lambda u: unit(k_dec, u), lambda u: unit(v_new, u))
            four_units(ps[3], "o_mm", 0, lambda u: unit(v_new, u), lambda u: unit(at_mat, u))
            pe.wait_ge(*at("short_rstd", 1))
            spread_rows("short_spread", "grp_sel", small[0:8, 7, :], 4, 8, (6, 0))
            pe.wait_ge(*at("w_t", 1))
            pe.wait_ge(*at("state", 1))
            for h in range(HEADS):
                pe.matmul(unit(ps[1], h), unit(tt_mat, HEADS + h), unit(v_beta, HEADS + h), start=(h == 0), stop=False,
                          skip_group_check=True)
                mm = pe.matmul(unit(ps[1], h), unit(x_mat, h), unit(state, h), start=False, stop=True, skip_group_check=True)
            mm.then_inc(S("v_mm"), 1)
            mix(14)
            pe.wait_ge(*at("v_new", 2))
            for h in range(HEADS):
                pe.matmul(unit(ps[2], h), unit(state, h), q_n[:, h, CH:2 * CH], start=(h == 0), stop=False, skip_group_check=True)
                mm = pe.matmul(unit(ps[2], h), unit(v_new, HEADS + h), unit(at_mat, HEADS + h), start=False, stop=True,
                               skip_group_check=True)
            mm.then_inc(S("o_mm"), 1)
            row_sums("o", "row_of", 0, 4, ps[3], ("o_sq", 1))
            pe.wait_ge(*at("o_rstd", 1))
            pe.wait_ge(*at("short_out", 2))
            spread_rows("o_spread", "row_sel", small[0:8, 7, :], 4, 8, (0, 1))
            pe.wait_ge(*at("mix_evac", 15))
            for n in range(4):
                if n >= 2:
                    pe.wait_ge(*at("mix_resid", n - 1))
                wide(FIRST["mix_out"] + n, ps[4 + n % 2], xh, xl, "mo_xl" if n == 0 else None, lambda k: k // 2 + 1)
            pe.wait_ge(*at("mix_resid", 3))
            ffn("ffn2", "n3", ("mix_resid", 4))

            column_sums("f", lambda k: kn[:, k, :], KT, ps[6][:, 0:T], ("f_sq", 1), by_pair=True)
            column_sums("f", lambda k: qn[:, k, :], KT, ps[5][:, 0:T], ("fg_sq", 8))
            for n in range(4):
                s = FIRST["glu"] + 2 * n
                if n >= 2:
                    pe.wait_ge(*at("glu", n - 1))
                wide(s, ps[4 + 2 * (n % 2)], xh, xl, "h_xl" if n == 0 else None, one)
                wide(s + 1, ps[5 + 2 * (n % 2)], xh, xl)
            s = FIRST["lat"]
            pe.wait_ge(*at("glu", 3))
            for n in range(3):
                if n == 2:
                    pe.wait_ge(*at("lat", 1))
                wide(s + n, ps[4 + n % 2], xh, xl)
            pe.wait_ge(*at("lat", 2))
            wide(SLAB_OF["gate_b", 0], ps[5], xh, xl)
            pe.wait_ge(*at("glu", 4))
            pe.wait_ge(*at("lat_sq", 1))
            for k in range(3):
                pe.matmul(ps[6][:, 0:T], ones, lat_sq[:, k, :], start=(k == 0), stop=(k == 2), skip_group_check=True)
            for k in range(2):
                mm = pe.matmul(ps[6][:, T:2 * T], ones, lat_sq[:, 3 + k, :], start=(k == 0), stop=(k == 1), skip_group_check=True)
            mm.then_inc(S("lat_stat"), 1)
            pe.wait_ge(*at("lat", 4))
            swap = const("swap", P)
            pe.matmul(ps[7][:, 0:T], swap, kr_raw, start=True, stop=True).then_inc(S("kr_swap"), 1)
            wide(SLAB_OF["gate_b", 1], ps[4], xh, xl)
            for n in range(3):
                s = FIRST["uq"] + n
                pe.wait_ge(low_done, s + 1)
                if n == 2:
                    pe.wait_ge(*at("logits", 2))
                h, l = (w[:, s % SLOTS, 0:1536].rearrange("p (k m) -> p k m", k=3) for w in (wh, wl))
                for m in range(4):
                    for k in range(3):
                        if n == 0 and m == 0:
                            pe.wait_ge(*at("lat_yl", k + 1))
                        for j, (w, r) in enumerate(((h, yh), (h, yl), (l, yh))):
                            mm = pe.matmul(ps[2 * n + m // 2][:, (m % 2) * T:(m % 2 + 1) * T], w[:, k, m * P:(m + 1) * P],
                                           r[:, k, :], start=(m % 2 == 0 and k == 0 and j == 0), stop=(k == 2 and j == 2),
                                           skip_group_check=True)
                mm.then_inc(taken, 1)
            s = FIRST["ukv"]
            pe.wait_ge(low_done, s + 1)
            pe.wait_ge(*at("lat_yl", 5))
            pe.wait_ge(*at("q", 2))
            pe.wait_ge(*at("kr", 1))
            h, l = (w[:, s % SLOTS, :].rearrange("p (k m) -> p k m", k=2) for w in (wh, wl))
            for m in range(NH):
                for k in range(2):
                    for j, (w, r) in enumerate(((h, yh), (h, yl), (l, yh))):
                        mm = pe.matmul(ps[KEY_BANKS[m // 2]][:, (m % 2) * T:(m % 2 + 1) * T], w[:, k, m * P:(m + 1) * P],
                                       r[:, 3 + k, :], start=(m % 2 == 0 and k == 0 and j == 0), stop=(k == 1 and j == 2),
                                       skip_group_check=True)
            mm.then_inc(taken, 1)
            pe.wait_ge(*at("q", 6))
            for b in range(2):
                pe.matmul(pair(ps[2 + b][:, :]), swap, qr_raw[:, 2 * b:2 * b + 2, :], start=True, stop=True).then_inc(S("q_swap"), 1)
            pe.wait_ge(low_done, s + 2)
            h, l = (w[:, (s + 1) % SLOTS, :].rearrange("p (k m) -> p k m", k=2) for w in (wh, wl))
            for b, bank in enumerate(VALUE_BANKS):
                tk, half = b // 2, b % 2
                if b == 2:
                    pe.wait_ge(*at("k", 2))
                for k in range(2):
                    for j, (w, r) in enumerate(((h, yh), (h, yl), (l, yh))):
                        mm = pe.matmul(ps[bank][:, :], r[:, 3 + k, tk * P:(tk + 1) * P], w[:, k, half * 512:(half + 1) * 512],
                                       start=(k == 0 and j == 0), stop=(k == 1 and j == 2), skip_group_check=True)
            mm.then_inc(taken, 1)

            def scores(h):
                if h >= 2:
                    pe.wait_ge(*at("att_max", h - 1))
                bank, off = ps[h % 2], ROPE * (h % 2)
                for qt in range(2):
                    out = bank[:, qt * P:qt * P + (qt + 1) * P]
                    n = (qt + 1) * P
                    pe.matmul(out, qn[:, h, qt * P:(qt + 1) * P], kn[:, h, 0:n], start=(qt == 0), stop=False, skip_group_check=True)
                    mm = pe.matmul(out, qr[off:off + ROPE, h // 2, qt * P:(qt + 1) * P], kr[off:off + ROPE, 0:n], start=False,
                                   stop=True, skip_group_check=True)
                mm.then_inc(S("att_s"), 1)

            def turn(h):
                pe.wait_ge(*at("att_norm", h + 1))
                if h >= 2:
                    pe.wait_ge(*at("att_pt", h - 1))
                for j in range(3):
                    mm = pe.transpose(ps[2 + h % 2][:, j * P:(j + 1) * P], prob[h % 2][:, j * P:(j + 1) * P], ident)
                mm.then_inc(S("att_turned"), 1)

            def weigh(h):
                pe.wait_ge(*at("att_pt", h + 1))
                if h >= 2:
                    pe.wait_ge(*at("o_yl", h - 1))
                bank = ps[4 + h % 2]
                pe.matmul(bank[:, 0:T], v[:, 0, h * P:(h + 1) * P], prob_t[h % 2][:, 0:T], start=True, stop=False,
                          skip_group_check=True)
                pe.matmul(bank[:, P:T], v[:, 1, h * P:(h + 1) * P], prob_t[h % 2][:, T:T + P], start=False, stop=True,
                          skip_group_check=True).then_inc(S("att_o"), 1)

            pe.wait_ge(*at("v", 4))
            pe.wait_ge(*at("k", 4))
            pe.wait_ge(*at("qr", 1))
            scores(0)
            n_gates = 2
            for h in range(NH + 2):
                if h + 1 < NH:
                    scores(h + 1)
                if h == NH:
                    pe.wait_ge(*at("conv_done", 1))
                    for k in range(KT):
                        mm = pe.matmul(ps[0][:, 0:T], ones, conv[:, k, :], start=(k == 0), stop=(k == KT - 1),
                                       skip_group_check=True)
                    mm.then_inc(S("ln_mean"), 1)
                if h in GATE_AT_HEAD:
                    n_gates += 1
                    if n_gates > 4:
                        pe.wait_ge(*at("logits", n_gates - 2))
                    wide(SLAB_OF[GATE_AT_HEAD[h]], ps[6 + GATE_AT_HEAD[h][1] % 2], xh, xl)
                if 1 <= h <= NH:
                    turn(h - 1)
                if h >= 2:
                    weigh(h - 2)

            def four(phase, x, y, freed, first=None, base=one, start_free=None, between=None):
                for n in range(4):
                    if n < 2 and start_free:
                        pe.wait_ge(*at(*start_free[n]))
                    if n >= 2:
                        pe.wait_ge(*at(freed, n - 1))
                    wide(FIRST[phase] + n, ps[4 + n % 2], x, y, first if n == 0 else None, base)
                    if between:
                        between(n)

            pe.wait_ge(*at("att_max", NH))
            column_sums("ln", lambda k: ln_squares[:, k, :], KT, ps[1][:, 0:T], ("ln_sq", 1), by_pair=True)
            four("attn_out", yh, yl, "mixed_b", "o_yl", one, start_free=(("o_yl", 7), ("o_yl", 8)))
            four("conv_out", xh, xl, "mixed", "c_xl", one, start_free=(("mixed_b", 3), ("mixed_b", 4)))

            def y_sums(n):
                for b in ((), (0,), (1,), (2, 3))[n]:
                    pe.wait_ge(*at("y_sq", b + 1))
                    for k in (2 * b, 2 * b + 1):
                        mm = pe.matmul(ps[6][:, 0:T], ones, v_sq[:, k, :], start=(k == 0), stop=(k == KT - 1),
                                       skip_group_check=True)
                if n == 3:
                    mm.then_inc(S("y_stat"), 1)

            pe.wait_ge(*at("ln_rstd", 1))
            four("w_out", yh, yl, "y", "w_yl", lambda k: k // 2 + 1, start_free=(("mixed", 3), ("mixed", 4)), between=y_sums)
            column_sums("x3", lambda k: v_sq[:, k, :], KT, ps[7][:, 0:T], ("x3_sq", 1), by_pair=True)

            s0 = FIRST["mlp_in"]
            pe.wait_ge(*at("y", 4))
            clear_sums()
            wide(s0, ps[4], xh, xl, "h2_xl", one)
            with pe.Fori(0, (MLP_STEPS - 1) // SLOTS) as i:
                for r in range(SLOTS):
                    s = s0 + 1 + 2 * r
                    pe.wait_ge(*at("mlp_relu", i * 3 + (r + 1)))
                    wide(i * 6 + s, ps[4], xh, xl, slab=s)
                    pe.wait_ge(*at("mlp_fl", i * 3 + (r + 1)))
                    deep(i * 6 + (s + 1), slab=s + 1)
            pe.wait_ge(*at("mlp_fl", MLP_STEPS))
            deep(N_SLABS - 1)
            column_sums("z", lambda k: v_sq[:, k, :], KT, ps[6][:, 0:T], ("z_sq", 1), by_pair=True)
            for n, (half, tk) in enumerate(OUT_ORDER):
                for t in range(4 * half, 4 * half + 4):
                    pe.wait_ge(*at("x4", t // 2 + 1))
                    mm = pe.transpose(ps[4 + n % 2 + 2 * (n // 2)][:, (t % 4) * P:(t % 4 + 1) * P],
                                      resid[:, t, tk * P:(tk + 1) * P], ident)
                mm.then_inc(S("turned"), 1)


_INS = ["x", "ffn1_norm", "ffn1_w_in", "ffn1_w_out", "mix_norm", "w_mix_in", "conv_short_w", "conv_out_norm",
        "gdn_conv_w", "gdn_A_log", "gdn_dt_bias", "gdn_out_norm", "w_mix_out", "ffn2_norm", "ffn2_w_in", "ffn2_w_out",
        "final_norm", "c_2", "positions_2", "w_ada_2", "b_ada_2", "g_pre_mix_2", "g_post_mix_2", "g_pre_mlp_2",
        "g_post_mlp_2", "w_in_2", "conv_w_2", "conv_b_2", "conv_norm_g_2", "conv_norm_b_2", "w_conv_out_2",
        "q_norm_g_2", "w_uq_2", "kv_norm_g_2", "w_ukv_2", "w_attn_out_2", "w_out_2", "w_mlp_in_2", "w_mlp_out_2"]


def kernel(**inputs):
    import concourse.bacc as bacc
    from concourse.bass_utils import run_bass_kernel_spmd

    nc = bacc.Bacc("TRN2", target_bir_lowering=False, num_devices=1)
    arrays = {f"in_{n}": np.ascontiguousarray(inputs[n]) for n in _INS}
    arrays["in_table"] = constants()
    aps = {n[3:]: nc.dram_tensor(n, v.shape, mybir.dt.from_np(v.dtype), kind="ExternalInput").ap()
           for n, v in arrays.items()}
    aps["out"] = nc.dram_tensor("out", (1, T, D), F32, kind="ExternalOutput").ap()
    two_blocks(nc, aps)
    return run_bass_kernel_spmd(nc, [arrays], core_ids=[0]).results[0]["out"]
```
